# Optimizing a Trainium2 kernel written in Bass

```python
import math
import jax, jax.numpy as jnp
from jax import lax
import numpy as np

D_MODEL = 1024
BATCH = 1
SEQ = 512
DEPTH = 2

GRID_W = 64
HEAD_DIM = 64
NA_HEADS = D_MODEL // 128
NA_WIDTH = NA_HEADS * HEAD_DIM
NA_KH_MAX = 8
NA_KW = 16
GQA_HEADS = D_MODEL // 128
GQA_KV_HEADS = max(1, GQA_HEADS // 4)
GQA_WIDTH = GQA_HEADS * HEAD_DIM
GQA_KV_WIDTH = GQA_KV_HEADS * HEAD_DIM
Q_BLOCK = 128
ROPE_THETA = 10000.0
ROPE_AXIS_DIM = HEAD_DIM // 2
SG_WIDTH = D_MODEL // 2
SG_GROUPS = SG_WIDTH // HEAD_DIM
SG_CHUNK = 128
N_BRANCH = 3
LN_EPS = 1e-5
RMS_EPS = 1e-6
DEEPNORM_ALPHA = (2.0 * DEPTH) ** 0.25
DEEPNORM_BETA = (8.0 * DEPTH) ** -0.25
IN_SPLITS = (NA_WIDTH, NA_WIDTH, NA_WIDTH, NA_WIDTH,
             GQA_WIDTH, GQA_KV_WIDTH, GQA_KV_WIDTH, GQA_WIDTH,
             SG_WIDTH, SG_WIDTH, SG_WIDTH,
             N_BRANCH * D_MODEL)
IN_WIDTH = 4 * NA_WIDTH + 2 * GQA_WIDTH + 2 * GQA_KV_WIDTH + 3 * SG_WIDTH + N_BRANCH * D_MODEL


def _split_points():
    pts, acc = [], 0
    for w in IN_SPLITS[:-1]:
        acc += w
        pts.append(acc)
    return pts

def layer_norm(x, g, b):
    xf = x.astype(jnp.float32)
    mu = jnp.mean(xf, axis=-1, keepdims=True)
    var = jnp.mean(jnp.square(xf - mu), axis=-1, keepdims=True)
    return ((xf - mu) * lax.rsqrt(var + LN_EPS)).astype(x.dtype) * g + b

def rms_norm(x, g):
    xf = x.astype(jnp.float32)
    ms = jnp.mean(jnp.square(xf), axis=-1, keepdims=True)
    return (xf * lax.rsqrt(ms + RMS_EPS)).astype(x.dtype) * g

def axial_rope_tables(s):
    t = jnp.arange(s)
    row = (t // GRID_W).astype(jnp.float32)
    col = (t % GRID_W).astype(jnp.float32)
    freqs = ROPE_THETA ** (-jnp.arange(0, ROPE_AXIS_DIM, 2, dtype=jnp.float32) / ROPE_AXIS_DIM)
    ang = jnp.concatenate([row[:, None] * freqs, col[:, None] * freqs], axis=-1)
    return jnp.cos(ang), jnp.sin(ang)

def apply_rope(x, cos, sin):
    xf = x.astype(jnp.float32).reshape(*x.shape[:-1], HEAD_DIM // 2, 2)
    x0, x1 = xf[..., 0], xf[..., 1]
    c = cos[None, :, None, :]
    s = sin[None, :, None, :]
    out = jnp.stack([x0 * c - x1 * s, x0 * s + x1 * c], axis=-1)
    return out.reshape(x.shape).astype(x.dtype)

def neighbourhood_attention(q, k, v, rpb):
    b, s, h, dh = q.shape
    rows = s // GRID_W
    kh = min(NA_KH_MAX, rows)
    r = jnp.arange(rows)
    row_start = jnp.clip(r - kh // 2, 0, rows - kh)
    key_rows = row_start[:, None] + jnp.arange(kh)[None, :]
    c = jnp.arange(GRID_W)
    col_start = jnp.clip(c - NA_KW // 2, 0, GRID_W - NA_KW)
    col_valid = (c[None, :] >= col_start[:, None]) & (c[None, :] < col_start[:, None] + NA_KW)
    qg = q.reshape(b, rows, GRID_W, h, dh)
    kg = k.reshape(b, rows, GRID_W, h, dh)[:, key_rows]
    vg = v.reshape(b, rows, GRID_W, h, dh)[:, key_rows]
    scores = jnp.einsum('brqhd,brjkhd->bhrqjk', qg, kg).astype(jnp.float32) * (dh ** -0.5)
    row_off = key_rows - r[:, None] + (NA_KH_MAX - 1)
    col_off = jnp.clip(c[None, :] - c[:, None] + (NA_KW - 1), 0, 2 * NA_KW - 2)
    bias = rpb[:, row_off[:, None, :, None], col_off[None, :, None, :]]
    scores = scores + bias.astype(jnp.float32)
    scores = jnp.where(col_valid[:, None, :], scores, jnp.float32(-1e30))
    shp = scores.shape
    p = jax.nn.softmax(scores.reshape(b, h, rows, GRID_W, kh * GRID_W), axis=-1)
    p = p.reshape(shp).astype(v.dtype)
    out = jnp.einsum('bhrqjk,brjkhd->brqhd', p, vg)
    return out.reshape(b, s, h * dh)

def gqa_attention(q, k, v):
    b, s, hq, dh = q.shape
    hkv = k.shape[2]
    grp = hq // hkv
    nblk = s // Q_BLOCK
    qb = q.reshape(b, nblk, Q_BLOCK, hkv, grp, dh).transpose(1, 0, 2, 3, 4, 5)
    scale = dh ** -0.5

    def block(qi):
        sc = jnp.einsum('bqkgd,bskd->bkgqs', qi, k).astype(jnp.float32) * scale
        p = jax.nn.softmax(sc, axis=-1).astype(v.dtype)
        return jnp.einsum('bkgqs,bskd->bqkgd', p, v)

    out = lax.map(block, qb)
    return out.transpose(1, 0, 2, 3, 4, 5).reshape(b, s, hq * dh)

def spatial_gating(u, v, ln_g, ln_b, w_s, b_s):
    b, s, wc = u.shape
    vn = layer_norm(v, ln_g, ln_b)
    vc = vn.reshape(b, s // SG_CHUNK, SG_CHUNK, SG_GROUPS, wc // SG_GROUPS)
    mixed = jnp.einsum('gmn,bcngd->bcmgd', w_s, vc) + b_s.T[None, None, :, :, None]
    return u * mixed.reshape(b, s, wc)

def hybrid_layer(x, w_in, b_in, na_rpb, q_norm_g, k_norm_g, sg_ln_g, sg_ln_b, sg_w, sg_b,
                 w_br_a, w_br_b, w_br_c, w_out, b_out, ln_g, ln_b, rope_cos, rope_sin):
    b, s, d = x.shape
    hcat = x @ w_in + b_in
    (na_q, na_k, na_v, na_z, gq_q, gq_k, gq_v, gq_z,
     sg_u, sg_v, sg_z, gates) = jnp.split(hcat, _split_points(), axis=-1)

    y_a = neighbourhood_attention(na_q.reshape(b, s, NA_HEADS, HEAD_DIM),
                                  na_k.reshape(b, s, NA_HEADS, HEAD_DIM),
                                  na_v.reshape(b, s, NA_HEADS, HEAD_DIM), na_rpb)
    p_a = (y_a * jax.nn.silu(na_z)) @ w_br_a

    q = apply_rope(rms_norm(gq_q.reshape(b, s, GQA_HEADS, HEAD_DIM), q_norm_g), rope_cos, rope_sin)
    k = apply_rope(rms_norm(gq_k.reshape(b, s, GQA_KV_HEADS, HEAD_DIM), k_norm_g), rope_cos, rope_sin)
    y_b = gqa_attention(q, k, gq_v.reshape(b, s, GQA_KV_HEADS, HEAD_DIM))
    p_b = (y_b * jax.nn.silu(gq_z)) @ w_br_b

    y_c = spatial_gating(sg_u, sg_v, sg_ln_g, sg_ln_b, sg_w, sg_b)
    p_c = (y_c * jax.nn.silu(sg_z)) @ w_br_c

    g = jax.nn.sigmoid(gates.reshape(b, s, N_BRANCH, d))
    merged = g[:, :, 0] * p_a + g[:, :, 1] * p_b + g[:, :, 2] * p_c
    sub = merged @ w_out + b_out
    return layer_norm(DEEPNORM_ALPHA * x + sub, ln_g, ln_b)

def first_inputs(seed: int = 0) -> dict:
    key = jax.random.key(seed)
    ks = jax.random.split(key, 20)
    L, D = DEPTH, D_MODEL

    def nrm(k, shape, scale):
        return jax.random.normal(k, shape, jnp.float32) * scale

    return {
        "x": nrm(ks[0], (BATCH, SEQ, D), 1.0),
        "ln_in_g": 1.0 + nrm(ks[1], (D,), 0.02),
        "ln_in_b": nrm(ks[2], (D,), 0.02),
        "w_in": nrm(ks[3], (L, D, IN_WIDTH), D ** -0.5),
        "b_in": nrm(ks[4], (L, IN_WIDTH), 0.02),
        "na_rpb": nrm(ks[5], (L, NA_HEADS, 2 * NA_KH_MAX - 1, 2 * NA_KW - 1), 0.1),
        "q_norm_g": 1.0 + nrm(ks[6], (L, HEAD_DIM), 0.02),
        "k_norm_g": 1.0 + nrm(ks[7], (L, HEAD_DIM), 0.02),
        "sg_ln_g": 1.0 + nrm(ks[8], (L, SG_WIDTH), 0.02),
        "sg_ln_b": nrm(ks[9], (L, SG_WIDTH), 0.02),
        "sg_w": nrm(ks[10], (L, SG_GROUPS, SG_CHUNK, SG_CHUNK), SG_CHUNK ** -0.5),
        "sg_b": 1.0 + nrm(ks[11], (L, SG_GROUPS, SG_CHUNK), 0.02),
        "w_br_a": nrm(ks[12], (L, NA_WIDTH, D), NA_WIDTH ** -0.5),
        "w_br_b": nrm(ks[13], (L, GQA_WIDTH, D), GQA_WIDTH ** -0.5),
        "w_br_c": nrm(ks[14], (L, SG_WIDTH, D), SG_WIDTH ** -0.5),
        "w_out": nrm(ks[15], (L, D, D), (D ** -0.5) * DEEPNORM_BETA),
        "b_out": nrm(ks[16], (L, D), 0.02),
        "ln_post_g": 1.0 + nrm(ks[17], (L, D), 0.02),
        "ln_post_b": nrm(ks[18], (L, D), 0.02),
    }

def first_block(x, ln_in_g, ln_in_b, w_in, b_in, na_rpb, q_norm_g, k_norm_g, sg_ln_g, sg_ln_b,
              sg_w, sg_b, w_br_a, w_br_b, w_br_c, w_out, b_out, ln_post_g, ln_post_b):
    s = x.shape[1]
    rope_cos, rope_sin = axial_rope_tables(s)
    h = layer_norm(x, ln_in_g, ln_in_b)
    for l in range(DEPTH):
        h = hybrid_layer(h, w_in[l], b_in[l], na_rpb[l], q_norm_g[l], k_norm_g[l],
                         sg_ln_g[l], sg_ln_b[l], sg_w[l], sg_b[l],
                         w_br_a[l], w_br_b[l], w_br_c[l], w_out[l], b_out[l],
                         ln_post_g[l], ln_post_b[l], rope_cos, rope_sin)
    return h


DEPTH_2 = 1

FOX_HEADS = 8
FOX_HEAD_DIM = 64
FOX_WIDTH = FOX_HEADS * FOX_HEAD_DIM
SSD_HEADS = 8
SSD_HEAD_DIM = 64
SSD_WIDTH = SSD_HEADS * SSD_HEAD_DIM
SSD_GROUPS = 2
SSD_STATE = 64
SSD_CONV = 4
SSD_CHUNK = 128
SSD_CONV_DIM = SSD_WIDTH + 2 * SSD_GROUPS * SSD_STATE
S5_GROUP = 16
S5_WIDTH = 512
S5_GROUPS = S5_WIDTH // S5_GROUP
S5_STATE = 64
D_FF = 2816
FFN_CONV = 3
BRANCH_WIDTH = 512
ALPHA = (2 * DEPTH_2) ** 0.25
BETA = (8 * DEPTH_2) ** -0.25
RMS_EPS_2 = 1e-5
D_IN_PROJ = 3 * FOX_WIDTH + FOX_HEADS + SSD_WIDTH + SSD_CONV_DIM + SSD_HEADS + S5_WIDTH + N_BRANCH * D_MODEL


def _split_points_2():
    sizes = [FOX_WIDTH, FOX_WIDTH, FOX_WIDTH, FOX_HEADS, SSD_WIDTH, SSD_CONV_DIM,
             SSD_HEADS, S5_WIDTH]
    pts, acc = [], 0
    for s in sizes:
        acc += s
        pts.append(acc)
    return pts

def layer_norm_2(x, g, b):
    xf = x.astype(jnp.float32)
    mu = jnp.mean(xf, axis=-1, keepdims=True)
    var = jnp.mean(jnp.square(xf - mu), axis=-1, keepdims=True)
    return ((xf - mu) * lax.rsqrt(var + LN_EPS) * g + b).astype(x.dtype)

def causal_dwconv(x, w, b):
    k, c = w.shape
    y = lax.conv_general_dilated(
        x, w[:, None, :].astype(x.dtype), window_strides=(1,), padding=((k - 1, 0),),
        dimension_numbers=("NWC", "WIO", "NWC"), feature_group_count=c)
    return y + b.astype(x.dtype)

def fox_attention(q, k, v, f_logit):
    b, l, h, dh = q.shape
    cum = jnp.cumsum(jax.nn.log_sigmoid(f_logit.astype(jnp.float32)), axis=1)
    cum = cum.transpose(0, 2, 1)
    scale = dh ** -0.5
    outs = []
    for i in range(l // Q_BLOCK):
        q0, q1 = i * Q_BLOCK, (i + 1) * Q_BLOCK
        s = jnp.einsum('bqhd,bkhd->bhqk', q[:, q0:q1], k[:, :q1]).astype(jnp.float32) * scale
        s = s + cum[:, :, q0:q1, None] - cum[:, :, None, :q1]
        causal = jnp.arange(q1)[None, :] <= jnp.arange(q0, q1)[:, None]
        p = jax.nn.softmax(jnp.where(causal, s, -jnp.inf), axis=-1)
        outs.append(jnp.einsum('bhqk,bkhd->bqhd', p.astype(v.dtype), v[:, :q1]))
    return jnp.concatenate(outs, axis=1).reshape(b, l, h * dh)

def segsum(a):
    t = a.shape[-1]
    cs = jnp.cumsum(a, axis=-1)
    diff = cs[..., :, None] - cs[..., None, :]
    return jnp.where(jnp.tril(jnp.ones((t, t), dtype=bool)), diff, -jnp.inf)

def ssd_mixer(z, xbc, dt_raw, conv_w, conv_b, dt_bias, a_log, d_skip, norm_w):
    f32 = jnp.float32
    bsz, l, _ = z.shape
    g, e, n, p, q = SSD_GROUPS, SSD_HEADS // SSD_GROUPS, SSD_STATE, SSD_HEAD_DIM, SSD_CHUNK
    c = l // q
    xbc = jax.nn.silu(causal_dwconv(xbc, conv_w, conv_b))
    xs, bm, cm = jnp.split(xbc, [SSD_WIDTH, SSD_WIDTH + g * n], axis=-1)
    xh = xs.reshape(bsz, l, SSD_HEADS, p).astype(f32)
    dt = jax.nn.softplus(dt_raw.astype(f32) + dt_bias.astype(f32))
    a = -jnp.exp(a_log.astype(f32))
    xdt = (xh * dt[..., None]).reshape(bsz, c, q, g, e, p)
    adt = (dt * a).reshape(bsz, c, q, g, e).transpose(0, 3, 4, 1, 2)
    bc = bm.astype(f32).reshape(bsz, c, q, g, n)
    cc = cm.astype(f32).reshape(bsz, c, q, g, n)
    a_cs = jnp.cumsum(adt, axis=-1)
    decay_in = jnp.exp(segsum(adt))
    cb = jnp.einsum('bclgn,bcsgn->bgcls', cc, bc)
    y_diag = jnp.einsum('bgecls,bcsgep->bclgep', cb[:, :, None] * decay_in, xdt)
    decay_to_end = jnp.exp(a_cs[..., -1:] - a_cs).transpose(0, 3, 4, 1, 2)
    states = jnp.einsum('bclgn,bclgep->bcgepn', bc, xdt * decay_to_end[..., None])
    states = jnp.concatenate([jnp.zeros_like(states[:, :1]), states], axis=1)
    chunk_tot = jnp.pad(a_cs[..., -1], ((0, 0), (0, 0), (0, 0), (1, 0)))
    chunk_decay = jnp.exp(segsum(chunk_tot))
    states = jnp.einsum('bgezc,bcgepn->bzgepn', chunk_decay, states)[:, :-1]
    decay_out = jnp.exp(a_cs).transpose(0, 3, 4, 1, 2)[..., None]
    y_off = jnp.einsum('bclgn,bcgepn->bclgep', cc, states) * decay_out
    y = (y_diag + y_off).reshape(bsz, l, SSD_HEADS, p) + d_skip.astype(f32)[:, None] * xh
    y = y.reshape(bsz, l, SSD_WIDTH) * jax.nn.silu(z.astype(f32))
    yg = y.reshape(bsz, l, g, SSD_WIDTH // g)
    yg = yg * lax.rsqrt(jnp.mean(yg * yg, axis=-1, keepdims=True) + RMS_EPS_2)
    return (yg.reshape(bsz, l, SSD_WIDTH) * norm_w.astype(f32)).astype(z.dtype)

def _complex_linear_combine(earlier, later):
    ar1, ai1, br1, bi1 = earlier
    ar2, ai2, br2, bi2 = later
    return (ar2 * ar1 - ai2 * ai1,
            ar2 * ai1 + ai2 * ar1,
            ar2 * br1 - ai2 * bi1 + br2,
            ar2 * bi1 + ai2 * br1 + bi2)

def s5_mixer(u, a_re, a_im, b_re, b_im, c_re, c_im, log_step, d_skip, w_glu, b_glu):
    f32 = jnp.float32
    bsz, l, _ = u.shape
    lam_re = jnp.minimum(a_re.astype(f32), -1e-4)
    lam_im = a_im.astype(f32)
    step = jnp.exp(log_step.astype(f32))[:, None]
    mag = jnp.exp(lam_re * step)
    abar_re = mag * jnp.cos(lam_im * step)
    abar_im = mag * jnp.sin(lam_im * step)
    den = lam_re * lam_re + lam_im * lam_im
    num_re = abar_re - 1.0
    k_re = (num_re * lam_re + abar_im * lam_im) / den
    k_im = (abar_im * lam_re - num_re * lam_im) / den
    bre, bim = b_re.astype(f32), b_im.astype(f32)
    bb_re = k_re[..., None] * bre - k_im[..., None] * bim
    bb_im = k_re[..., None] * bim + k_im[..., None] * bre
    ug = u.astype(f32).reshape(bsz, l, S5_GROUPS, S5_GROUP)
    bu_re = jnp.einsum('blgh,gnh->lbgn', ug, bb_re)
    bu_im = jnp.einsum('blgh,gnh->lbgn', ug, bb_im)
    a_seq_re = jnp.broadcast_to(abar_re[None, None], (l, 1) + abar_re.shape)
    a_seq_im = jnp.broadcast_to(abar_im[None, None], (l, 1) + abar_im.shape)
    _, _, h_re, h_im = lax.associative_scan(
        _complex_linear_combine, (a_seq_re, a_seq_im, bu_re, bu_im), axis=0)
    y = (jnp.einsum('lbgn,ghn->blgh', h_re, c_re.astype(f32))
         - jnp.einsum('lbgn,ghn->blgh', h_im, c_im.astype(f32)))
    y = y.reshape(bsz, l, S5_WIDTH) + d_skip.astype(f32) * u.astype(f32)
    gy = jax.nn.gelu(y)
    out = gy * jax.nn.sigmoid(gy @ w_glu.astype(f32) + b_glu.astype(f32))
    return out.astype(u.dtype)

def mixer_sublayer(x, w_in, fox_f_bias, ssd_conv_w, ssd_conv_b, ssd_dt_bias, ssd_a_log,
                   ssd_d, ssd_norm_w, s5_a_re, s5_a_im, s5_b_re, s5_b_im, s5_c_re, s5_c_im,
                   s5_log_step, s5_d, s5_w_glu, s5_b_glu, w_branch, b_gate, w_out):
    bsz, l, _ = x.shape
    proj = x @ w_in
    q, k, v, f_logit, z, xbc, dt_raw, u, gate_logit = jnp.split(proj, _split_points_2(), axis=-1)
    hs = (bsz, l, FOX_HEADS, FOX_HEAD_DIM)
    y_a = fox_attention(q.reshape(hs), k.reshape(hs), v.reshape(hs), f_logit + fox_f_bias)
    y_b = ssd_mixer(z, xbc, dt_raw, ssd_conv_w, ssd_conv_b, ssd_dt_bias, ssd_a_log,
                    ssd_d, ssd_norm_w)
    y_c = s5_mixer(u, s5_a_re, s5_a_im, s5_b_re, s5_b_im, s5_c_re, s5_c_im,
                   s5_log_step, s5_d, s5_w_glu, s5_b_glu)
    branches = jnp.stack([y_a, y_b.astype(y_a.dtype), y_c.astype(y_a.dtype)], axis=2)
    proj_br = jnp.einsum('blrw,rwd->blrd', branches, w_branch)
    gates = jax.nn.sigmoid(gate_logit.reshape(bsz, l, N_BRANCH, D_MODEL) + b_gate)
    merged = jnp.sum(gates * proj_br, axis=2)
    return merged @ w_out

def conv_ffn(x, w_up, conv_w, conv_b, w_down):
    h = causal_dwconv(x @ w_up, conv_w, conv_b)
    val, gate = jnp.split(h, 2, axis=-1)
    return (jax.nn.silu(gate) * val) @ w_down

def second_inputs(seed: int = 0) -> dict:
    key = jax.random.key(seed)
    ks = iter(jax.random.split(key, 40))
    nrm = lambda shape, s: jax.random.normal(next(ks), shape, jnp.float32) * s
    L_ = DEPTH_2
    dt0 = jnp.exp(jax.random.uniform(next(ks), (L_, SSD_HEADS), jnp.float32,
                                     math.log(1e-3), math.log(1e-1)))
    inputs = {
        "x": nrm((BATCH, SEQ, D_MODEL), 1.0),
        "w_in": nrm((L_, D_MODEL, D_IN_PROJ), D_MODEL ** -0.5),
        "fox_f_bias": 2.0 + nrm((L_, FOX_HEADS), 0.5),
        "ssd_conv_w": nrm((L_, SSD_CONV, SSD_CONV_DIM), SSD_CONV ** -0.5),
        "ssd_conv_b": nrm((L_, SSD_CONV_DIM), 0.01),
        "ssd_dt_bias": dt0 + jnp.log(-jnp.expm1(-dt0)),
        "ssd_a_log": jnp.log(jax.random.uniform(next(ks), (L_, SSD_HEADS), jnp.float32, 1.0, 16.0)),
        "ssd_d": 1.0 + nrm((L_, SSD_HEADS), 0.1),
        "ssd_norm_w": 1.0 + nrm((L_, SSD_WIDTH), 0.02),
        "s5_a_re": -0.5 + nrm((L_, S5_GROUPS, S5_STATE), 0.01),
        "s5_a_im": jnp.pi * jnp.arange(S5_STATE, dtype=jnp.float32) + nrm((L_, S5_GROUPS, S5_STATE), 0.01),
        "s5_b_re": nrm((L_, S5_GROUPS, S5_STATE, S5_GROUP), (2 * S5_GROUP) ** -0.5),
        "s5_b_im": nrm((L_, S5_GROUPS, S5_STATE, S5_GROUP), (2 * S5_GROUP) ** -0.5),
        "s5_c_re": nrm((L_, S5_GROUPS, S5_GROUP, S5_STATE), 0.5),
        "s5_c_im": nrm((L_, S5_GROUPS, S5_GROUP, S5_STATE), 0.5),
        "s5_log_step": jax.random.uniform(next(ks), (L_, S5_GROUPS), jnp.float32,
                                          math.log(1e-3), math.log(1e-1)),
        "s5_d": nrm((L_, S5_WIDTH), 1.0),
        "s5_w_glu": nrm((L_, S5_WIDTH, S5_WIDTH), S5_WIDTH ** -0.5),
        "s5_b_glu": nrm((L_, S5_WIDTH), 0.01),
        "w_branch": nrm((L_, N_BRANCH, BRANCH_WIDTH, D_MODEL), BRANCH_WIDTH ** -0.5),
        "b_gate": nrm((L_, N_BRANCH, D_MODEL), 0.01),
        "w_out": nrm((L_, D_MODEL, D_MODEL), BETA * D_MODEL ** -0.5),
        "ln1_g": 1.0 + nrm((L_, D_MODEL), 0.02),
        "ln1_b": nrm((L_, D_MODEL), 0.01),
        "ffn_w_up": nrm((L_, D_MODEL, 2 * D_FF), D_MODEL ** -0.5),
        "ffn_conv_w": nrm((L_, FFN_CONV, 2 * D_FF), FFN_CONV ** -0.5),
        "ffn_conv_b": nrm((L_, 2 * D_FF), 0.01),
        "ffn_w_down": nrm((L_, D_FF, D_MODEL), BETA * D_FF ** -0.5),
        "ln2_g": 1.0 + nrm((L_, D_MODEL), 0.02),
        "ln2_b": nrm((L_, D_MODEL), 0.01),
    }
    return inputs

def second_block(x, w_in, fox_f_bias, ssd_conv_w, ssd_conv_b, ssd_dt_bias, ssd_a_log, ssd_d,
              ssd_norm_w, s5_a_re, s5_a_im, s5_b_re, s5_b_im, s5_c_re, s5_c_im, s5_log_step,
              s5_d, s5_w_glu, s5_b_glu, w_branch, b_gate, w_out, ln1_g, ln1_b, ffn_w_up,
              ffn_conv_w, ffn_conv_b, ffn_w_down, ln2_g, ln2_b):
    for i in range(DEPTH_2):
        mix = mixer_sublayer(x, w_in[i], fox_f_bias[i], ssd_conv_w[i], ssd_conv_b[i],
                             ssd_dt_bias[i], ssd_a_log[i], ssd_d[i], ssd_norm_w[i],
                             s5_a_re[i], s5_a_im[i], s5_b_re[i], s5_b_im[i], s5_c_re[i],
                             s5_c_im[i], s5_log_step[i], s5_d[i], s5_w_glu[i], s5_b_glu[i],
                             w_branch[i], b_gate[i], w_out[i])
        x = layer_norm_2(ALPHA * x + mix.astype(x.dtype), ln1_g[i], ln1_b[i])
        ffn = conv_ffn(x, ffn_w_up[i], ffn_conv_w[i], ffn_conv_b[i], ffn_w_down[i])
        x = layer_norm_2(ALPHA * x + ffn.astype(x.dtype), ln2_g[i], ln2_b[i])
    return x


_first_inputs = second_inputs


def second_inputs(seed=0):
    import zlib

    import numpy as np

    out = dict(_first_inputs(seed))
    spreads = {}
    factors = {'ssd_conv_b': 8.0,
     'ssd_norm_w': 22.361,
     's5_a_re': 200.0,
     's5_b_glu': 200.0,
     'b_gate': 8.0,
     'ln1_g': 2.71,
     'ln1_b': 5.567,
     'ffn_conv_b': 8.0,
     'ln2_g': 20.473,
     'ln2_b': 43.861,
     'fox_f_bias': 24.32,
     's5_a_im': 64.0,
     's5_b_re': 64.0,
     's5_b_im': 64.0,
     's5_c_re': 64.0,
     's5_c_im': 64.0,
     's5_log_step': 64.0,
     's5_w_glu': 19.207,
     's5_d': 2.788}
    for name, (base, spread) in spreads.items():
        noise = np.random.default_rng([zlib.crc32(name.encode()), seed]).standard_normal(out[name].shape)
        drawn = base * np.exp(spread * noise) if base else spread * noise
        out[name] = __import__('jax').numpy.asarray(drawn.astype(out[name].dtype))
    for name, factor in factors.items():
        out[name] = (out[name] * factor).astype(out[name].dtype)
    return out


_narrow_inputs = second_inputs


def second_inputs(seed=0):
    out = dict(_narrow_inputs(seed))
    wider = {'fox_f_bias': 12.0, 's5_b_glu': 9.0, 'ln2_g': 3.08, 'ln2_b': 3.08}
    for name, times in wider.items():
        mean = out[name].mean()
        out[name] = (mean + times * (out[name] - mean)).astype(out[name].dtype)
    return out


def setup_inputs(seed=0):
    out = dict(first_inputs(seed))
    for name, value in second_inputs(seed + 1).items():
        if name != "x":
            out[name + "_2"] = value
    return out


def reference(
    x, ln_in_g, ln_in_b, w_in, b_in, na_rpb, q_norm_g, k_norm_g, sg_ln_g, sg_ln_b, sg_w, sg_b,
    w_br_a, w_br_b, w_br_c, w_out, b_out, ln_post_g, ln_post_b, w_in_2, fox_f_bias_2,
    ssd_conv_w_2, ssd_conv_b_2, ssd_dt_bias_2, ssd_a_log_2, ssd_d_2, ssd_norm_w_2, s5_a_re_2,
    s5_a_im_2, s5_b_re_2, s5_b_im_2, s5_c_re_2, s5_c_im_2, s5_log_step_2, s5_d_2, s5_w_glu_2,
    s5_b_glu_2, w_branch_2, b_gate_2, w_out_2, ln1_g_2, ln1_b_2, ffn_w_up_2, ffn_conv_w_2,
    ffn_conv_b_2, ffn_w_down_2, ln2_g_2, ln2_b_2,
):
    x = first_block(
        x, ln_in_g, ln_in_b, w_in, b_in, na_rpb, q_norm_g, k_norm_g, sg_ln_g, sg_ln_b, sg_w,
        sg_b, w_br_a, w_br_b, w_br_c, w_out, b_out, ln_post_g, ln_post_b,
    )
    return second_block(
        x, w_in_2, fox_f_bias_2, ssd_conv_w_2, ssd_conv_b_2, ssd_dt_bias_2, ssd_a_log_2,
        ssd_d_2, ssd_norm_w_2, s5_a_re_2, s5_a_im_2, s5_b_re_2, s5_b_im_2, s5_c_re_2, s5_c_im_2,
        s5_log_step_2, s5_d_2, s5_w_glu_2, s5_b_glu_2, w_branch_2, b_gate_2, w_out_2, ln1_g_2,
        ln1_b_2, ffn_w_up_2, ffn_conv_w_2, ffn_conv_b_2, ffn_w_down_2, ln2_g_2, ln2_b_2,
    )


_drawn_inputs = setup_inputs


def setup_inputs(seed=0):
    import zlib

    import numpy as np

    out = dict(_drawn_inputs(seed))
    spreads = {}
    factors = {'b_in': 3.345,
     'na_rpb': 8.0,
     'q_norm_g': 8.0,
     'k_norm_g': 8.0,
     'sg_ln_g': 8.0,
     'sg_ln_b': 8.0,
     'sg_b': 8.0,
     'fox_f_bias_2': 2.712}
    for name, (base, spread) in spreads.items():
        noise = np.random.default_rng([zlib.crc32(name.encode()), seed]).standard_normal(out[name].shape)
        drawn = base * np.exp(spread * noise) if base else spread * noise
        out[name] = __import__('jax').numpy.asarray(drawn.astype(out[name].dtype))
    for name, factor in factors.items():
        out[name] = (out[name] * factor).astype(out[name].dtype)
    return out
```

```python
from contextlib import ExitStack

import concourse.bass as bass
import numpy as np
from concourse import mybir

F32 = mybir.dt.float32
F32R = mybir.dt.float32r
I32 = mybir.dt.int32
ACT = mybir.ActivationFunctionType
ALU = mybir.AluOpType
AX = mybir.AxisListType

P = 128
SEQ, D = 512, 1024
NT = SEQ // P
ND = D // P
HD = 64
HEADS = 8
WID = HEADS * HD
NW = WID // P
GRID = 64
KW = 16
LAYERS = 2
ALPHA_1 = (2.0 * LAYERS) ** 0.25
ALPHA_2 = 2.0 ** 0.25
LN_EPS, RMS_EPS, RMS_EPS_2 = 1e-5, 1e-6, 1e-5
UNIT = 2048
RAW, SPLIT = 3, 2
GRING = 4
SM = HD ** -0.5
NEG = -1e30
LOWEST = -3.0e38


class Signals:

    def __init__(self, nc, known):
        self.nc, self.known = nc, known
        self.sems, self.count, self.seen, self.phase = {}, {}, {}, ""

    def sem(self, name):
        if name not in self.sems:
            self.sems[name] = self.ctx.enter_context(self.nc.semaphore(name))
        return self.sems[name]

    def begin(self, phase):
        self.phase, self.count, self.sems = phase, {}, {}
        self.ctx = ExitStack()

    def end(self):
        for s in self.sems.values():
            self.nc.sync.sem_clear(s)
        self.nc.all_engine_barrier()
        self.ctx.close()

    def inc(self, name, *key, by=1):
        self.count[name] = self.count.get(name, 0) + by
        self.seen[(self.phase, name) + key] = self.count[name]
        return self.sem(name), by

    def after(self, name, *key):
        if self.known is None:
            return self.sem(name) if name != "unit_done" else self.sem("group"), 1
        value = self.known[(self.phase, name) + key]
        return self.after(*value) if isinstance(value, tuple) else (self.sem(name), value)


class Unit:

    def __init__(self, kind, src, nk, cols, evac, k0=0, of=None, col0=0):
        self.kind, self.src, self.nk, self.cols, self.evac = kind, src, nk, cols, evac
        self.k0, self.of, self.col0 = k0, of or nk, col0
        self.n = nk * cols
        self.gids = []
        self.banks = 4


def plan_groups(units):
    gid = 0
    for n, u in enumerate(units):
        u.n_ = n
        if u.kind == "F":
            blocks = u.cols // P
            u.gids = list(range(gid, gid + blocks))
            gid += blocks
        elif u.k0 == 0:
            u.gids = list(range(gid, gid + NT))
            gid += NT
        else:
            u.gids = units[n - 1].gids


def quarters(u):
    if u.kind == "F" and u.cols == 2 * P:
        h = u.nk // 2
        return [(q // 2, (q % 2) * h, (q % 2) * h + h) for q in range(4)]
    return [(q, 0, u.nk) for q in range(4)]


class Stream:

    def __init__(self, nc, sig, mem, units, w_dram, srcs, ready):
        self.nc, self.sig, self.mem, self.units, self.w_dram = nc, sig, mem, units, w_dram
        self.srcs, self.ready = srcs, ready
        plan_groups(units)
        self.by_gid = {}
        for u in units:
            for b, g in enumerate(u.gids):
                self.by_gid[g] = (u, b)
        self.bank_of, self.before, last = {}, {}, {}
        for g in sorted(self.by_gid):
            bank = g % self.by_gid[g][0].banks
            self.bank_of[g], self.before[g] = bank, last.get(bank)
            last[bank] = g

    def wait_slot_free(self, eng, gid):
        if self.before[gid] is not None:
            self.wait_read(eng, self.before[gid])

    def wait_read(self, eng, gid):
        u, b = self.by_gid[gid]
        for name in EVAC_READERS[u.evac[0]]:
            eng.wait_ge(*self.sig.after(name, gid))

    def bank(self, gid):
        return self.mem.bank[self.bank_of[gid]]

    def load(self, sp, n):
        u, s = self.units[n], n % RAW
        if n >= RAW:
            sp.wait_ge(*self.sig.after("w_lo", n - RAW))
        sp.dma_start(self.mem.raw[s][:, 0:u.n], self.w_dram(n)[:, 0:u.n]).then_inc(
            *self.sig.inc(f"w_raw{s}", n, by=16))

    def hi(self, act, n):
        if n >= len(self.units):
            return
        u, s = self.units[n], n % SPLIT
        act.wait_ge(*self.sig.after(f"w_raw{n % RAW}", n))
        if n >= SPLIT:
            act.wait_ge(*self.sig.after("unit_done", n - SPLIT))
        self.nc.scalar.activation(self.mem.wh[s][:, 0:u.n], self.mem.raw[n % RAW][:, 0:u.n],
                                  ACT.Copy).then_inc(*self.sig.inc("w_hi", n))

    def lo(self, dve, n):
        if n >= len(self.units):
            return
        u, s = self.units[n], n % SPLIT
        dve.wait_ge(*self.sig.after("w_hi", n))
        self.nc.vector.tensor_tensor(self.mem.wl[s][:, 0:u.n], self.mem.raw[n % RAW][:, 0:u.n],
                                     self.mem.wh[s][:, 0:u.n].bitcast(F32), ALU.subtract).then_inc(
            *self.sig.inc("w_lo", n))

    def multiply(self, pe, n, q):
        u, s = self.units[n], n % SPLIT
        if q == 0:
            pe.wait_ge(*self.sig.after("w_lo", n))
            for what in self.ready(u):
                pe.wait_ge(*self.sig.after(*what))
        b, ka, kb = quarters(u)[q]
        gid = u.gids[b]
        first = u.k0 + ka == 0
        if first:
            self.wait_slot_free(pe, gid)
        wh = self.mem.wh[s][:, 0:u.n].rearrange("p (k c) -> p k c", c=u.cols)
        wl = self.mem.wl[s][:, 0:u.n].rearrange("p (k c) -> p k c", c=u.cols)
        xh, xl = self.srcs[u.src]
        last = None
        for k in range(ka, kb):
            kk = u.k0 + k
            stop = kk == u.of - 1
            if u.kind == "F":
                w = slice(b * P, (b + 1) * P)
                trio = [(wh[:, k, w], xh[:, kk, :]), (wh[:, k, w], xl[:, kk, :]),
                        (wl[:, k, w], xh[:, kk, :])]
                dst = self.bank(gid)[:, :]
            else:
                t = slice(b * P, (b + 1) * P)
                trio = [(xh[:, kk, t], wh[:, k, :]), (xh[:, kk, t], wl[:, k, :]),
                        (xl[:, kk, t], wh[:, k, :])]
                dst = self.bank(gid)[:, 0:u.cols]
            for i, (stationary, moving) in enumerate(trio):
                last = self.nc.tensor.matmul(dst, stationary, moving, start=kk == 0 and i == 0,
                                             stop=stop and i == 2)
        complete = u.k0 + kb == u.of
        if complete:
            last.then_inc(*self.sig.inc("group", gid))
        if q == 3:
            if complete:
                self.sig.seen[(self.sig.phase, "unit_done", n)] = ("group", gid)
            else:
                last.then_inc(*self.sig.inc("unit_part", n))
                self.sig.seen[(self.sig.phase, "unit_done", n)] = ("unit_part", n)


EVAC_READERS = {
    "scaled": ("ev_act",), "silu": ("ev_act",), "gate": ("ev_act",), "biased": ("ev_dve",),
    "branch": ("ev_dve",), "residual": ("ev_dve",), "plain": ("ev_act",), "copy_t": ("ev_dve",),
    "conv": ("ev_dve",), "conv_ffn": ("ev_dve",), "glu": ("ev_act",),
}


class Memory:

    def __init__(self, nc, ctx):
        self.nc, self.ctx = nc, ctx
        sb = lambda name, shape, dt=F32: ctx.enter_context(nc.sbuf_tensor(name, shape, dt))
        self.x_base = (nc.sbuf_base + 31) // 32 * 32
        self.xh = sb("x_hi", [P, ND, SEQ], F32R)
        self.xl = sb("x_lo", [P, ND, SEQ], F32R)
        self.raw = [sb(f"w_raw_{i}", [P, UNIT]) for i in range(RAW)]
        self.wh = [sb(f"w_hi_{i}", [P, UNIT], F32R) for i in range(SPLIT)]
        self.wl = [sb(f"w_lo_{i}", [P, UNIT], F32R) for i in range(SPLIT)]
        self.ident = sb("ident", [P, P])
        self.tbias = [sb(f"tbias_{i}", [P, 512]) for i in range(2)]
        self.half = sb("minus_half", [P, 16])
        self.small = sb("small", [P, 512])
        self.small2 = sb("small_2", [P, 352])
        self.rope = sb("rope", [P, 2 * NT * 32])
        self.mask = sb("causal_mask", [P, P])
        self.arena_kb = 110
        self.base = (nc.sbuf_base + 31) // 32 * 32
        ctx.enter_context(nc.sbuf_tensor("arena", [P, self.arena_kb * 256], F32))
        self.bank = [ctx.enter_context(nc.psum_tensor(f"bank_{i}", [P, 512], F32)) for i in range(4)]
        self.upper = ctx.enter_context(nc.psum_tensor("banks_4_to_7", [P, 4, 512], F32))
        self.bank += [self.upper[:, i, :] for i in range(4)]

    def at(self, name, kb, shape, dt=F32):
        n = 4 * int(np.prod(shape[1:]))
        assert kb * 1024 + n <= self.arena_kb * 1024, name
        return self.nc.alloc_sbuf_tensor_at(name, shape, dt, offset=int(self.base + kb * 1024))


class LayerNorm:

    def __init__(self, nc, sig, mem, xt, gamma, beta, keep, banks, source):
        self.nc, self.sig, self.mem, self.xt = nc, sig, mem, xt
        self.gamma, self.beta, self.keep, self.source = gamma, beta, keep, source
        self.stats = mem.small[:, 0:NT * 12].rearrange("p (t s) -> p t s", s=12)
        self.mv = mem.small[:, 48:48 + 2 * NT].rearrange("p (t s) -> p t s", s=2)
        self.rstd = mem.small[:, 56:56 + NT]
        self.banks = banks

    def statistics(self, dve, t):
        sig, nc = self.sig, self.nc
        dve.wait_ge(*sig.after(*self.source(t)))
        for i in range(2):
            nc.vector.bn_stats(self.stats[:, t, 6 * i:6 * i + 6],
                               self.xt[:, t, 512 * i:512 * i + 512]).then_inc(
                *sig.inc("ln_stats", t, i))
        dve.wait_ge(*sig.after("ln_stats", t, 1))
        nc.vector.bn_aggr(self.mv[:, t, :], self.stats[:, t, :]).then_inc(*sig.inc("ln_mv", t))
        dve.wait_ge(*sig.after("ln_mv", t))
        nc.vector.tensor_scalar(self.mv[:, t, 1:2], self.mv[:, t, 1:2], LN_EPS, None,
                                ALU.add).then_inc(*sig.inc("ln_var", t))

    def power(self, pool, t):
        pool.wait_ge(*self.sig.after("ln_var", t))
        self.nc.gpsimd.tensor_tensor(self.rstd[:, t:t + 1], self.mv[:, t, 1:2],
                                     self.mem.half[:, 0:1], ALU.pow).then_inc(
            *self.sig.inc("ln_rstd", t))

    def normalise(self, dve, t):
        dve.wait_ge(*self.sig.after("ln_rstd", t))
        self.nc.vector.tensor_scalar(self.xt[:, t, :], self.xt[:, t, :], self.mv[:, t, 0:1],
                                     self.rstd[:, t:t + 1], ALU.subtract, ALU.mult).then_inc(
            *self.sig.inc("ln_centred", t))

    def affine(self, pool, t):
        sig = self.sig
        if t == 0:
            pool.wait_ge(*sig.after("ln_params"))
        pool.wait_ge(*sig.after("ln_centred", t))
        self.nc.gpsimd.tensor_tensor(self.xt[:, t, :], self.xt[:, t, :], self.gamma[:, :],
                                     ALU.mult).then_inc(*sig.inc("ln_scaled", t))
        pool.wait_ge(*sig.after("ln_scaled", t))
        self.nc.gpsimd.tensor_tensor(self.xt[:, t, :], self.xt[:, t, :], self.beta[:, :],
                                     ALU.add).then_inc(*sig.inc("ln_out", t))

    def store(self, sp, t):
        sp.wait_ge(*self.sig.after("ln_out", t))
        sp.dma_start(self.keep(t), self.xt[:, t, :]).then_inc(*self.sig.inc("ln_stored", t, by=16))

    def transpose(self, pe, t):
        sig = self.sig
        pe.wait_ge(*sig.after("ln_out", t))
        for half in range(2):
            if t:
                pe.wait_ge(*sig.after("x_lo", t - 1, half))
            for i in range(4):
                f = 4 * half + i
                last = self.nc.tensor.transpose(self.mem.bank[self.banks[half]][:, i * P:(i + 1) * P],
                                                self.xt[:, t, f * P:(f + 1) * P], self.mem.ident[:, :])
            last.then_inc(*sig.inc("x_transposed", t, half))

    def split_hi(self, act, t):
        for half in range(2):
            act.wait_ge(*self.sig.after("x_transposed", t, half))
            self.nc.scalar.activation(
                self.mem.xh[:, 4 * half:4 * half + 4, t * P:(t + 1) * P],
                self.mem.bank[self.banks[half]][:, :].rearrange("p (f c) -> p f c", c=P),
                ACT.Copy).then_inc(*self.sig.inc("x_hi", t, half))

    def split_lo(self, dve, t):
        for half in range(2):
            dve.wait_ge(*self.sig.after("x_hi", t, half))
            x = slice(4 * half, 4 * half + 4), slice(t * P, (t + 1) * P)
            self.nc.vector.tensor_tensor(
                self.mem.xl[:, x[0], x[1]],
                self.mem.bank[self.banks[half]][:, :].rearrange("p (f c) -> p f c", c=P),
                self.mem.xh[:, x[0], x[1]].bitcast(F32), ALU.subtract).then_inc(
                *self.sig.inc("x_lo", t, half))


class Attention:

    LAG_T, LAG_PV = 2, 7
    STEPS = HEADS * NT + LAG_PV

    def __init__(self, nc, sig, mem, name, q, k, v, y, causal, bias, probs, pt, scale=1.0,
                 gate=None, needs=None, base=(), rows=None):
        self.nc, self.sig, self.mem, self.name = nc, sig, mem, name
        self.q, self.k, self.v, self.y, self.causal, self.bias = q, k, v, y, causal, bias
        self.probs, self.pt, self.scale, self.gate = probs, pt, scale, gate
        self.needs, self.base, self.rows = needs, base, rows

    def keys(self, i):
        return (i + 1) * P if self.causal else SEQ

    def scores(self, pe, j):
        if not 0 <= j < HEADS * NT:
            return
        h, i = divmod(j, NT)
        if j >= 2:
            pe.wait_ge(*self.sig.after(self.name + "_exp", j - 2))
        else:
            for w in self.base:
                pe.wait_ge(*self.sig.after(*w))
        for w in self.needs(h):
            pe.wait_ge(*self.sig.after(*w))
        n = self.keys(i)
        self.nc.tensor.matmul(self.mem.bank[4 + j % 2][:, 0:n], self.q(h, i), self.k(h)[:, 0:n],
                              start=True, stop=True).then_inc(*self.sig.inc(self.name + "_scores", j))

    def maximum(self, dve, j):
        if not 0 <= j < HEADS * NT:
            return
        sig, nc, name = self.sig, self.nc, self.name
        h, i = divmod(j, NT)
        n = self.keys(i)
        dve.wait_ge(*sig.after(name + "_scores", j))
        mx, nmx = self.mem.small[:, 64 + j % 8:65 + j % 8], self.mem.small[:, 72 + j % 8:73 + j % 8]
        ps = self.mem.bank[4 + j % 2]
        if self.bias is not None:
            if self.causal:
                nc.vector.tensor_tensor(ps[:, n - P:n], ps[:, n - P:n], self.mem.mask[:, :],
                                        ALU.add).then_inc(*sig.inc(name + "_masked", j))
                dve.wait_ge(*sig.after(name + "_masked", j))
            ap, ready = self.bias(h, i)
            dve.wait_ge(*sig.after(*ready))
            if j >= 3:
                dve.wait_ge(*sig.after(name + "_transposed", j - 3))
            nc.vector.tensor_tensor_reduce(
                out=self.probs[:, j % 3, 0:n], in0=ps[:, 0:n], in1=ap[:, 0:n], scale=1.0,
                scalar=LOWEST, op0=ALU.add, op1=ALU.max, accum_out=mx).then_inc(
                *sig.inc(name + "_max", j))
        else:
            nc.vector.tensor_reduce(mx, ps[:, 0:n], AX.X, ALU.max).then_inc(
                *sig.inc(name + "_max", j))
        dve.wait_ge(*sig.after(name + "_max", j))
        if self.rows is not None:
            c = self.rows(h, i)
            nc.vector.tensor_scalar(mx, mx, c, -1.0, ALU.add, ALU.mult).then_inc(
                *sig.inc(name + "_rowmax", j))
            dve.wait_ge(*sig.after(name + "_rowmax", j))
            nc.vector.tensor_scalar(nmx, mx, c, None, ALU.add).then_inc(*sig.inc(name + "_nmax", j))
        else:
            nc.vector.tensor_scalar(nmx, mx, -self.scale, None, ALU.mult).then_inc(
                *sig.inc(name + "_nmax", j))

    def exponent(self, act, j):
        if not 0 <= j < HEADS * NT:
            return
        sig, name = self.sig, self.name
        n = self.keys(j % NT)
        act.wait_ge(*sig.after(name + "_nmax", j))
        src = self.probs[:, j % 3, 0:n] if self.bias is not None else self.mem.bank[4 + j % 2][:, 0:n]
        if self.bias is None and j >= 3:
            act.wait_ge(*sig.after(name + "_transposed", j - 3))
        self.nc.scalar.activation(self.probs[:, j % 3, 0:n], src, ACT.Exp,
                                  bias=self.mem.small[:, 72 + j % 8:73 + j % 8], scale=self.scale,
                                  accum_out=self.mem.small[:, 80 + j % 8:81 + j % 8]).then_inc(
            *sig.inc(name + "_exp", j))

    def normalise(self, dve, j):
        if not 0 <= j < HEADS * NT:
            return
        sig, nc, name = self.sig, self.nc, self.name
        n = self.keys(j % NT)
        dve.wait_ge(*sig.after(name + "_exp", j))
        inv = self.mem.small[:, 88 + j % 8:89 + j % 8]
        nc.vector.reciprocal(inv, self.mem.small[:, 80 + j % 8:81 + j % 8]).then_inc(
            *sig.inc(name + "_inv", j))
        dve.wait_ge(*sig.after(name + "_inv", j))
        nc.vector.tensor_scalar(self.probs[:, j % 3, 0:n], self.probs[:, j % 3, 0:n], inv, None,
                                ALU.mult).then_inc(*sig.inc(name + "_probs", j))

    def transpose(self, pe, j):
        if not 0 <= j < HEADS * NT:
            return
        sig, name = self.sig, self.name
        pe.wait_ge(*sig.after(name + "_probs", j))
        if j:
            pe.wait_ge(*sig.after(name + "_pt", j - 1))
        for kb in range(self.keys(j % NT) // P):
            last = self.nc.tensor.transpose(self.mem.bank[6][:, kb * P:(kb + 1) * P],
                                            self.probs[:, j % 3, kb * P:(kb + 1) * P],
                                            self.mem.ident[:, :])
        last.then_inc(*sig.inc(name + "_transposed", j))

    def keep_transposed(self, act, j):
        if not 0 <= j < HEADS * NT:
            return
        sig, name = self.sig, self.name
        h, i = divmod(j, NT)
        nk = self.keys(i) // P
        act.wait_ge(*sig.after(name + "_transposed", j))
        if h >= 2:
            act.wait_ge(*sig.after(name + "_pv", h - 2))
        self.nc.scalar.activation(
            self.pt[:, h % 2, 0:nk, i * P:(i + 1) * P],
            self.mem.bank[6][:, 0:nk * P].rearrange("p (k c) -> p k c", c=P), ACT.Copy).then_inc(
            *sig.inc(name + "_pt", j))

    def values(self, pe, j):
        if not 0 <= j < HEADS * NT:
            return
        sig, name = self.sig, self.name
        h, kb = divmod(j, NT)
        if kb == 0:
            pe.wait_ge(*sig.after(name + "_pt", h * NT + NT - 1))
            if h:
                pe.wait_ge(*sig.after(name + "_y", h - 1))
        q0 = kb * P if self.causal else 0
        half = slice((h % 2) * HD, (h % 2) * HD + HD)
        ins = self.nc.tensor.matmul(self.mem.bank[7][half, q0:SEQ], self.v(h, kb),
                                    self.pt[:, h % 2, kb, q0:SEQ], start=kb == 0, stop=kb == NT - 1)
        if kb == NT - 1:
            ins.then_inc(*sig.inc(name + "_pv", h))

    def output(self, dve, j):
        if not 0 <= j < HEADS * NT or j % NT != NT - 1:
            return
        sig, h = self.sig, j // NT
        dve.wait_ge(*sig.after(self.name + "_pv", h))
        half = slice((h % 2) * HD, (h % 2) * HD + HD)
        y = self.y[half, h // 2, :]
        if self.gate is None:
            ins = self.nc.vector.tensor_copy(y, self.mem.bank[7][half, :])
        else:
            dve.wait_ge(*sig.after(*self.gate(h)))
            ins = self.nc.vector.tensor_tensor(y, self.mem.bank[7][half, :], y, ALU.mult)
        ins.then_inc(*sig.inc(self.name + "_y", h))

    def on_pe(self, pe, j):
        self.scores(pe, j)
        self.transpose(pe, j - self.LAG_T)
        self.values(pe, j - self.LAG_PV)

    def on_act(self, act, j):
        self.exponent(act, j)
        self.keep_transposed(act, j - self.LAG_T)

    def on_dve(self, dve, j):
        self.maximum(dve, j)
        self.normalise(dve, j - 1)
        self.output(dve, j - self.LAG_PV)


def emit_common_evac(nc, sig, mem, stream, u, b, gid, eng_name, eng, ctx):
    kind, tag = u.evac[0], u.evac[1]
    ps = stream.bank(gid)
    if eng_name == "act":
        if kind == "scaled":
            dst, bias, scale = ctx["scaled"](tag, u.evac[2] + b)
            eng.wait_ge(*sig.after("group", gid))
            for w in ctx["before"](tag):
                eng.wait_ge(*sig.after(*w))
            nc.scalar.activation(dst, ps[:, :], ACT.Identity, bias=bias, scale=scale).then_inc(
                *sig.inc("ev_act", gid))
        elif kind in ("silu", "gate"):
            g = ctx["g_slot"][gid]
            eng.wait_ge(*sig.after("group", gid))
            if g >= GRING:
                eng.wait_ge(*sig.after(*ctx["g_used"][g - GRING]))
            for w in ctx["before"](tag):
                eng.wait_ge(*sig.after(*w))
            bias = ctx["half_bias"](tag, u.evac[2] + b)
            ins = nc.scalar.activation(ctx["g"][:, g % GRING, :], ps[:, :], ACT.Tanh, bias=bias,
                                       scale=0.5)
            if kind == "silu":
                ins.then_inc(*sig.inc("tanh", gid))
                nc.scalar.activation(ctx["scaled"](tag, u.evac[2] + b)[0], ps[:, :], ACT.Identity,
                                     bias=bias, scale=0.5).then_inc(*sig.inc("ev_act", gid))
            else:
                ins.then_inc(*sig.inc("ev_act", gid))
        elif kind == "plain":
            eng.wait_ge(*sig.after("group", gid))
            nc.scalar.activation(ctx["scaled"](tag, u.evac[2] + b)[0], ps[:, :], ACT.Copy).then_inc(
                *sig.inc("ev_act", gid))
    if eng_name == "dve":
        if kind == "silu":
            g = ctx["g_slot"][gid]
            eng.wait_ge(*sig.after("ev_act", gid))
            z = ctx["scaled"](tag, u.evac[2] + b)[0]
            nc.vector.scalar_tensor_tensor(z, ctx["g"][:, g % GRING, :], 1.0, z, ALU.add,
                                           ALU.mult).then_inc(*sig.inc("silu", gid))
        elif kind == "biased":
            eng.wait_ge(*sig.after("group", gid))
            if b == 0:
                eng.wait_ge(*sig.after("tbias", u.evac[2]))
                for w in ctx["before"](tag):
                    eng.wait_ge(*sig.after(*w))
            nc.vector.tensor_tensor(ctx["t_dst"](tag, b), ps[:, 0:u.cols],
                                    mem.tbias[u.evac[2] % 2][:, 0:u.cols], ALU.add).then_inc(
                *sig.inc("ev_dve", gid))
        elif kind == "copy_t":
            eng.wait_ge(*sig.after("group", gid))
            nc.vector.tensor_copy(ctx["t_dst"](tag, b), ps[:, 0:u.cols]).then_inc(
                *sig.inc("ev_dve", gid))
        elif kind == "branch":
            fb = u.evac[2] + b
            gate_gid = ctx["gate_of"][(tag, fb)]
            eng.wait_ge(*sig.after("group", gid))
            eng.wait_ge(*sig.after("ev_act", gate_gid))
            if tag == "a":
                if fb == 0:
                    for w in ctx["before"]("merged"):
                        eng.wait_ge(*sig.after(*w))
                dst = ctx["merged"][:, fb, :]
            else:
                i = ctx["tmp_index"][gid]
                dst = ctx["tmp"][:, i % 2, :]
                if i >= 2:
                    eng.wait_ge(*sig.after("merge", i - 2))
            nc.vector.scalar_tensor_tensor(dst, ctx["g"][:, ctx["g_slot"][gate_gid] % GRING, :], 1.0,
                                           ps[:, :], ALU.add, ALU.mult).then_inc(
                *sig.inc("ev_dve", gid))
        elif kind == "residual":
            eng.wait_ge(*sig.after("group", gid))
            if b == 0:
                eng.wait_ge(*sig.after("residual"))
            c = u.evac[2]
            nc.vector.tensor_tensor(ctx["xt"][:, b, c:c + 512], ctx["xt"][:, b, c:c + 512],
                                    ps[:, :], ALU.add).then_inc(*sig.inc("ev_dve", gid))
    if eng_name == "pool" and kind == "branch" and tag != "a":
        fb = u.evac[2] + b
        i = ctx["tmp_index"][gid]
        eng.wait_ge(*sig.after("ev_dve", gid))
        if i == 0:
            eng.wait_ge(*sig.after("ev_dve", ctx["branch_gid"][("a", ND - 1)]))
        if i >= ND:
            eng.wait_ge(*sig.after("merge", i - ND))
        nc.gpsimd.tensor_tensor(ctx["merged"][:, fb, :], ctx["merged"][:, fb, :],
                                ctx["tmp"][:, i % 2, :], ALU.add).then_inc(*sig.inc("merge", i))


def gate_plan(stream):
    slot, used, gate_of, branch_gid, tmp_index, n, m = {}, {}, {}, {}, {}, 0, 0
    for gid in sorted(stream.by_gid):
        u, b = stream.by_gid[gid]
        if u.evac[0] in ("silu", "gate"):
            slot[gid] = n
            if u.evac[0] == "silu":
                used[n] = ("silu", gid)
            else:
                gate_of[(u.evac[1], u.evac[2] + b)] = gid
            n += 1
        elif u.evac[0] == "branch":
            branch_gid[(u.evac[1], u.evac[2] + b)] = gid
            if u.evac[1] != "a":
                tmp_index[gid] = m
                m += 1
    for key, gid in branch_gid.items():
        used[slot[gate_of[key]]] = ("ev_dve", gid)
    return dict(g_slot=slot, g_used=used, gate_of=gate_of, branch_gid=branch_gid,
                tmp_index=tmp_index)


def layer_units():
    units, what = [], []

    def f_blocks(evac, tag, col, nblocks, blk0=0):
        for i in range(0, nblocks, 2):
            units.append(Unit("F", "x", ND, 2 * P, (evac, tag, blk0 + i)))
            what.append(("in", 0, ND, col + i * P, 2 * P))

    def t_cols(evac, tag, col, section, src="x", w="in"):
        for half in range(2):
            units.append(Unit("T", src, 4, 512, (evac, tag, section), k0=4 * half, of=ND))
            what.append((w, 4 * half, 4, col, 512))

    def branch(tag, col):
        for half in range(2):
            f_blocks("gate", tag, col + 4 * half * P, 4, 4 * half)
            units.append(Unit("F", "y", NW, 512, ("branch", tag, 4 * half)))
            what.append(("br_" + tag, 0, NW, 512 * half, 512))

    f_blocks("scaled", "na_q", 0, NW)
    f_blocks("scaled", "na_k", WID, NW)
    t_cols("biased", "na_v", 2 * WID, 0)
    f_blocks("silu", "z_a", 3 * WID, NW)
    gq = 4 * WID
    t_cols("biased", "gq_q", gq, 1)
    units.append(Unit("T", "x", ND, 256, ("biased", "gq_kv", 2)))
    what.append(("in", 0, ND, gq + WID, 256))
    gz = gq + WID + 256
    sg = gz + WID
    t_cols("biased", "sg_u", sg, 3)
    t_cols("biased", "sg_v", sg + WID, 4)
    t_cols("biased", "sg_z", sg + 2 * WID, 5)
    f_blocks("silu", "z_b", gz, NW)
    gates = sg + 3 * WID
    branch("a", gates)
    branch("c", gates + 2 * D)
    branch("b", gates + D)
    for c in (0, 512):
        t_cols("residual", "out", c, c, src="m", w="out")
    return units, what


F_BIAS = [(0, NW, SM), (WID, NW, 1.0), (3 * WID, NW, 0.5), (4 * WID + WID + 256, NW, 0.5),
          (5 * WID + 256 + 4 * WID, 3 * ND, 0.5)]
F_BLOCK = {"na_q": 0, "na_k": 4, "z_a": 8, "z_b": 12, "a": 16, "b": 24, "c": 32}
NF = 40


def layer_phase(nc, sig, mem, d, layer):
    units, _ = layer_units()
    n_units = len(units)
    at = mem.at
    nq = at("na_q", 0, [P, NW, SEQ])
    nk = at("na_k", 8, [P, NW, SEQ])
    nv = at("na_v", 16, [P, NT, WID])
    yh = at("y_hi", 0, [P, NW, SEQ], F32R)
    yl = at("y_lo", 8, [P, NW, SEQ], F32R)
    sz = at("sg_z", 0, [P, NT, WID])
    sgw = at("sg_w", 8, [P, 8, P])
    sgg = at("sg_g", 12, [P, WID])
    sgbeta = at("sg_beta", 14, [P, WID])
    qkg = at("qk_g", 16, [P, 10, HD])
    yc = at("y_c", 16, [P, NW, SEQ])
    gamma = at("gamma", 16, [P, D])
    beta = at("beta", 20, [P, D])
    qk = at("gq_qk", 24, [P, NT, 640])
    yb = at("y_b", 24, [P, NW, SEQ])
    mh = at("m_hi", 24, [P, ND, SEQ], F32R)
    ml = at("m_lo", 40, [P, ND, SEQ], F32R)
    gv = at("gq_v", 34, [P, NT, P])
    gq = at("gq_q", 36, [P, NW, SEQ])
    gk = at("gq_k", 44, [P, 2, SEQ])
    probs = at("probs", 48, [P, 3, SEQ])
    pt = at("probs_t", 54, [P, 2, NT, SEQ])
    sgt = at("sg_tanh", 54, [P, NT, WID])
    nab = at("na_bias", 70, [P, 2, 14 * GRID])
    xt = at("x_t", 58, [P, NT, D])
    sq = at("squares", 70, [P, 640])
    ro = at("rotated", 72.5, [P, 6 * P])
    su = at("sg_u", 77, [P, NT, WID])
    sv = at("sg_v", 85, [P, NT, WID])
    merged = at("merged", 77, [P, ND, SEQ])
    ya = at("y_a", 93, [P, NW, SEQ])
    bout = at("b_out", 93, [P, D])
    tmp = at("branch_tmp", 97, [P, 2, SEQ])
    g = at("gates", 101, [P, GRING, SEQ])
    sgb = mem.small[:, 96:104]
    ss, r = mem.small[:, 104:114], mem.small[:, 114:124]
    sst = mem.small[:, 124:148].rearrange("p (t s) -> p t s", s=6)
    smv = mem.small[:, 148:156].rearrange("p (t s) -> p t s", s=2)
    srs = mem.small[:, 156:160]
    fb_raw = mem.small[:, 160:160 + NF]
    fb_ = mem.small[:, 200:200 + NF]
    fscale = mem.small[:, 240:240 + NF]
    cos = mem.rope[:, 0:NT * 32].rearrange("p (t f) -> p t f", f=32)
    sin = mem.rope[:, NT * 32:].rearrange("p (t f) -> p t f", f=32)

    w_dram = lambda n: d["w1"][bass.ds(layer, 1), n].rearrange("o p c -> (o p) c")
    gid_of = {}

    def ready(u):
        if u.src == "y":
            return [("y_lo", u.evac[1])]
        if u.src == "m":
            return [("m_lo", 4 * (u.k0 // 4) + 3)]
        return []

    st = Stream(nc, sig, mem, units, w_dram, {"x": (mem.xh, mem.xl), "y": (yh, yl), "m": (mh, ml)},
                ready)
    for gid, (u, b) in st.by_gid.items():
        gid_of[(u.evac[1], u.evac[2] + b if u.kind == "F" else b)] = gid
        if u.evac[0] == "residual":
            gid_of[("out", u.evac[2], b)] = gid
    G = gid_of.get
    last_u = {u.evac[1]: n for n, u in enumerate(units)}

    def before(tag):
        return {"sg_z": [("na_pv", HEADS - 1)], "z_b": [("rope_done", NT - 1)],
                "merged": [("yct", NW - 1), ("mix", 3)]}.get(tag, [])

    dst = {"na_q": nq, "na_k": nk, "z_a": ya, "z_b": yb}
    ctx = dict(g=g, merged=merged, tmp=tmp, xt=xt, before=before, **gate_plan(st))
    ctx["scaled"] = lambda tag, b: (dst[tag][:, b, :], fb_[:, F_BLOCK[tag] + b:F_BLOCK[tag] + b + 1],
                                    SM if tag == "na_q" else 1.0)
    ctx["half_bias"] = lambda tag, b: fb_[:, F_BLOCK[tag] + b:F_BLOCK[tag] + b + 1]
    ctx["t_dst"] = lambda tag, t: {"na_v": nv[:, t, :], "gq_q": qk[:, t, 0:WID], "sg_u": su[:, t, :],
                                   "sg_v": sv[:, t, :], "sg_z": sz[:, t, :]}[tag]

    na = Attention(
        nc, sig, mem, "na",
        q=lambda h, i: nq[(h % 2) * HD:(h % 2) * HD + HD, h // 2, i * P:(i + 1) * P],
        k=lambda h: nk[(h % 2) * HD:(h % 2) * HD + HD, h // 2, :],
        v=lambda h, kb: nv[:, kb, h * HD:(h + 1) * HD], y=ya, causal=False,
        bias=lambda h, i: (nab[:, h % 2, (6 - 2 * i) * GRID:(6 - 2 * i) * GRID + SEQ],
                           ("na_bias", h)),
        probs=probs, pt=pt, gate=lambda h: ("silu", G(("z_a", h // 2))),
        needs=lambda h: [("ev_act", G(("na_k", h // 2))), ("ev_dve", G(("na_v", NT - 1)))])
    gqa = Attention(
        nc, sig, mem, "gq",
        q=lambda h, i: gq[(h % 2) * HD:(h % 2) * HD + HD, h // 2, i * P:(i + 1) * P],
        k=lambda h: gk[(h % 2) * HD:(h % 2) * HD + HD, h // 4, :],
        v=lambda h, kb: gv[:, kb, (h // 4) * HD:(h // 4) * HD + HD], y=yb, causal=False,
        bias=None, probs=probs, pt=pt, scale=SM, gate=lambda h: ("silu", G(("z_b", h // 2))),
        base=[("na_y", HEADS - 1), ("rot_kept", NT - 1), ("ycf", NW - 1), ("mixed", 3)],
        needs=lambda h: [])
    ln = LayerNorm(nc, sig, mem, xt, gamma, beta, lambda t: d["resid"][t], banks=(4, 5),
                   source=lambda t: ("ev_dve", G(("out", 512, t))))

    steps = []
    order = [(n, q) for n in range(n_units) for q in range(4)]
    i_na = next(n for n, u in enumerate(units) if u.evac[1] == "z_a") * 4
    i_sz = next(n for n, u in enumerate(units) if u.evac[1] == "sg_z") * 4
    i_zb = next(n for n, u in enumerate(units) if u.evac[1] == "z_b") * 4
    i_br = next(n for n, u in enumerate(units) if u.evac[1] == "a") * 4
    extras = {}

    def extra(at_step, *e):
        extras.setdefault(at_step, []).append(e)

    spare = Attention.STEPS - (i_sz - i_na)
    for j in range(Attention.STEPS):
        extra(min(i_na + j, i_sz - 1), "na", j)
    assert spare < 8
    for t in range(NT):
        extra(i_sz + 2 * t, "prep", t)
        extra(i_sz + 2 * t + 1, "vnorm", t)
    for p in range(4):
        extra(i_zb + 1 + p, "mix", p)
    extra(i_zb + 5, "sg_gate")
    for f in range(NW):
        extra(i_zb + 7 if f < 2 else i_br, "yct", f)
    extra(i_br, "y_split", "a")
    for j in range(Attention.STEPS):
        extra(i_br + 1 + j, "gq", j)
    n_c = next(n for n, u in enumerate(units) if u.evac[:2] == ("branch", "c")) * 4
    extra(n_c - 3, "y_split", "c")
    extra(4 * last_u["c"] + 4, "y_split", "b")
    assert 4 * last_u["a"] + 3 < n_c - 3
    i_out = next(n for n, u in enumerate(units) if u.evac[1] == "out") * 4
    for fb in range(ND):
        n_b = [n for n, u in enumerate(units) if u.evac[:2] == ("branch", "b")][fb // 4]
        extra(4 * n_b + fb % 4, "m_split", fb)
    for t in range(NT):
        extra(4 * n_units - 4 + t, "ln", t)
    steps = [(n, q, extras.get(4 * n + q, [])) for n, q in order]
    assert max(extras) < len(order)

    y_of = {"a": (ya, "na_y"), "c": (yc, None), "b": (yb, "gq_y")}

    def split_y_hi(act, tag):
        y, head = y_of[tag]
        if tag == "a":
            act.wait_ge(*sig.after("sg_y"))
            act.wait_ge(*sig.after("mix", 3))
            act.wait_ge(*sig.after("na_y", HEADS - 1))
        elif tag == "c":
            act.wait_ge(*sig.after("unit_done", last_unit("branch", "a")))
        else:
            act.wait_ge(*sig.after("unit_done", last_unit("branch", "c")))
            act.wait_ge(*sig.after("gq_y", HEADS - 1))
        nc.scalar.activation(yh[:, :, :], y[:, :, :], ACT.Copy).then_inc(*sig.inc("y_hi", tag))

    def last_unit(kind, tag):
        return max(n for n, u in enumerate(units) if u.evac[:2] == (kind, tag))

    def rope(dve, t):
        dve.wait_ge(*sig.after("squared", t))
        nc.vector.tensor_reduce(ss, sq[:, :].rearrange("p (h c) -> p h c", c=HD), AX.X,
                                ALU.add).then_inc(*sig.inc("sum_square", t))
        dve.wait_ge(*sig.after("sum_square", t))
        nc.vector.tensor_scalar(ss, ss, 1.0 / HD, RMS_EPS, ALU.mult, ALU.add).then_inc(
            *sig.inc("mean_square", t))
        dve.wait_ge(*sig.after("qk_normed", t))
        x = qk[:, t, :].rearrange("p (h c two) -> p h c two", c=HD // 2, two=2)
        x0, x1 = x[:, :, :, 0], x[:, :, :, 1]
        c = cos[:, t, :].unsqueeze(1).broadcast_to([P, 10, 32])
        s = sin[:, t, :].unsqueeze(1).broadcast_to([P, 10, 32])
        a = sq[:, 0:320].rearrange("p (h c) -> p h c", c=32)
        b = sq[:, 320:640].rearrange("p (h c) -> p h c", c=32)
        oq = ro[:, 0:WID].rearrange("p (h c two) -> p h c two", c=32, two=2)
        ok = ro[:, WID:].rearrange("p (h r c two) -> p h r c two", r=2, c=32, two=2)
        for part, (f0, f1, op) in enumerate(((c, s, ALU.subtract), (s, c, ALU.add))):
            nc.vector.tensor_tensor(a, x0, f0, ALU.mult)
            nc.vector.tensor_tensor(b, x1, f1, ALU.mult).then_inc(
                *sig.inc("rope_products", t, part))
            dve.wait_ge(*sig.after("rope_products", t, part))
            if t and part == 0:
                dve.wait_ge(*sig.after("rot_transposed", t - 1))
            nc.vector.tensor_tensor(oq[:, :, :, part], a[:, 0:8, :], b[:, 0:8, :], op)
            for rep in range(2):
                ins = nc.vector.tensor_tensor(ok[:, :, rep, :, part], a[:, 8:10, :],
                                              b[:, 8:10, :], op)
            ins.then_inc(*sig.inc("rope_out", t, part))
            dve.wait_ge(*sig.after("rope_out", t, part))
        sig.seen[(sig.phase, "rope_done", t)] = ("rope_out", t, 1)

    with nc.Block() as block:
        @block.sync
        def _(sp):
            for n in range(n_units):
                st.load(sp, n)
            for t in range(NT):
                ln.store(sp, t)
            sp.wait_ge(*sig.after("ln_stored", NT - 1))

        @block.gpsimd
        def _(pool):
            for n, q, ex in steps:
                u = units[n]
                for e in ex:
                    if e[0] == "prep":
                        t = e[1]
                        if t == 0:
                            pool.wait_ge(*sig.after("ev_dve", G(("gq_kv", NT - 1))))
                            pool.wait_ge(*sig.after("na_max", HEADS * NT - 1))
                            pool.wait_ge(*sig.after("qk_g"))
                        else:
                            pool.wait_ge(*sig.after("rope_done", t - 1))
                        heads = qk[:, t, :].rearrange("p (h c) -> p h c", c=HD)
                        nc.gpsimd.tensor_tensor(sq[:, :], qk[:, t, :], qk[:, t, :],
                                                ALU.mult).then_inc(*sig.inc("squared", t))
                        pool.wait_ge(*sig.after("mean_square", t))
                        nc.gpsimd.tensor_tensor(r, ss, mem.half[:, 0:10], ALU.pow).then_inc(
                            *sig.inc("rms", t))
                        pool.wait_ge(*sig.after("rms", t))
                        nc.gpsimd.tensor_tensor(heads, heads,
                                                r.unsqueeze(2).broadcast_to([P, 10, HD]),
                                                ALU.mult).then_inc(*sig.inc("rms_scaled", t))
                        pool.wait_ge(*sig.after("rms_scaled", t))
                        nc.gpsimd.tensor_tensor(heads, heads, qkg[:, :, :], ALU.mult).then_inc(
                            *sig.inc("qk_normed", t))
                    if e[0] == "vnorm":
                        t = e[1]
                        if t == 0:
                            pool.wait_ge(*sig.after("sg_g"))
                            pool.wait_ge(*sig.after("sg_beta"))
                        pool.wait_ge(*sig.after("sv_var", t))
                        nc.gpsimd.tensor_tensor(srs[:, t:t + 1], smv[:, t, 1:2], mem.half[:, 0:1],
                                                ALU.pow).then_inc(*sig.inc("sv_rstd", t))
                        pool.wait_ge(*sig.after("sv_centred", t))
                        nc.gpsimd.tensor_tensor(sv[:, t, :], sv[:, t, :], sgg[:, :],
                                                ALU.mult).then_inc(*sig.inc("sv_scaled", t))
                        pool.wait_ge(*sig.after("sv_scaled", t))
                        nc.gpsimd.tensor_tensor(sv[:, t, :], sv[:, t, :], sgbeta[:, :],
                                                ALU.add).then_inc(*sig.inc("sv_ready", t))
                for gid, b in [(gg, bb) for gg, (uu, bb) in st.by_gid.items() if uu is u]:
                    if completes(u, q, b):
                        emit_common_evac(nc, sig, mem, st, u, b, gid, "pool", pool, ctx)
                if n == i_out // 4 and q == 0:
                    pool.wait_ge(*sig.after("x_t_loaded"))
                    pool.wait_ge(*sig.after("b_out"))
                    nc.gpsimd.tensor_scalar(xt[:, :, :], xt[:, :, :], ALPHA_1, None,
                                            ALU.mult).then_inc(*sig.inc("x_scaled"))
                    pool.wait_ge(*sig.after("x_scaled"))
                    for t in range(NT):
                        ins = nc.gpsimd.tensor_tensor(xt[:, t, :], xt[:, t, :], bout[:, :], ALU.add)
                    ins.then_inc(*sig.inc("residual"))
                for e in ex:
                    if e[0] == "ln":
                        ln.power(pool, e[1])
                        ln.affine(pool, e[1])

        @block.scalar
        def _(act):
            one = lambda ap, n: ap.rearrange("o c -> (o c)").partition_broadcast(P)
            act.dma_start(fb_raw, d["f_bias"][bass.ds(layer, 1)].rearrange("o p c -> (o p) c")
                           ).then_inc(*sig.inc("f_bias_raw", by=16))
            act.dma_start(fscale, d["f_scale"]).then_inc(*sig.inc("f_scale", by=16))
            act.dma_start(sgb, d["sg_b"][bass.ds(layer, 1)].rearrange("o p c -> (o p) c")).then_inc(
                *sig.inc("sg_b", by=16))

            def tbias(m):
                cols = 256 if m == 2 else 512
                if m >= 2:
                    tag = ("na_v", "gq_q", "gq_kv", "sg_u", "sg_v", "sg_z")[m - 2]
                    act.wait_ge(*sig.after("ev_dve", G((tag, NT - 1))))
                act.dma_start(mem.tbias[m % 2][:, 0:cols],
                               one(d["t_bias"][bass.ds(layer, 1), m * 512:m * 512 + cols], cols)
                               ).then_inc(*sig.inc(f"tbias_{m % 2}", m, by=16))
                sig.seen[(sig.phase, "tbias", m)] = (f"tbias_{m % 2}", m)

            def na_bias(h):
                if h >= 2:
                    act.wait_ge(*sig.after("na_max", 4 * (h - 2) + 3))
                act.dma_start(nab[:, h % 2, :], d["na_bias"][bass.ds(layer, 1), h].rearrange(
                    "o p c -> (o p) c")).then_inc(*sig.inc(f"na_bias_{h % 2}", h, by=16))
                sig.seen[(sig.phase, "na_bias", h)] = (f"na_bias_{h % 2}", h)

            for m in range(2):
                tbias(m)
            for h in range(2):
                na_bias(h)
            st.hi(act, 0)
            act.wait_ge(*sig.after("f_bias"))
            for n, q, ex in steps:
                u = units[n]
                if q == 0:
                    st.hi(act, n + 1)
                for gid, b in [(gg, bb) for gg, (uu, bb) in st.by_gid.items() if uu is u]:
                    if completes(u, q, b):
                        emit_common_evac(nc, sig, mem, st, u, b, gid, "act", act, ctx)
                for e in ex:
                    if e[0] == "na":
                        na.on_act(act, e[1])
                    if e[0] == "gq":
                        gqa.on_act(act, e[1])
                    if e[0] == "prep":
                        t = e[1]
                        act.wait_ge(*sig.after("rot_transposed", t))
                        nc.scalar.activation(gq[:, :, t * P:(t + 1) * P],
                                             mem.bank[4][:, :].rearrange("p (f c) -> p f c", c=P),
                                             ACT.Copy)
                        nc.scalar.activation(gk[:, :, t * P:(t + 1) * P],
                                             mem.bank[5][:, 0:2 * P].rearrange(
                                                 "p (f c) -> p f c", c=P),
                                             ACT.Copy).then_inc(*sig.inc("rot_kept", t))
                    if e == ("mix", 0):
                        act.wait_ge(*sig.after("ev_dve", G(("sg_z", NT - 1))))
                        act.wait_ge(*sig.after("na_pv", HEADS - 1))
                        for t in range(NT):
                            nc.scalar.activation(sgt[:, t, :], sz[:, t, :], ACT.Tanh,
                                                 scale=0.5).then_inc(*sig.inc("sg_tanh", t))
                    if e[0] == "yct":
                        f = e[1]
                        act.wait_ge(*sig.after("yct", f))
                        if f == 0:
                            act.wait_ge(*sig.after("qk_normed", NT - 1))
                        nc.scalar.activation(yc[:, f, :], mem.bank[4 + f][:, :], ACT.Copy).then_inc(
                            *sig.inc("ycf", f))
                    if e[0] == "y_split":
                        split_y_hi(act, e[1])
                    if e[0] == "m_split":
                        fb = e[1]
                        act.wait_ge(*sig.after("merge", ND + fb))
                        nc.scalar.activation(mh[:, fb, :], merged[:, fb, :], ACT.Copy,
                                             scale=0.5).then_inc(*sig.inc("m_hi", fb))
                    if e[0] == "ln":
                        ln.split_hi(act, e[1])
                    if e[0] == "na" and e[1] % 4 == 3 and 2 <= (e[1] + 1) // 4 + 1 < HEADS:
                        na_bias((e[1] + 1) // 4 + 1)
                    if e == ("na", Attention.STEPS - 1):
                        act.wait_ge(*sig.after("na_pv", HEADS - 1))
                        act.dma_start(qkg[:, :, :], one(d["qk_g"][bass.ds(layer, 1)], 640).rearrange(
                            "p (h c) -> p h c", c=HD)).then_inc(*sig.inc("qk_g", by=16))
                        act.dma_start(sgg[:, :], one(d["sg_gb"][bass.ds(layer, 1), 0], 512)
                                       ).then_inc(*sig.inc("sg_g", by=16))
                        act.dma_start(sgbeta[:, :], one(d["sg_gb"][bass.ds(layer, 1), 1], 512)
                                       ).then_inc(*sig.inc("sg_beta", by=16))
                        act.dma_start(sgw[:, :, :], d["sg_w"][bass.ds(layer, 1)].rearrange(
                            "o p g c -> (o p) g c")).then_inc(*sig.inc("sg_w", by=16))
                    if e == ("y_split", "c"):
                        act.wait_ge(*sig.after("y_lo", "a"))
                        act.dma_start(bout[:, :], one(d["b_out"][bass.ds(layer, 1)], D)).then_inc(
                            *sig.inc("b_out", by=16))
                    if e == ("y_split", "b"):
                        act.wait_ge(*sig.after("y_lo", "c"))
                        for i, row in enumerate((gamma, beta)):
                            act.dma_start(row[:, :], one(d["ln_post"][bass.ds(layer, 1), i], D)
                                           ).then_inc(*sig.inc("ln_params", i, by=16))
                        sig.seen[(sig.phase, "ln_params")] = ("ln_params", 1)
                        act.wait_ge(*sig.after("gq_y", HEADS - 1))
                        act.dma_start(xt[:, :, :], d["resid"].rearrange("t p c -> p t c")).then_inc(
                            *sig.inc("x_t_loaded", by=16))
                tags = ("na_v", "gq_q", "gq_kv", "sg_u", "sg_v", "sg_z")
                if u.evac[1] in tags and q == 3 and u.k0 + u.nk == ND:
                    m = tags.index(u.evac[1]) + 2
                    if m < len(tags):
                        tbias(m)

        @block.vector
        def _(dve):
            st.lo(dve, 0)
            dve.wait_ge(*sig.after("f_bias_raw"))
            dve.wait_ge(*sig.after("f_scale"))
            nc.vector.tensor_tensor(fb_, fb_raw, fscale, ALU.mult).then_inc(*sig.inc("f_bias"))
            for n, q, ex in steps:
                u = units[n]
                if q == 0:
                    st.lo(dve, n + 1)
                for gid, b in [(gg, bb) for gg, (uu, bb) in st.by_gid.items() if uu is u]:
                    if completes(u, q, b):
                        if u.evac[1] == "gq_kv":
                            dve.wait_ge(*sig.after("group", gid))
                            if b == 0:
                                dve.wait_ge(*sig.after("tbias", 2))
                            nc.vector.tensor_tensor(qk[:, b, WID:WID + P], st.bank(gid)[:, 0:P],
                                                    mem.tbias[0][:, 0:P], ALU.add)
                            nc.vector.tensor_tensor(gv[:, b, :], st.bank(gid)[:, P:2 * P],
                                                    mem.tbias[0][:, P:2 * P], ALU.add).then_inc(
                                *sig.inc("ev_dve", gid))
                        else:
                            emit_common_evac(nc, sig, mem, st, u, b, gid, "dve", dve, ctx)
                for e in ex:
                    if e[0] == "na":
                        na.on_dve(dve, e[1])
                    if e[0] == "gq":
                        gqa.on_dve(dve, e[1])
                    if e[0] == "prep":
                        rope(dve, e[1])
                    if e[0] == "vnorm":
                        t = e[1]
                        dve.wait_ge(*sig.after("ev_dve", G(("sg_v", t))))
                        nc.vector.bn_stats(sst[:, t, :], sv[:, t, :]).then_inc(
                            *sig.inc("sv_stats", t))
                        dve.wait_ge(*sig.after("sv_stats", t))
                        nc.vector.bn_aggr(smv[:, t, :], sst[:, t, :]).then_inc(*sig.inc("sv_mv", t))
                        dve.wait_ge(*sig.after("sv_mv", t))
                        nc.vector.tensor_scalar(smv[:, t, 1:2], smv[:, t, 1:2], LN_EPS, None,
                                                ALU.add).then_inc(*sig.inc("sv_var", t))
                        dve.wait_ge(*sig.after("sv_rstd", t))
                        nc.vector.tensor_scalar(sv[:, t, :], sv[:, t, :], smv[:, t, 0:1],
                                                srs[:, t:t + 1], ALU.subtract, ALU.mult).then_inc(
                            *sig.inc("sv_centred", t))
                    if e[0] == "mix":
                        p = e[1]
                        dve.wait_ge(*sig.after("mix", p))
                        if p == 0:
                            dve.wait_ge(*sig.after("sg_b"))
                            dve.wait_ge(*sig.after("ev_dve", G(("sg_u", NT - 1))))
                        for i in range(2):
                            gg = 2 * p + i
                            cols = su[:, :, gg * HD:(gg + 1) * HD]
                            ins = nc.vector.scalar_tensor_tensor(
                                cols, mem.bank[4 + p][:, i * 256:(i + 1) * 256].rearrange(
                                    "p (c d) -> p c d", d=HD), sgb[:, gg:gg + 1], cols,
                                ALU.add, ALU.mult)
                        ins.then_inc(*sig.inc("mixed", p))
                    if e == ("sg_gate",):
                        dve.wait_ge(*sig.after("mixed", 3))
                        for t in range(NT):
                            dve.wait_ge(*sig.after("sg_tanh", t))
                            nc.vector.scalar_tensor_tensor(
                                sz[:, t, :], sgt[:, t, :], 1.0, sz[:, t, :], ALU.add,
                                ALU.mult).then_inc(*sig.inc("sg_silu", t))
                            dve.wait_ge(*sig.after("sg_silu", t))
                            ins = nc.vector.scalar_tensor_tensor(
                                su[:, t, :], su[:, t, :], 0.5, sz[:, t, :], ALU.mult, ALU.mult)
                        ins.then_inc(*sig.inc("sg_y"))
                    if e[0] == "y_split":
                        y, _ = y_of[e[1]]
                        dve.wait_ge(*sig.after("y_hi", e[1]))
                        nc.vector.tensor_tensor(yl[:, :, :], y[:, :, :], yh[:, :, :].bitcast(F32),
                                                ALU.subtract).then_inc(*sig.inc("y_lo", e[1]))
                    if e[0] == "m_split":
                        fb = e[1]
                        dve.wait_ge(*sig.after("m_hi", fb))
                        nc.vector.scalar_tensor_tensor(
                            ml[:, fb, :], merged[:, fb, :], 0.5, mh[:, fb, :].bitcast(F32), ALU.mult,
                            ALU.subtract).then_inc(*sig.inc("m_lo", fb))
                    if e[0] == "ln":
                        ln.statistics(dve, e[1])
                        ln.normalise(dve, e[1])
                        ln.split_lo(dve, e[1])

        @block.tensor
        def _(pe):
            for n, q, ex in steps:
                st.multiply(pe, n, q)
                for e in ex:
                    if e[0] == "na":
                        na.on_pe(pe, e[1])
                    if e[0] == "gq":
                        gqa.on_pe(pe, e[1])
                    if e[0] == "prep":
                        t = e[1]
                        pe.wait_ge(*sig.after("rope_done", t))
                        if t:
                            pe.wait_ge(*sig.after("rot_kept", t - 1))
                        else:
                            pe.wait_ge(*sig.after("na_exp", HEADS * NT - 1))
                        for f in range(6):
                            last = nc.tensor.transpose(
                                mem.bank[4 + f // 4][:, (f % 4) * P:(f % 4 + 1) * P],
                                ro[:, f * P:(f + 1) * P], mem.ident[:, :])
                        last.then_inc(*sig.inc("rot_transposed", t))
                    if e[0] == "mix":
                        p = e[1]
                        if p == 0:
                            pe.wait_ge(*sig.after("sg_w"))
                            pe.wait_ge(*sig.after("sv_ready", NT - 1))
                            pe.wait_ge(*sig.after("rot_kept", NT - 1))
                            pe.wait_ge(*sig.after("na_y", HEADS - 1))
                            pe.wait_ge(*sig.after("na_pt", HEADS * NT - 1))
                        for i in range(2):
                            gg = 2 * p + i
                            last = nc.tensor.matmul(
                                mem.bank[4 + p][:, i * 256:(i + 1) * 256].rearrange(
                                    "p (c d) -> p c d", d=HD), sgw[:, gg, :],
                                sv[:, :, gg * HD:(gg + 1) * HD], start=True, stop=True)
                        last.then_inc(*sig.inc("mix", p))
                    if e[0] == "yct":
                        f = e[1]
                        pe.wait_ge(*sig.after("sg_y"))
                        pe.wait_ge(*sig.after("mixed", f))
                        for t in range(NT):
                            last = nc.tensor.transpose(mem.bank[4 + f][:, t * P:(t + 1) * P],
                                                       su[:, t, f * P:(f + 1) * P], mem.ident[:, :])
                        last.then_inc(*sig.inc("yct", f))
                    if e[0] == "ln":
                        ln.transpose(pe, e[1])


def completes(u, q, b):
    if u.kind == "F" and u.cols == 2 * P:
        return q == 2 * b + 1
    return q == b and u.k0 + u.nk == u.of


C_F = 3 * WID
C_Z = C_F + HEADS
C_XBC = C_Z + WID
NXBC = 6
C_DT = C_XBC + NXBC * P
C_U = C_DT + HEADS
C_GATE = C_U + WID
S5_TILES = 16
S5_IT = 16
S5_LAG = 3
TWO_PI_PARTS = (6.28125, 0.0019350051879882812, 3.019915981956753e-07)
ROUND = 12582912.0
PI_BELOW = 3.1415925
D_FF = 2816
NF2 = D_FF // P
GELU_A, GELU_B = 0.044715, 0.7978845608028654


def mixer_units():
    units, what = [], []

    def f_blocks(evac, tag, col, nblocks, blk0=0):
        for i in range(0, nblocks, 2):
            units.append(Unit("F", "x", ND, 2 * P, (evac, tag, blk0 + i)))
            what.append(("in", 0, ND, col + i * P, 2 * P))

    def t_cols(evac, tag, col, section, src="x", w="in"):
        for half in range(2):
            units.append(Unit("T", src, 4, 512, (evac, tag, section), k0=4 * half, of=ND))
            what.append((w, 4 * half, 4, col, 512))

    units.append(Unit("T", "x", ND, 16, ("copy_t", "fdt", 0)))
    what.append(("fdt", 0, ND, 0, 16))
    f_blocks("plain", "fq", 0, NW)
    f_blocks("plain", "fk", WID, NW)
    t_cols("copy_t", "fv", 2 * WID, 0)
    t_cols("copy_t", "z", C_Z, 0)
    f_blocks("plain", "xbc", C_XBC, NXBC)
    f_blocks("plain", "u", C_U, NW)
    for r, tag in enumerate("abc"):
        for half in range(2):
            f_blocks("gate", tag, C_GATE + r * D + 4 * half * P, 4, 4 * half)
            if tag == "c" and half == 0:
                units.append(Unit("F", "y", NW, 512, ("glu", "glu", 0)))
                what.append(("glu", 0, NW, 0, 512))
            units.append(Unit("F", "y", NW, 512, ("branch", tag, 4 * half)))
            what.append(("br_" + tag, 0, NW, 512 * half, 512))
    for c in (0, 512):
        t_cols("residual", "out", c, c, src="m", w="out")
    return units, what


def mixer_phase(nc, sig, mem, d):
    units, _ = mixer_units()
    n_units = len(units)
    at = lambda name, *a: mem.at("mx_" + name, *a)
    fq = at("fox_q", 0, [P, NW, SEQ])
    fk = at("fox_k", 8, [P, NW, SEQ])
    fv = at("fox_v", 16, [P, NT, WID])
    yh = at("y_hi", 0, [P, NW, SEQ], F32R)
    yl = at("y_lo", 8, [P, NW, SEQ], F32R)
    xh = at("ssd_x", 16, [P, NT, WID])
    ct = at("s5_c", 16, [P, 2, S5_TILES, 32])
    bbt = at("s5_bt", 20, [P, 2, 4, P])
    gamma = at("gamma", 16, [P, D])
    beta = at("beta", 20, [P, D])
    minus_cum = at("minus_cum", 24, [P, HEADS, SEQ])
    merged = at("merged", 24, [P, ND, SEQ])
    z = at("z", 40, [P, NT, WID])
    yb = at("y_b", 40, [P, NW, SEQ])
    yc = at("y_c", 40, [P, NW, SEQ])
    ones = at("ones", 48, [P, P])
    probs = at("probs", 48, [P, 3, SEQ])
    pt = at("probs_t", 54, [P, 2, NT, SEQ])
    xdt = at("ssd_xdt", 48, [P, NT, WID])
    states = at("ssd_states", 56, [P, 3, WID])
    xdd = at("ssd_x_decayed", 62, [P, WID])
    bt = at("ssd_b_t", 64, [P, NT, P])
    cbm = at("ssd_cb", 66, [P, 2, SEQ])
    norm_w = at("ssd_norm_w", 56, [P, WID])
    ctab = at("s5_cos", 48, [P, 2, SEQ])
    stab = at("s5_sin", 52, [P, 2, SEQ])
    mtab = at("s5_mag", 56, [P, 2, SEQ])
    w_s5 = at("s5_w", 60, [P, 2, 2, SEQ])
    p_s5 = at("s5_p", 68, [P, 2, 4, SEQ])
    acc = at("conv_acc", 70, [P, SEQ])
    xbc = at("xbc", 72, [P, NXBC, SEQ + 3])
    yt = at("ssd_y", 72, [P, NT, WID])
    u_ = at("s5_u", 84.5, [P, NW, SEQ])
    tri = at("tri", 92.5, [P, P])
    ya = at("y_a", 93, [P, NW, SEQ])
    seg = at("ssd_seg", 93, [P, 2, SEQ])
    ubd = at("s5_u_blocks", 93, [P, 2, SEQ])
    tmp = at("branch_tmp", 97, [P, 2, SEQ])
    g = at("gates", 101, [P, GRING, SEQ])
    s5p = at("s5_params", 109, [P, 16, 16])
    mh = at("m_hi", 44, [P, ND, SEQ], F32R)
    ml = at("m_lo", 60, [P, ND, SEQ], F32R)
    xt = at("x_t", 76, [P, NT, D])
    sm = lambda a, b: mem.small[:, a:b]
    fd = sm(104, 168).rearrange("p (t c) -> p t c", c=16)
    e_ = sm(168, 232).rearrange("p (t c) -> p t c", c=16)
    l_ = sm(232, 296).rearrange("p (t c) -> p t c", c=16)
    w_ = sm(296, 360).rearrange("p (t c) -> p t c", c=16)
    cums = sm(360, 424).rearrange("p (t c) -> p t c", c=16)
    tot = sm(424, 456).rearrange("p (t h) -> p t h", h=8)
    dte = sm(456, 488).rearrange("p (t h) -> p t h", h=8)
    r8 = sm(488, 496)
    dskip = sm(496, 504)
    a_neg = sm(504, 512)
    bias16 = mem.small2[:, 0:16]
    cw = mem.small2[:, 16:46].rearrange("p (f k) -> p f k", k=5)
    s5d = mem.small2[:, 46:50]
    glub = mem.small2[:, 50:54]
    dout = mem.small2[:, 54:86].rearrange("p (t h) -> p t h", h=8)
    ncum = mem.small2[:, 86:118].rearrange("p (t h) -> p t h", h=8)
    pre = mem.small2[:, 118:150].rearrange("p (t h) -> p t h", h=8)
    lf = mem.small2[:, 150:182].rearrange("p (t h) -> p t h", h=8)
    adt = mem.small2[:, 182:214].rearrange("p (t h) -> p t h", h=8)
    gb = mem.small2[:, 214:238]
    nacs = mem.small2[:, 238:270].rearrange("p (t h) -> p t h", h=8)
    carry = mem.small2[:, 270:302].rearrange("p (k a i) -> p k a i", k=4, i=4)
    t4 = mem.small2[:, 302:334]
    qmask = mem.small2[:, 334:338]
    ones4 = mem.small2[:, 338:342]
    cum_f = at("row_sums", 50, [16, SEQ])

    w_dram = lambda n: d["w2"][n]

    def ready(u):
        if u.src == "y":
            return [("y_lo", "gy" if u.evac[0] == "glu" else u.evac[1])]
        if u.src == "m":
            return [("m_lo", 4 * (u.k0 // 4) + 3)]
        return []

    n_glu = next(n for n, u in enumerate(units) if u.evac[0] == "glu")
    n_s5 = next(n for n, u in enumerate(units) if u.evac[:2] == ("gate", "b"))
    for u in units[n_s5:n_glu]:
        u.banks = 3
    st = Stream(nc, sig, mem, units, w_dram, {"x": (mem.xh, mem.xl), "y": (yh, yl), "m": (mh, ml)},
                ready)
    last_in_3 = max(g for g, (u, _) in st.by_gid.items() if st.bank_of[g] == 3 and u.n_ < n_s5)
    gid_of = {}
    for gid, (u, b) in st.by_gid.items():
        gid_of[(u.evac[1], u.evac[2] + b if u.kind == "F" else b)] = gid
        if u.evac[0] == "residual":
            gid_of[("out", u.evac[2], b)] = gid
    G = gid_of.get
    first_u = {}
    for n, u in enumerate(units):
        first_u.setdefault(u.evac[:2], n)
    last_u = {u.evac[:2]: n for n, u in enumerate(units)}

    def before(tag):
        return {"merged": [("a_y", HEADS - 1)]}.get(tag, [])

    plain = {"fq": fq, "fk": fk, "u": u_}
    ctx = dict(g=g, merged=merged, tmp=tmp, xt=xt, before=before, **gate_plan(st))
    ctx["scaled"] = lambda tag, b: (xbc[:, b, 3:SEQ + 3] if tag == "xbc" else plain[tag][:, b, :],
                                    None, SM if tag == "fq" else 1.0)
    ctx["half_bias"] = lambda tag, b: gb[:, "abc".index(tag) * ND + b:"abc".index(tag) * ND + b + 1]
    ctx["t_dst"] = lambda tag, t: {"fdt": fd[:, t, :], "fv": fv[:, t, :], "z": z[:, t, :]}[tag]

    fox = Attention(
        nc, sig, mem, "a",
        q=lambda h, i: fq[(h % 2) * HD:(h % 2) * HD + HD, h // 2, i * P:(i + 1) * P],
        k=lambda h: fk[(h % 2) * HD:(h % 2) * HD + HD, h // 2, :],
        v=lambda h, kb: fv[:, kb, h * HD:(h + 1) * HD], y=ya, causal=True,
        bias=lambda h, i: (minus_cum[:, h, :], ("minus_cum", h)),
        probs=probs, pt=pt, rows=lambda h, i: ncum[:, i, h:h + 1],
        base=[("cums_kept",)],
        needs=lambda h: [("ev_act", G(("fk", h // 2))), ("ev_dve", G(("fv", NT - 1)))])
    ln = LayerNorm(nc, sig, mem, xt, gamma, beta, lambda t: d["resid"][t], banks=(4, 5),
                   source=lambda t: ("ev_dve", G(("out", 512, t))))

    extras = {}

    def extra(at_step, *e):
        extras.setdefault(at_step, []).append(e)

    extra(4 * first_u[("plain", "fq")], "setup")
    i_z = 4 * first_u[("copy_t", "z")]
    i_a = 4 * first_u[("gate", "a")]
    i_ya = 4 * first_u[("branch", "a")]
    for j in range(Attention.STEPS):
        extra(min(i_z + j, i_ya - 1), "fox", j)
    x0 = 4 * first_u[("plain", "xbc")]
    for f in range(NXBC):
        extra(x0 + 4 + 3 * f, "conv", f)
    extra(i_ya - 1, "y_split", "a")
    s = i_ya
    for f in range(5):
        extra(s + 1 + f // 2, "x_t", f)
    extra(s + 3, "cb")
    extra(s + 3, "xdt")
    for c in range(3):
        extra(s + 4 + c, "state", c)
    for h in range(HEADS):
        extra(s + 7 + h, "head", h)
    extra(s + 16, "ssd_out")
    for f in range(NW):
        extra(s + 17, "ybt", f)
    extra(4 * first_u[("branch", "b")] - 2, "y_split", "b")
    s5_at = s + 19
    extra(s5_at, "s5_b")
    n_it = S5_IT
    s5_last = 4 * first_u[("glu", "glu")] - 2
    s5_slots = S5_IT + S5_LAG
    for slot in range(s5_slots):
        at_step = s5_at + 1 + (s5_last - s5_at - 1) * slot // s5_slots
        if slot >= 4 and slot % 4 == 2 and slot < S5_IT - 4:
            extra(at_step, "s5_tables", slot // 4 + 1)
        extra(at_step, "s5", slot)
    extra(s5_last, "gelu")
    extra(s5_last, "y_split", "gy")
    extra(4 * first_u[("branch", "c")] - 1, "y_split", "c")
    i_out = 4 * first_u[("residual", "out")]
    for fb in range(ND):
        n_b = [n for n, u in enumerate(units) if u.evac[:2] == ("branch", "c")][fb // 4]
        extra(4 * n_b + fb % 4, "m_split", fb)
    for t in range(NT):
        extra(4 * n_units - 4 + t, "ln", t)
    steps = [(n, q, extras.get(4 * n + q, [])) for n in range(n_units) for q in range(4)]
    assert max(extras) < len(steps)

    def groups_done(u, q):
        return [(gid, b) for b, gid in enumerate(u.gids) if completes(u, q, b)]

    def s5_in_slot(slot):
        return slot if 0 <= slot < S5_IT else None

    def s5_it(k):
        return k // NT, k % NT

    (A_RE, A_IM, L_STEP, MAG, TH, CO, SI, K_RE, K_IM, T0, T1, T2, T3, MR, MI, T4_) = range(16)
    row = lambda i: s5p[:, i, :]

    class Chain:

        def __init__(self, eng, name):
            self.eng, self.name, self.n = eng, name, 0

        def __call__(self, ins):
            key = self.n
            self.n += 1
            ins.then_inc(*sig.inc(self.name, key))
            self.eng.wait_ge(*sig.after(self.name, key))

    V, A, Q = nc.vector, nc.scalar, nc.gpsimd
    tt, ts = V.tensor_tensor, V.tensor_scalar

    def act_extra(act, e):
        if e[0] == "setup":
            act.wait_ge(*sig.after("fd_abs"))
            A.activation(e_, e_, ACT.Exp, scale=-1.0).then_inc(*sig.inc("fd_exp"))
            act.wait_ge(*sig.after("a_log"))
            A.activation(a_neg, a_neg, ACT.Exp).then_inc(*sig.inc("a_exp"))
            act.wait_ge(*sig.after("s5in"))
            A.activation(row(L_STEP), row(L_STEP), ACT.Exp).then_inc(*sig.inc("s5_step"))
            act.wait_ge(*sig.after("s5_lam"))
            A.activation(row(MAG), row(MAG), ACT.Exp).then_inc(*sig.inc("s5_mag"))
            act.wait_ge(*sig.after("fd_one_plus"))
            A.activation(l_, w_, ACT.Ln).then_inc(*sig.inc("fd_ln"))
            act.wait_ge(*sig.after("s5_angle"))
            A.activation(row(SI), row(TH), ACT.Sin).then_inc(*sig.inc("s5_sin"))
            A.activation(row(CO), row(TH), ACT.Sin, scale=0.5).then_inc(*sig.inc("s5_sin_half"))
            act.wait_ge(*sig.after("cum_transposed"))
            A.activation(cum_f[:, :], mem.bank[5][0:16, :], ACT.Copy).then_inc(
                *sig.inc("cum_rows"))
            act.wait_ge(*sig.after("decay_arg"))
            A.activation(dte, dte, ACT.Exp)
            A.activation(dout, dout, ACT.Exp)
            A.activation(tot, tot, ACT.Exp).then_inc(*sig.inc("decays"))
        if e[0] == "fox":
            fox.on_act(act, e[1])
        if e[0] == "conv":
            f = e[1]
            act.wait_ge(*sig.after("ev_act", G(("xbc", f))))
            act.wait_ge(*sig.after("params_halved"))
            if f:
                act.wait_ge(*sig.after("conv", f - 1))
            A.activation(acc[:, :], xbc[:, f, 3:SEQ + 3], ACT.Identity, bias=cw[:, f, 4:5],
                         scale=cw[:, f, 3:4]).then_inc(*sig.inc("conv_acc", f))
            act.wait_ge(*sig.after("conv_taps", f))
            A.activation(xbc[:, f, 3:SEQ + 3], acc[:, :], ACT.Tanh).then_inc(
                *sig.inc("conv_tanh", f))
        if e[0] == "y_split":
            tag = e[1]
            if tag == "a":
                act.wait_ge(*sig.after("a_y", HEADS - 1))
                y = ya
            if tag == "b":
                act.wait_ge(*sig.after("unit_done", last_u[("branch", "a")]))
                y = yb
            if tag == "gy":
                act.wait_ge(*sig.after("unit_done", last_u[("branch", "b")]))
                act.wait_ge(*sig.after("gelu"))
                y = yc
            if tag == "c":
                act.wait_ge(*sig.after("unit_done", first_u[("glu", "glu")]))
                act.wait_ge(*sig.after("glu_used", NW - 1))
                y = yc
            A.activation(yh[:, :, :], y[:, :, :], ACT.Copy,
                         scale=0.5 if tag in ("gy", "c") else 1.0).then_inc(
                *sig.inc("y_hi", tag))
            if tag == "b":
                act.wait_ge(*sig.after("xh_free"))
            if tag == "c":
                act.wait_ge(*sig.after("s5_done"))
                for i, r_ in enumerate((gamma, beta)):
                    act.dma_start(r_[:, :], d["ln1"][i].partition_broadcast(P)).then_inc(
                        *sig.inc("ln_params", i, by=16))
                sig.seen[(sig.phase, "ln_params")] = ("ln_params", 1)
        if e[0] == "x_t":
            f = e[1]
            act.wait_ge(*sig.after("x_t", f))
            dst = bt[:, :, :] if f == 4 else xh[:, :, f * P:(f + 1) * P]
            A.activation(dst, mem.bank[4 + f % 4][:, :].rearrange("p (c k) -> p c k", k=P),
                         ACT.Copy).then_inc(*sig.inc("x_t_kept", f))
            if f == 4:
                act.wait_ge(*sig.after("y_lo", "a"))
                for h in range(2):
                    seg_load(act, h)
        if e[0] == "head":
            h = e[1]
            act.wait_ge(*sig.after("seg", h))
            A.activation(seg[:, h % 2, :], seg[:, h % 2, :], ACT.Exp).then_inc(
                *sig.inc("seg_exp", h))
            act.wait_ge(*sig.after("ssd_products", h))
            A.activation(yt[:, :, h * HD:(h + 1) * HD],
                         mem.bank[4 + h % 2][:, 0:256].rearrange("p (c k) -> p c k", k=HD),
                         ACT.Copy).then_inc(*sig.inc("ssd_diag", h))
            if h + 2 < HEADS:
                seg_load(act, h + 2)
        if e[0] == "ssd_out":
            act.wait_ge(*sig.after("ssd_products", HEADS - 1))
            act.dma_start(norm_w[:, :], d["ssd_norm_w"].partition_broadcast(P)).then_inc(
                *sig.inc("norm_w", by=16))
            act.wait_ge(*sig.after("ev_dve", G(("z", NT - 1))))
            A.activation(xdt[:, :, :], z[:, :, :], ACT.Tanh, scale=0.5).then_inc(
                *sig.inc("z_tanh"))
        if e[0] == "ybt":
            f = e[1]
            act.wait_ge(*sig.after("ybt", f))
            A.activation(yb[:, f, :], mem.bank[4 + f][:, :], ACT.Copy).then_inc(
                *sig.inc("ybf", f))
        if e[0] == "s5_b":
            act.wait_ge(*sig.after("xh_free"))
            act.wait_ge(*sig.after("ybt", NW - 1))
            for i in range(2):
                act.dma_start(ct[:, i, :, :], d["s5_c"][i].rearrange("p (t c) -> p t c", c=32)
                              ).then_inc(*sig.inc("s5_c", i, by=16))
                act.dma_start(p_s5[:, 0, i, :], d["s5_b"][i]).then_inc(
                    *sig.inc("s5_b", i, by=16))
            act.wait_ge(*sig.after("s5_b_transposed"))
            for i in range(2):
                A.activation(bbt[:, i, :, :],
                             mem.bank[4 + i][:, :].rearrange("p (a c) -> p a c", c=P),
                             ACT.Copy).then_inc(*sig.inc("s5_b_kept", i))
        if e[0] == "gelu":
            act.wait_ge(*sig.after("gelu_arg"))
            A.activation(p_s5[:, 0, :, :], p_s5[:, 0, :, :], ACT.Tanh, scale=GELU_B).then_inc(
                *sig.inc("gelu_tanh"))
        if e[0] == "m_split":
            fb = e[1]
            act.wait_ge(*sig.after("merge", ND + fb))
            if fb == 0:
                act.wait_ge(*sig.after("y_lo", "c"))
            A.activation(mh[:, fb, :], merged[:, fb, :], ACT.Copy, scale=0.5).then_inc(
                *sig.inc("m_hi", fb))
            if fb == 3:
                act.dma_start(xt[:, :, :], d["resid"].rearrange("t p c -> p t c")).then_inc(
                    *sig.inc("x_t_loaded", by=16))
        if e[0] == "ln":
            ln.split_hi(act, e[1])

    def seg_load(act, h):
        if h >= 2:
            act.wait_ge(*sig.after("ssd_products", h - 2))
        act.dma_start(seg[:, h % 2, :], d["rows"][8 + h].partition_broadcast(P)).then_inc(
            *sig.inc(f"seg_loaded_{h % 2}", h, by=16))
        sig.seen[(sig.phase, "seg_loaded", h)] = (f"seg_loaded_{h % 2}", h)

    def pool_extra(pool, e, pch):
        bh = lambda ap: ap.unsqueeze(2).broadcast_to([P, HEADS, HD])
        hv = lambda ap: ap.rearrange("p (h c) -> p h c", c=HD)
        if e[0] == "xdt":
            for f in range(NW):
                pool.wait_ge(*sig.after("x_t_kept", f))
            pool.wait_ge(*sig.after("a_pv", HEADS - 1))
            pool.wait_ge(*sig.after("decays"))
            for c in range(NT):
                ins = Q.tensor_tensor(hv(xdt[:, c, :]), hv(xh[:, c, :]), bh(fd[:, c, 8:16]),
                                      ALU.mult)
            ins.then_inc(*sig.inc("xdt"))
        if e[0] == "state":
            c = e[1]
            pool.wait_ge(*sig.after("xdt"))
            if c:
                pool.wait_ge(*sig.after("state_product", c - 1))
            Q.tensor_tensor(hv(xdd[:, :]), hv(xdt[:, c, :]), bh(dte[:, c, :]),
                            ALU.mult).then_inc(*sig.inc("xdd", c))
            if c:
                pool.wait_ge(*sig.after("state", c - 1))
                Q.tensor_tensor(hv(states[:, c, :]), hv(states[:, c - 1, :]), bh(tot[:, c, :]),
                                ALU.mult).then_inc(*sig.inc("state_decayed", c))
        if e[0] == "head":
            h = e[1]
            pool.wait_ge(*sig.after("seg_exp", h))
            pool.wait_ge(*sig.after("cb_masked", h // 4))
            Q.tensor_tensor(seg[:, h % 2, :], seg[:, h % 2, :], cbm[:, h // 4, :],
                            ALU.mult).then_inc(*sig.inc("ssd_m", h))
        if e[0] == "ssd_out":
            pool.wait_ge(*sig.after("dskip"))
            for c in range(NT):
                ins = Q.tensor_tensor(hv(xh[:, c, :]), hv(xh[:, c, :]), bh(dskip), ALU.mult)
            ins.then_inc(*sig.inc("x_skip"))
            pool.wait_ge(*sig.after("x_skip"))
            pool.wait_ge(*sig.after("ssd_head", HEADS - 1))
            Q.tensor_tensor(yt[:, :, :], yt[:, :, :], xh[:, :, :], ALU.add).then_inc(
                *sig.inc("xh_free"))
            pool.wait_ge(*sig.after("ssd_gated"))
            Q.tensor_tensor(xdt[:, :, :], yt[:, :, :], yt[:, :, :], ALU.mult).then_inc(
                *sig.inc("ssd_squares"))
            pool.wait_ge(*sig.after("ssd_ms"))
            Q.tensor_tensor(r8, r8, mem.half[:, 0:8], ALU.pow).then_inc(*sig.inc("ssd_rms"))
            pool.wait_ge(*sig.after("norm_w"))
            for c in range(NT):
                Q.tensor_tensor(xh[:, c, :].rearrange("p (g k) -> p g k", g=2),
                                norm_w[:, :].rearrange("p (g k) -> p g k", g=2),
                                yt[:, c, :].rearrange("p (g k) -> p g k", g=2),
                                ALU.mult).then_inc(*sig.inc("ssd_weighted", c))
        if e[0] == "s5_b":
            s5_tables(pool, Q, 1, pch)
        if e[0] == "s5":
            slot = e[1]
            if slot == 0:
                pool.wait_ge(*sig.after("ssd_products", HEADS - 1))
                pool.wait_ge(*sig.after("s5_q"))
                pool.wait_ge(*sig.after("ev_act", G(("u", NW - 1))))
                s5_inputs(pool, 0)
            k = s5_in_slot(slot + 1)
            if k is not None:
                s5_inputs(pool, k)
            k = s5_in_slot(slot - 1)
            if k is not None:
                pool.wait_ge(*sig.after("s5_products", k))
                if k >= 2:
                    pool.wait_ge(*sig.after("s5_back", k - 2))
                Q.tensor_tensor(w_s5[:, k % 2, 0, :], p_s5[:, k % 2, 0, :],
                                p_s5[:, k % 2, 1, :], ALU.add)
                Q.tensor_tensor(w_s5[:, k % 2, 1, :], p_s5[:, k % 2, 2, :],
                                p_s5[:, k % 2, 3, :], ALU.subtract).then_inc(
                    *sig.inc("s5_rotated", k))
            m = s5_in_slot(slot - 2)
            if m is not None:
                pool.wait_ge(*sig.after("s5_back", m))
                Q.tensor_tensor(p_s5[:, m % 2, 0, :], p_s5[:, m % 2, 0, :],
                                p_s5[:, m % 2, 1, :], ALU.subtract)
                Q.tensor_tensor(p_s5[:, m % 2, 2, :], p_s5[:, m % 2, 2, :],
                                p_s5[:, m % 2, 3, :], ALU.add).then_inc(
                    *sig.inc("s5_h", m))
        if e[0] == "gelu":
            pool.wait_ge(*sig.after("s5_y", n_it - 1))
            Q.tensor_tensor(p_s5[:, 0, :, :], yc[:, :, :], yc[:, :, :], ALU.mult).then_inc(
                *sig.inc("gelu_square"))
        if e[0] == "ln":
            ln.power(pool, e[1])
            ln.affine(pool, e[1])

    def s5_inputs(pool, k):
        a, c = s5_it(k)
        if k >= 2:
            pool.wait_ge(*sig.after("s5_bu", k - 2))
        Q.tensor_tensor(ubd[:, k % 2, :].rearrange("p (q t) -> p q t", t=P),
                        u_[:, a, c * P:(c + 1) * P].unsqueeze(1).broadcast_to([P, 4, P]),
                        qmask.unsqueeze(2).broadcast_to([P, 4, P]), ALU.mult).then_inc(
            *sig.inc("s5_u", k))

    def s5_tables(eng, on, a, ch):
        tiles = slice(4 * a, 4 * a + 4)
        qtt, qts = on.tensor_tensor, on.tensor_scalar
        by_tile = lambda ap: ap.rearrange("p (k t) -> p k t", t=P)
        cv, sv, mv = (by_tile(x[:, a % 2, :]) for x in (ctab, stab, mtab))
        er, ei, t0, t1, t2 = (row(i)[:, tiles] for i in (T0, T1, T2, T3, T4_))
        if a >= 2:
            eng.wait_ge(*sig.after("s5_back", NT * (a - 1) - 1))
        else:
            eng.wait_ge(*sig.after("ssd_weighted", NT - 1))
            eng.wait_ge(*sig.after("s5_bb_rows"))
        on.memset(cv[:, :, 0:1], 1.0)
        on.memset(sv[:, :, 0:1], 0.0)
        ch(qtt(mv, row(MAG)[:, tiles].unsqueeze(2).broadcast_to([P, 4, P]),
               ones4.unsqueeze(2).broadcast_to([P, 4, P]), ALU.mult))
        on.memset(mv[:, :, 0:1], 0.0)
        on.tensor_copy(er, row(CO)[:, tiles])
        ch(on.tensor_copy(ei, row(SI)[:, tiles]))
        n = 1
        work = (ubd[:, 0, :], ubd[:, 1, :]) if a == 1 else (mem.tbias[0], mem.tbias[1])
        pa = [x[:, i:i + 256] for x in work for i in (0, 256)]
        while n < P:
            bc = lambda ap: ap.unsqueeze(2).broadcast_to([P, 4, n])
            q_ = [x[:, 0:4 * n].rearrange("p (k t) -> p k t", t=n) for x in pa]
            qtt(q_[0], cv[:, :, 0:n], bc(er), ALU.mult)
            qtt(q_[1], sv[:, :, 0:n], bc(ei), ALU.mult)
            qtt(q_[2], cv[:, :, 0:n], bc(ei), ALU.mult)
            qtt(q_[3], sv[:, :, 0:n], bc(er), ALU.mult)
            qtt(t0, er, er, ALU.mult)
            qtt(t1, ei, ei, ALU.mult)
            ch(qtt(t2, er, ei, ALU.mult))
            qtt(cv[:, :, n:2 * n], q_[0], q_[1], ALU.subtract)
            qtt(sv[:, :, n:2 * n], q_[2], q_[3], ALU.add)
            qtt(er, t0, t1, ALU.subtract)
            ch(qts(ei, t2, 2.0, None, ALU.mult))
            n *= 2
        qtt(row(MR)[:, tiles], er, row(MAG)[:, tiles], ALU.mult)
        qtt(row(MI)[:, tiles], ei, row(MAG)[:, tiles], ALU.mult).then_inc(*sig.inc("s5_tables", a))

    def dve_extra(dve, e, ch):
        if e[0] == "setup":
            dve.wait_ge(*sig.after("bias16"))
            dve.wait_ge(*sig.after("ev_dve", G(("fdt", NT - 1))))
            ch(tt(fd, fd, bias16.unsqueeze(1).broadcast_to([P, NT, 16]), ALU.add))
            ch(ts(fd[:, :, 0:8], fd[:, :, 0:8], -1.0, None, ALU.mult))
            ch(ts(e_, fd, -1.0, None, ALU.mult))
            tt(e_, e_, fd, ALU.max).then_inc(*sig.inc("fd_abs"))
            dve.wait_ge(*sig.after("fd_exp"))
            ts(w_, e_, 1.0, None, ALU.add).then_inc(*sig.inc("fd_one_plus"))
            dve.wait_ge(*sig.after("s5_step"))
            ch(ts(row(A_RE), row(A_RE), -1e-4, None, ALU.min))
            ch(tt(row(MAG), row(A_RE), row(L_STEP), ALU.mult))
            tt(row(TH), row(A_IM), row(L_STEP), ALU.mult).then_inc(*sig.inc("s5_lam"))
            dve.wait_ge(*sig.after("s5_lam"))
            ch(ts(row(T0), row(TH), 1.0 / (2 * np.pi), None, ALU.mult))
            ch(ts(row(T0), row(T0), ROUND, None, ALU.add))
            ch(ts(row(T0), row(T0), ROUND, None, ALU.subtract))
            for part in TWO_PI_PARTS:
                ch(V.scalar_tensor_tensor(row(TH), row(T0), -part, row(TH), ALU.mult, ALU.add))
            ts(row(TH), row(TH), PI_BELOW, -PI_BELOW, ALU.min, ALU.max).then_inc(
                *sig.inc("s5_angle"))
            dve.wait_ge(*sig.after("fd_ln"))
            ch(ts(w_, w_, 1.0, None, ALU.subtract))
            ch(ts(cums, w_, 0.0, None, ALU.is_equal))
            ch(tt(w_, w_, cums, ALU.add))
            ch(V.reciprocal(w_, w_))
            ch(tt(l_, l_, w_, ALU.mult))
            ch(tt(l_, l_, cums, ALU.add))
            ch(tt(l_, l_, e_, ALU.mult))
            ch(ts(fd, fd, 0.0, None, ALU.max))
            ch(tt(fd, fd, l_, ALU.add))
            ch(ts(lf, fd[:, :, 0:8], -1.0, None, ALU.mult))
            ch(V.memset(pre[:, 0, :], 0.0))
            for c in range(1, NT):
                ch(tt(pre[:, c, :], pre[:, c - 1, :], lf[:, c - 1, :], ALU.add))
            dve.wait_ge(*sig.after("a_exp"))
            ch(ts(a_neg, a_neg, -1.0, None, ALU.mult))
            tt(adt, fd[:, :, 8:16], a_neg.unsqueeze(1).broadcast_to([P, NT, 8]),
               ALU.mult).then_inc(*sig.inc("sums_ready"))
            dve.wait_ge(*sig.after("cum_sums"))
            b4 = mem.bank[4]
            v = lambda i: b4[:, 32 * i:32 * i + 32].rearrange("p (t h) -> p t h", h=8)
            V.tensor_copy(ncum, v(0))
            ts(cums[:, :, 0:8], v(0), -1.0, None, ALU.mult)
            V.tensor_copy(dout, v(1))
            V.tensor_copy(tot, v(2))
            V.tensor_copy(cums[:, :, 8:16], v(1)).then_inc(*sig.inc("cums"))
            dve.wait_ge(*sig.after("cums"))
            ts(nacs, cums[:, :, 8:16], -1.0, None, ALU.mult)
            tt(dte, tot, cums[:, :, 8:16], ALU.subtract).then_inc(*sig.inc("decay_arg"))
            sig.seen[(sig.phase, "cums_kept")] = ("decay_arg",)
            dve.wait_ge(*sig.after("s5_sin_half"))
            ch(tt(row(CO), row(CO), row(CO), ALU.mult))
            ch(ts(row(CO), row(CO), -2.0, 1.0, ALU.mult, ALU.add))
            dve.wait_ge(*sig.after("s5_mag"))
            ch(tt(row(T0), row(MAG), row(CO), ALU.mult))
            ch(ts(row(T0), row(T0), -1.0, None, ALU.add))
            ch(tt(row(T1), row(MAG), row(SI), ALU.mult))
            ch(tt(row(T2), row(A_RE), row(A_RE), ALU.mult))
            ch(tt(row(T3), row(A_IM), row(A_IM), ALU.mult))
            ch(tt(row(T2), row(T2), row(T3), ALU.add))
            ch(V.reciprocal(row(T2), row(T2)))
            ch(tt(row(K_RE), row(T0), row(A_RE), ALU.mult))
            ch(tt(row(T3), row(T1), row(A_IM), ALU.mult))
            ch(tt(row(K_RE), row(K_RE), row(T3), ALU.add))
            ch(tt(row(K_RE), row(K_RE), row(T2), ALU.mult))
            ch(tt(row(K_IM), row(T1), row(A_RE), ALU.mult))
            ch(tt(row(T3), row(T0), row(A_IM), ALU.mult))
            ch(tt(row(K_IM), row(K_IM), row(T3), ALU.subtract))
            ch(tt(row(K_IM), row(K_IM), row(T2), ALU.mult))
            V.memset(ones4, 1.0).then_inc(*sig.inc("s5_bb_rows"))
        if e[0] == "fox":
            fox.on_dve(dve, e[1])
        if e[0] == "conv":
            f = e[1]
            if f == 0:
                dve.wait_ge(*sig.after("conv_pad"))
            dve.wait_ge(*sig.after("conv_acc", f))
            for k in range(3):
                V.scalar_tensor_tensor(acc[:, :], xbc[:, f, k:k + SEQ], cw[:, f, k:k + 1],
                                       acc[:, :], ALU.mult, ALU.add).then_inc(
                    *sig.inc("conv_tap", f, k))
                dve.wait_ge(*sig.after("conv_tap", f, k))
            sig.seen[(sig.phase, "conv_taps", f)] = ("conv_tap", f, 2)
            dve.wait_ge(*sig.after("conv_tanh", f))
            x = xbc[:, f, 3:SEQ + 3]
            V.scalar_tensor_tensor(x, x, 1.0, acc[:, :], ALU.add, ALU.mult).then_inc(
                *sig.inc("conv", f))
        if e[0] == "y_split":
            tag = e[1]
            y = {"a": ya, "b": yb, "gy": yc, "c": yc}[tag]
            dve.wait_ge(*sig.after("y_hi", tag))
            if tag in ("gy", "c"):
                V.scalar_tensor_tensor(yl[:, :, :], y[:, :, :], 0.5, yh[:, :, :].bitcast(F32),
                                       ALU.mult, ALU.subtract).then_inc(*sig.inc("y_lo", tag))
            else:
                tt(yl[:, :, :], y[:, :, :], yh[:, :, :].bitcast(F32), ALU.subtract).then_inc(
                    *sig.inc("y_lo", tag))
        if e[0] == "cb":
            for gg in range(2):
                dve.wait_ge(*sig.after("cb", gg))
                tt(cbm[:, gg, :].rearrange("p (c l) -> p c l", l=P),
                   mem.bank[6 + gg][:, :].rearrange("p (c l) -> p c l", l=P),
                   tri[:, :].unsqueeze(1).broadcast_to([P, NT, P]), ALU.mult).then_inc(
                    *sig.inc("cb_masked", gg))
        if e[0] == "state":
            c = e[1]
            dve.wait_ge(*sig.after("state_product", c))
            if c:
                dve.wait_ge(*sig.after("state_decayed", c))
                tt(states[:, c, :], states[:, c, :], mem.bank[4][:, :], ALU.add).then_inc(
                    *sig.inc("state", c))
            else:
                V.tensor_copy(states[:, 0, :], mem.bank[4][:, :]).then_inc(
                    *sig.inc("state", c))
        if e[0] == "head":
            h = e[1]
            dve.wait_ge(*sig.after("seg_loaded", h))
            for c in range(NT):
                x = seg[:, h % 2, c * P:(c + 1) * P]
                ins = ts(x, x, nacs[:, c, h:h + 1], 0.0, ALU.add, ALU.min)
            ins.then_inc(*sig.inc("seg", h))
            dve.wait_ge(*sig.after("ssd_diag", h))
            for c in range(1, NT):
                y = yt[:, c, h * HD:(h + 1) * HD]
                ins = V.scalar_tensor_tensor(
                    y, mem.bank[4 + h % 2][:, 256 + (c - 1) * HD:256 + c * HD],
                    dout[:, c, h:h + 1], y, ALU.mult, ALU.add)
            ins.then_inc(*sig.inc("ssd_head", h))
        if e[0] == "ssd_out":
            dve.wait_ge(*sig.after("z_tanh"))
            V.scalar_tensor_tensor(z[:, :, :], xdt[:, :, :], 1.0, z[:, :, :], ALU.add,
                                   ALU.mult).then_inc(*sig.inc("ssd_silu"))
            dve.wait_ge(*sig.after("ssd_silu"))
            dve.wait_ge(*sig.after("xh_free"))
            V.scalar_tensor_tensor(yt[:, :, :], yt[:, :, :], 0.5, z[:, :, :], ALU.mult,
                                   ALU.mult).then_inc(*sig.inc("ssd_gated"))
            dve.wait_ge(*sig.after("ssd_squares"))
            ch(V.tensor_reduce(r8, xdt[:, :, :].rearrange("p t (g k) -> p (t g) k", g=2), AX.X,
                               ALU.add))
            ts(r8, r8, 1.0 / 256, RMS_EPS_2, ALU.mult, ALU.add).then_inc(*sig.inc("ssd_ms"))
            dve.wait_ge(*sig.after("ssd_rms"))
            for c in range(NT):
                dve.wait_ge(*sig.after("ssd_weighted", c))
                for gg in range(2):
                    x = slice(gg * 256, gg * 256 + 256)
                    ins = ts(yt[:, c, x], xh[:, c, x], r8[:, 2 * c + gg:2 * c + gg + 1], None,
                             ALU.mult)
                ins.then_inc(*sig.inc("ssd_normed", c))
        if e[0] == "s5_tables":
            s5_tables(dve, V, e[1], ch)
        if e[0] == "s5_b":
            s5_tables(dve, V, 0, ch)
            for i in range(2):
                dve.wait_ge(*sig.after("s5_b", i))
                dve.wait_ge(*sig.after("s5_c", i))
            b3 = lambda i: p_s5[:, 0, i, :].rearrange("p (t c) -> p t c", c=32)
            o3 = lambda i: p_s5[:, 1, i, :].rearrange("p (t c) -> p t c", c=32)
            kb = lambda r_: row(r_).unsqueeze(2).broadcast_to([P, S5_TILES, 32])
            ch(ts(ct[:, 1, :, :], ct[:, 1, :, :], -1.0, None, ALU.mult))
            ch(tt(o3(0), b3(0), kb(K_RE), ALU.mult))
            ch(tt(o3(2), b3(1), kb(K_IM), ALU.mult))
            ch(tt(o3(0), o3(0), o3(2), ALU.subtract))
            ch(tt(o3(1), b3(1), kb(K_RE), ALU.mult))
            ch(tt(o3(3), b3(0), kb(K_IM), ALU.mult))
            tt(o3(1), o3(1), o3(3), ALU.add).then_inc(*sig.inc("s5_bb"))
        if e[0] == "s5":
            s5_dve(dve, e[1], ch)
        if e[0] == "gelu":
            x = p_s5[:, 0, :, :]
            dve.wait_ge(*sig.after("gelu_square"))
            ch(ts(x, x, GELU_A, 1.0, ALU.mult, ALU.add))
            tt(x, x, yc[:, :, :], ALU.mult).then_inc(*sig.inc("gelu_arg"))
            dve.wait_ge(*sig.after("gelu_tanh"))
            V.scalar_tensor_tensor(yc[:, :, :], x, 1.0, yc[:, :, :], ALU.add,
                                   ALU.mult).then_inc(*sig.inc("gelu"))
        if e[0] == "m_split":
            fb = e[1]
            dve.wait_ge(*sig.after("m_hi", fb))
            V.scalar_tensor_tensor(ml[:, fb, :], merged[:, fb, :], 0.5,
                                   mh[:, fb, :].bitcast(F32), ALU.mult,
                                   ALU.subtract).then_inc(*sig.inc("m_lo", fb))
        if e[0] == "ln":
            ln.statistics(dve, e[1])
            ln.normalise(dve, e[1])
            ln.split_lo(dve, e[1])

    def s5_dve(dve, slot, ch):
        k = s5_in_slot(slot - 1)
        if k is not None:
            a, c = s5_it(k)
            if c == 0:
                dve.wait_ge(*sig.after("s5_tables", a))
            dve.wait_ge(*sig.after("s5_bu", k))
            if k >= 2:
                dve.wait_ge(*sig.after("s5_out", k - 2))
            re, im = mem.bank[4 + 2 * (k % 2)][:, :], mem.bank[5 + 2 * (k % 2)][:, :]
            pk, cq, sq = p_s5[:, k % 2, :, :], ctab[:, a % 2, :], stab[:, a % 2, :]
            tt(pk[:, 0, :], re, cq, ALU.mult)
            tt(pk[:, 1, :], im, sq, ALU.mult)
            tt(pk[:, 2, :], im, cq, ALU.mult)
            tt(pk[:, 3, :], re, sq, ALU.mult).then_inc(*sig.inc("s5_products", k))
        m = s5_in_slot(slot - 2)
        if m is not None:
            a, c = s5_it(m)
            dve.wait_ge(*sig.after("s5_rotated", m))
            w = w_s5[:, m % 2, :, :]
            a4 = slice(4 * a, 4 * a + 4)
            first = [w[:, i, :].rearrange("p (k t) -> p k t", t=P)[:, :, 0] for i in range(2)]
            last = [w[:, i, :].rearrange("p (k t) -> p k t", t=P)[:, :, P - 1] for i in range(2)]
            if c:
                for i in range(2):
                    tt(first[i], first[i], carry[:, i, 0, :], ALU.add).then_inc(
                        *sig.inc("s5_entered", m, i))
                dve.wait_ge(*sig.after("s5_entered", m, 1))
            for i in range(2):
                V.tensor_tensor_scan(w[:, i, :], mtab[:, a % 2, :], w[:, i, :], 0.0, ALU.mult,
                                     ALU.add).then_inc(*sig.inc("s5_scan", m, i))
            dve.wait_ge(*sig.after("s5_scan", m, 1))
            pm = p_s5[:, m % 2, :, :]
            if c < NT - 1:
                t_ = [t4[:, 4 * i:4 * i + 4] for i in range(4)]
                tt(t_[0], last[0], row(MR)[:, a4], ALU.mult)
                tt(t_[1], last[1], row(MI)[:, a4], ALU.mult)
                tt(t_[2], last[0], row(MI)[:, a4], ALU.mult)
                tt(t_[3], last[1], row(MR)[:, a4], ALU.mult).then_inc(*sig.inc("s5_end", m))
            tt(pm[:, 0, :], w[:, 0, :], ctab[:, a % 2, :], ALU.mult)
            if c < NT - 1:
                dve.wait_ge(*sig.after("s5_end", m))
                tt(carry[:, 0, 0, :], t_[0], t_[1], ALU.subtract)
                tt(carry[:, 1, 0, :], t_[2], t_[3], ALU.add).then_inc(*sig.inc("s5_carry", m))
            tt(pm[:, 1, :], w[:, 1, :], stab[:, a % 2, :], ALU.mult)
            tt(pm[:, 2, :], w[:, 0, :], stab[:, a % 2, :], ALU.mult)
            tt(pm[:, 3, :], w[:, 1, :], ctab[:, a % 2, :], ALU.mult).then_inc(
                *sig.inc("s5_back", m))
            if c < NT - 1:
                dve.wait_ge(*sig.after("s5_carry", m))
        m = s5_in_slot(slot - S5_LAG)
        if m is not None:
            a, c = s5_it(m)
            dve.wait_ge(*sig.after("s5_out", m))
            if m == 0:
                dve.wait_ge(*sig.after("y_lo", "b"))
            cs = slice(c * P, (c + 1) * P)
            V.scalar_tensor_tensor(yc[:, a, cs], u_[:, a, cs], s5d[:, a:a + 1],
                                   mem.bank[3][:, 0:P], ALU.mult, ALU.add).then_inc(
                *sig.inc("s5_y", m))

    def pe_extra(pe, e):
        mm, tr = nc.tensor.matmul, nc.tensor.transpose
        if e[0] == "setup":
            pe.wait_ge(*sig.after("sums_ready"))
            pe.wait_ge(*sig.after("tri"))
            pe.wait_ge(*sig.after("ones"))
            b4 = mem.bank[4]
            flat = lambda ap: ap.rearrange("p t h -> p (t h)")
            mm(b4[:, 0:32], tri[:, :], flat(lf), start=True, stop=False)
            mm(b4[:, 0:32], ones[:, :], flat(pre), start=False, stop=True)
            mm(b4[:, 32:64], tri[:, :], flat(adt), start=True, stop=True)
            mm(b4[:, 64:96], ones[:, :], flat(adt), start=True, stop=True).then_inc(
                *sig.inc("cum_sums"))
            pe.wait_ge(*sig.after("cums"))
            for c in range(NT):
                last = tr(mem.bank[5][0:16, c * P:(c + 1) * P], cums[:, c, :], mem.ident[:, :])
            last.then_inc(*sig.inc("cum_transposed"))
        if e[0] == "fox":
            if e[1] == 0:
                pe.wait_ge(*sig.after("cum_rows"))
            fox.on_pe(pe, e[1])
        if e[0] == "x_t":
            f = e[1]
            pe.wait_ge(*sig.after("conv", f))
            if f == 0:
                pe.wait_ge(*sig.after("a_y", HEADS - 1))
            if f == 4:
                pe.wait_ge(*sig.after("x_t_kept", 0))
            for c in range(NT):
                last = tr(mem.bank[4 + f % 4][:, c * P:(c + 1) * P],
                          xbc[:, f, 3 + c * P:3 + (c + 1) * P], mem.ident[:, :])
            last.then_inc(*sig.inc("x_t", f))
        if e[0] == "cb":
            pe.wait_ge(*sig.after("conv", 5))
            pe.wait_ge(*sig.after("x_t_kept", 3))
            for gg in range(2):
                r_ = slice(gg * HD, gg * HD + HD)
                for c in range(NT):
                    x = slice(3 + c * P, 3 + (c + 1) * P)
                    last = mm(mem.bank[6 + gg][:, c * P:(c + 1) * P], xbc[r_, 4, x],
                              xbc[r_, 5, x], start=True, stop=True)
                last.then_inc(*sig.inc("cb", gg))
        if e[0] == "state":
            c = e[1]
            pe.wait_ge(*sig.after("xdd", c))
            pe.wait_ge(*sig.after("x_t_kept", 4))
            if c:
                pe.wait_ge(*sig.after("state", c - 1))
            mm(mem.bank[4][:, :], bt[:, c, :], xdd[:, :], start=True, stop=True).then_inc(
                *sig.inc("state_product", c))
        if e[0] == "head":
            h = e[1]
            pe.wait_ge(*sig.after("ssd_m", h))
            if h == 0:
                pe.wait_ge(*sig.after("state", 2))
            if h >= 2:
                pe.wait_ge(*sig.after("ssd_head", h - 2))
            bank, gg = mem.bank[4 + h % 2], h // 4
            r_ = slice(gg * HD, gg * HD + HD)
            hs = slice(h * HD, (h + 1) * HD)
            for c in range(NT):
                mm(bank[:, c * HD:(c + 1) * HD], seg[:, h % 2, c * P:(c + 1) * P],
                   xdt[:, c, hs], start=True, stop=True)
            for c in range(1, NT):
                last = mm(bank[:, 256 + (c - 1) * HD:256 + c * HD],
                          xbc[r_, 5, 3 + c * P:3 + (c + 1) * P], states[r_, c - 1, hs],
                          start=True, stop=True)
            last.then_inc(*sig.inc("ssd_products", h))
        if e[0] == "ybt":
            f = e[1]
            pe.wait_ge(*sig.after("ssd_normed", NT - 1))
            if f == 0:
                pe.wait_ge(*sig.after("ssd_head", HEADS - 1))
            for t in range(NT):
                last = tr(mem.bank[4 + f][:, t * P:(t + 1) * P], yt[:, t, f * P:(f + 1) * P],
                          mem.ident[:, :])
            last.then_inc(*sig.inc("ybt", f))
        if e[0] == "s5_b":
            pe.wait_ge(*sig.after("s5_bb"))
            pe.wait_ge(*sig.after("ybf", NW - 1))
            for i in range(2):
                for a in range(4):
                    last = tr(mem.bank[4 + i][:, a * P:(a + 1) * P],
                              p_s5[:, 1, i, a * P:(a + 1) * P], mem.ident[:, :])
            last.then_inc(*sig.inc("s5_b_transposed"))
        if e[0] == "s5":
            m = s5_in_slot(e[1] - S5_LAG)
            if m is not None:
                a, c = s5_it(m)
                pe.wait_ge(*sig.after("s5_h", m))
                if m == 0:
                    st.wait_read(pe, last_in_3)
                else:
                    pe.wait_ge(*sig.after("s5_y", m - 1))
                for q_ in range(4):
                    o = mem.bank[3][32 * q_:32 * q_ + 32, 0:P]
                    mm(o, ct[:, 0, 4 * a + q_, :], p_s5[:, m % 2, 0, q_ * P:(q_ + 1) * P],
                       start=True, stop=False, tile_position=(0, 32 * q_))
                    last = mm(o, ct[:, 1, 4 * a + q_, :],
                              p_s5[:, m % 2, 2, q_ * P:(q_ + 1) * P], start=False, stop=True,
                              tile_position=(0, 32 * q_))
                last.then_inc(*sig.inc("s5_out", m))
                if m == n_it - 1:
                    sig.seen[(sig.phase, "s5_done")] = ("s5_out", m)
            k = s5_in_slot(e[1])
            if k is not None:
                a, c = s5_it(k)
                if k == 0:
                    pe.wait_ge(*sig.after("s5_b_kept", 1))
                if k >= 2:
                    pe.wait_ge(*sig.after("s5_products", k - 2))
                pe.wait_ge(*sig.after("s5_u", k))
                for i in range(2):
                    last = mm(mem.bank[4 + 2 * (k % 2) + i][:, :], bbt[:, i, a, :],
                              ubd[:, k % 2, :], start=True, stop=True)
                last.then_inc(*sig.inc("s5_bu", k))
        if e[0] == "ln":
            ln.transpose(pe, e[1])




    with nc.Block() as block:
        @block.sync
        def _(sp):
            for n in range(3):
                st.load(sp, n)
            sp.wait_ge(*sig.after("cum_rows"))
            sp.dma_start(d["rows"], cum_f[:, :]).then_inc(*sig.inc("rows_stored", by=16))
            for n in range(3, 6):
                st.load(sp, n)
            sp.wait_ge(*sig.after("rows_stored"))
            for h in range(HEADS):
                sp.dma_start(minus_cum[:, h, :], d["rows"][h].partition_broadcast(P)).then_inc(
                    *sig.inc(f"minus_cum_{h}", by=16))
                sig.seen[(sig.phase, "minus_cum", h)] = (f"minus_cum_{h}",)
            for n in range(6, n_units):
                st.load(sp, n)
            for t in range(NT):
                ln.store(sp, t)
            sp.wait_ge(*sig.after("ln_stored", NT - 1))

        @block.scalar
        def _(act):
            for name, dst in (("bias16", bias16), ("dskip", dskip), ("a_log", a_neg)):
                act.dma_start(dst, d[name].partition_broadcast(P)).then_inc(*sig.inc(name, by=16))
            for name, dst in (("cw", mem.small2[:, 16:46]), ("s5d", s5d), ("glub", glub),
                              ("gb", gb), ("s5_q", qmask), ("s5in", s5p[:, 0:3, :]), ("tri", tri[:, :]),
                              ("ones", ones[:, :])):
                act.dma_start(dst, d[name]).then_inc(*sig.inc(name, by=16))
            st.hi(act, 0)
            for n, q, ex in steps:
                u = units[n]
                if q == 0:
                    st.hi(act, n + 1)
                if n == 0 and q == 3:
                    act.wait_ge(*sig.after("params_halved"))
                for gid, b in groups_done(u, q):
                    if u.evac[0] == "plain":
                        dst, _, scale = ctx["scaled"](u.evac[1], u.evac[2] + b)
                        act.wait_ge(*sig.after("group", gid))
                        A.activation(dst, st.bank(gid)[:, :], ACT.Copy, scale=scale).then_inc(
                            *sig.inc("ev_act", gid))
                    elif u.evac[0] == "glu":
                        act.wait_ge(*sig.after("group", gid))
                        A.activation(p_s5[:, 1, b, :], st.bank(gid)[:, :], ACT.Tanh,
                                     bias=glub[:, b:b + 1], scale=0.5).then_inc(
                            *sig.inc("ev_act", gid))
                    else:
                        emit_common_evac(nc, sig, mem, st, u, b, gid, "act", act, ctx)
                for e in ex:
                    act_extra(act, e)

        @block.gpsimd
        def _(pool):
            pch = Chain(pool, "pool_chain")
            Q.memset(xbc[:, :, 0:3], 0.0).then_inc(*sig.inc("conv_pad"))
            for n, q, ex in steps:
                u = units[n]
                for gid, b in groups_done(u, q):
                    emit_common_evac(nc, sig, mem, st, u, b, gid, "pool", pool, ctx)
                if 4 * n + q == i_out:
                    pool.wait_ge(*sig.after("x_t_loaded"))
                    Q.tensor_scalar(xt[:, :, :], xt[:, :, :], ALPHA_2, None, ALU.mult).then_inc(
                        *sig.inc("residual"))
                for e in ex:
                    pool_extra(pool, e, pch)

        @block.vector
        def _(dve):
            ch = Chain(dve, "dve_chain")
            st.lo(dve, 0)
            for name in ("cw", "gb", "glub"):
                dve.wait_ge(*sig.after(name))
            ts(cw, cw, 0.5, None, ALU.mult)
            ts(gb, gb, 0.5, None, ALU.mult)
            ts(glub, glub, 0.5, None, ALU.mult).then_inc(*sig.inc("params_halved"))
            for n, q, ex in steps:
                u = units[n]
                if q == 0:
                    st.lo(dve, n + 1)
                for gid, b in groups_done(u, q):
                    if u.evac[0] == "glu":
                        dve.wait_ge(*sig.after("ev_act", gid))
                        V.scalar_tensor_tensor(p_s5[:, 1, b, :], p_s5[:, 1, b, :], 1.0,
                                               yc[:, b, :], ALU.add, ALU.mult).then_inc(
                            *sig.inc("glu_product", b))
                        dve.wait_ge(*sig.after("glu_product", b))
                        ts(yc[:, b, :], p_s5[:, 1, b, :], 0.5, None, ALU.mult).then_inc(
                            *sig.inc("glu_used", b))
                    else:
                        emit_common_evac(nc, sig, mem, st, u, b, gid, "dve", dve, ctx)
                for e in ex:
                    dve_extra(dve, e, ch)

        @block.tensor
        def _(pe):
            for n, q, ex in steps:
                st.multiply(pe, n, q)
                for e in ex:
                    pe_extra(pe, e)

def ffn_units():
    units, what = [], []
    for i in range(NF2):
        units.append(Unit("F", "x", ND, 2 * P, ("conv_ffn", "up", 2 * i)))
        what.append(("up", 0, ND, 2 * i * P, 2 * P))
    for c in (0, 512):
        for k0 in range(0, NF2, 4):
            nk = min(4, NF2 - k0)
            units.append(Unit("T", "h", nk, 512, ("residual", "down", c), k0=k0, of=NF2))
            what.append(("down", k0, nk, c, 512))
    return units, what


def ffn_phase(nc, sig, mem, d):
    units, _ = ffn_units()
    n_units = len(units)
    at = lambda name, *a: mem.at("ff_" + name, *a)
    hh = at("h_hi", 0, [P, NF2, SEQ], F32R)
    hl = at("h_lo", 44, [P, NF2, SEQ], F32R)
    val = at("val", 88, [P, 2, SEQ])
    gat = at("gate", 92, [P, 2, SEQ])
    th = at("tanh", 96, [P, 2, SEQ])
    gamma = at("gamma", 100, [P, D])
    beta = at("beta", 104, [P, D])
    xt = nc.alloc_sbuf_tensor_at("ff_x_t", [P, NT, D], F32, offset=int(mem.x_base))
    cw = mem.small2[:, 0:4 * 2 * NF2].rearrange("p (f k) -> p f k", k=4)
    st = Stream(nc, sig, mem, units, lambda n: d["w3"][n],
                {"x": (mem.xh, mem.xl), "h": (hh, hl)},
                lambda u: [("h_lo", u.k0 + u.nk - 1)] if u.src == "h" else [])
    gid_of = {(u.evac[1], u.evac[2], b): gid for gid, (u, b) in st.by_gid.items()}
    ctx = dict(xt=xt, before=lambda tag: [], **gate_plan(st))
    ln = LayerNorm(nc, sig, mem, xt, gamma, beta, lambda t: d["out"][t], banks=(4, 5),
                   source=lambda t: ("ev_dve", gid_of[("down", 512, t)]))
    V, A, Q = nc.vector, nc.scalar, nc.gpsimd
    steps = [(n, q) for n in range(n_units) for q in range(4)]

    def groups_done(u, q):
        return [(gid, b) for b, gid in enumerate(u.gids) if completes(u, q, b)]

    def high(act, i):
        act.wait_ge(*sig.after("h", i))
        A.activation(hh[:, i, :], val[:, i % 2, :], ACT.Copy).then_inc(*sig.inc("h_hi", i))

    def low(dve, i):
        dve.wait_ge(*sig.after("h_hi", i))
        V.tensor_tensor(hl[:, i, :], val[:, i % 2, :], hh[:, i, :].bitcast(F32),
                        ALU.subtract).then_inc(*sig.inc("h_lo", i))

    with nc.Block() as block:
        @block.sync
        def _(sp):
            for n in range(n_units):
                st.load(sp, n)
                if n == NF2 + RAW:
                    sp.wait_ge(*sig.after("unit_done", NF2 - 1))
                    sp.dma_start(xt[:, :, :], d["resid"].rearrange("t p c -> p t c")).then_inc(
                        *sig.inc("x_t_loaded", by=16))
            for t in range(NT):
                ln.store(sp, t)
            sp.wait_ge(*sig.after("ln_stored", NT - 1))

        @block.gpsimd
        def _(pool):
            for i in range(NF2):
                pool.wait_ge(*sig.after("silu", i))
                Q.tensor_tensor(val[:, i % 2, :], val[:, i % 2, :], gat[:, i % 2, :],
                                ALU.mult).then_inc(*sig.inc("h", i))
            pool.wait_ge(*sig.after("x_t_loaded"))
            Q.tensor_scalar(xt[:, :, :], xt[:, :, :], ALPHA_2, None, ALU.mult).then_inc(
                *sig.inc("residual"))
            for t in range(NT):
                ln.power(pool, t)
                ln.affine(pool, t)

        @block.scalar
        def _(act):
            act.dma_start(mem.small2[:, 0:8 * NF2], d["ffn_cw"]).then_inc(*sig.inc("cw", by=16))
            for i, r_ in enumerate((gamma, beta)):
                act.dma_start(r_[:, :], d["ln2"][i].partition_broadcast(P)).then_inc(
                    *sig.inc("ln_params", i, by=16))
            sig.seen[(sig.phase, "ln_params")] = ("ln_params", 1)
            st.hi(act, 0)
            act.wait_ge(*sig.after("cw_ready"))
            for n, q in steps:
                u = units[n]
                if q == 0:
                    st.hi(act, n + 1)
                for gid, b in groups_done(u, q):
                    if u.evac[0] != "conv_ffn":
                        continue
                    f = u.evac[2] + b
                    dst = (val, gat)[b][:, n % 2, :]
                    act.wait_ge(*sig.after("group", gid))
                    if n >= 2:
                        act.wait_ge(*sig.after("h_lo", n - 2))
                    A.activation(dst, st.bank(gid)[:, :], ACT.Identity, bias=cw[:, f, 3:4],
                                 scale=cw[:, f, 2:3]).then_inc(*sig.inc("tap2", gid))
                if n < NF2 and q == 1 and n:
                    high(act, n - 1)
                if n < NF2 and q == 3:
                    act.wait_ge(*sig.after("ev_dve", u.gids[1]))
                    A.activation(th[:, n % 2, :], gat[:, n % 2, :], ACT.Tanh).then_inc(
                        *sig.inc("tanh", n))
                if n == NF2 and q == 0:
                    high(act, NF2 - 1)

        @block.vector
        def _(dve):
            dve.wait_ge(*sig.after("cw"))
            gcw = mem.small2[:, 0:8 * NF2].rearrange("p (f two k) -> p f two k", two=2, k=4)
            V.tensor_scalar(gcw[:, :, 1, :], gcw[:, :, 1, :], 0.5, None, ALU.mult).then_inc(
                *sig.inc("cw_ready"))
            dve.wait_ge(*sig.after("cw_ready"))
            st.lo(dve, 0)
            for n, q in steps:
                u = units[n]
                if q == 0:
                    st.lo(dve, n + 1)
                for gid, b in groups_done(u, q):
                    if u.evac[0] == "conv_ffn":
                        f = u.evac[2] + b
                        dst = (val, gat)[b][:, n % 2, :]
                        ps = st.bank(gid)
                        dve.wait_ge(*sig.after("tap2", gid))
                        V.scalar_tensor_tensor(dst[:, 1:SEQ], ps[:, 0:SEQ - 1], cw[:, f, 1:2],
                                               dst[:, 1:SEQ], ALU.mult, ALU.add).then_inc(
                            *sig.inc("tap1", gid))
                        dve.wait_ge(*sig.after("tap1", gid))
                        V.scalar_tensor_tensor(dst[:, 2:SEQ], ps[:, 0:SEQ - 2], cw[:, f, 0:1],
                                               dst[:, 2:SEQ], ALU.mult, ALU.add).then_inc(
                            *sig.inc("ev_dve", gid))
                    else:
                        emit_common_evac(nc, sig, mem, st, u, b, gid, "dve", dve, ctx)
                if n < NF2 and q == 1 and n:
                    low(dve, n - 1)
                if n < NF2 and q == 3:
                    dve.wait_ge(*sig.after("tanh", n))
                    x = gat[:, n % 2, :]
                    V.scalar_tensor_tensor(x, th[:, n % 2, :], 1.0, x, ALU.add,
                                           ALU.mult).then_inc(*sig.inc("silu", n))
                if n == NF2 and q == 0:
                    low(dve, NF2 - 1)
                if n == n_units - 1:
                    ln.statistics(dve, q)
                    ln.normalise(dve, q)

        @block.tensor
        def _(pe):
            for n, q in steps:
                st.multiply(pe, n, q)


def third_phases(nc, sig, mem, d):
    sig.begin("mixer")
    mixer_phase(nc, sig, mem, d)
    sig.end()
    sig.begin("ffn")
    ffn_phase(nc, sig, mem, d)


def input_phase(nc, sig, mem, d):
    xt = mem.at("x_t_in", 58, [P, NT, D])
    gamma = mem.at("gamma_in", 16, [P, D])
    beta = mem.at("beta_in", 20, [P, D])
    ln = LayerNorm(nc, sig, mem, xt, gamma, beta, lambda t: d["resid"][t], banks=(4, 5),
                   source=lambda t: (f"x_in_{t}",))
    with nc.Block() as block:
        @block.sync
        def _(sp):
            for t in range(NT):
                sp.dma_start(xt[:, t, :], d["x"][t]).then_inc(*sig.inc(f"x_in_{t}", by=16))
            for i, row in enumerate((gamma, beta)):
                sp.dma_start(row[:, :], d["ln_in"][i].partition_broadcast(P)).then_inc(
                    *sig.inc("ln_params", i, by=16))
            sig.seen[(sig.phase, "ln_params")] = ("ln_params", 1)
            sp.dma_start(mem.ident[:, :], d["ident"]).then_inc(*sig.inc("consts", by=16))
            sp.dma_start(mem.rope[:, :], d["rope"]).then_inc(*sig.inc("consts", by=16))
            sp.dma_start(mem.mask[:, :], d["mask"]).then_inc(*sig.inc("consts", by=16))
            for t in range(NT):
                ln.store(sp, t)
            sp.wait_ge(*sig.after("ln_stored", NT - 1))

        @block.gpsimd
        def _(pool):
            nc.gpsimd.memset(mem.half[:, :], -0.5).then_inc(*sig.inc("half"))
            pool.wait_ge(*sig.after("half"))
            for t in range(NT):
                ln.power(pool, t)
                ln.affine(pool, t)

        @block.scalar
        def _(act):
            for t in range(NT):
                ln.split_hi(act, t)

        @block.vector
        def _(dve):
            for t in range(NT):
                ln.statistics(dve, t)
                ln.normalise(dve, t)
                ln.split_lo(dve, t)

        @block.tensor
        def _(pe):
            pe.wait_ge(*sig.after("consts"))
            for t in range(NT):
                ln.transpose(pe, t)


def program(nc, d, known):
    with ExitStack() as ctx:
        sig = Signals(nc, known)
        mem = Memory(nc, ctx)
        sig.begin("input")
        input_phase(nc, sig, mem, d)
        sig.end()
        sig.begin("layer")
        with nc.Fori(0, LAYERS) as layer:
            layer_phase(nc, sig, mem, d, layer)
            sig.end()
        third_phases(nc, sig, mem, d)
        return sig.seen


def pack_units(what, mats):
    out = np.zeros((len(what), P, UNIT), np.float32)
    for n, (w, k0, nk, c0, cols) in enumerate(what):
        part = mats[w][k0 * P:(k0 + nk) * P, c0:c0 + cols].reshape(nk, P, -1).transpose(1, 0, 2)
        if part.shape[2] < cols:
            part = np.concatenate([part, np.zeros((P, nk, cols - part.shape[2]), np.float32)], 2)
        out[n, :, :nk * cols] = part.reshape(P, -1)
    return out


def blocks(v, col, n):
    return v[col:col + n * P].reshape(n, P).T


def shape_constants():
    t = np.arange(SEQ)
    freqs = np.float32(10000.0) ** (-np.arange(0, 32, 2, dtype=np.float32) / np.float32(32))
    ang = np.concatenate([(t // GRID).astype(np.float32)[:, None] * freqs,
                          (t % GRID).astype(np.float32)[:, None] * freqs], -1).astype(np.float32)
    table = lambda f: f(ang).astype(np.float32).reshape(NT, P, 32).transpose(1, 0, 2).reshape(P, -1)
    i = np.arange(P)
    scale = np.concatenate([np.full((P, n), s, np.float32) for _, n, s in F_BIAS], 1)
    return {
        "ident": np.eye(P, dtype=np.float32),
        "rope": np.concatenate([table(np.cos), table(np.sin)], 1),
        "mask": np.where(i[None, :] <= i[:, None], 0.0, NEG).astype(np.float32),
        "f_scale": scale,
        "s5_q": (i[:, None] // 32 == np.arange(4)[None, :]).astype(np.float32),
        "tri": (i[:, None] <= i[None, :]).astype(np.float32),
        "ones": np.ones((P, P), np.float32),
    }


def lay_out(a):
    o = shape_constants()
    o["x"] = a["x"].reshape(NT, P, D)
    o["ln_in"] = np.stack([a["ln_in_g"], a["ln_in_b"]])
    _, what = layer_units()
    w1, fb, tb, nab = [], [], [], []
    c = np.arange(GRID)
    start = np.clip(c - KW // 2, 0, GRID - KW)
    valid = (c[None, :] >= start[:, None]) & (c[None, :] < start[:, None] + KW)
    col_off = np.clip(c[None, :] - c[:, None] + KW - 1, 0, 2 * KW - 2)
    for l in range(LAYERS):
        mats = {"in": a["w_in"][l], "br_a": a["w_br_a"][l], "br_b": a["w_br_b"][l],
                "br_c": a["w_br_c"][l], "out": a["w_out"][l]}
        w1.append(pack_units(what, mats))
        b = a["b_in"][l]
        fb.append(np.concatenate([blocks(b, col, n) for col, n, _ in F_BIAS], 1))
        gq, sg = 4 * WID, 6 * WID + 256
        pad = np.zeros(256, np.float32)
        tb.append(np.concatenate([b[2 * WID:3 * WID], b[gq:gq + WID], b[gq + WID:gq + WID + 256],
                                  pad, b[sg:sg + 3 * WID]]))
        e = np.where(valid[None, None], a["na_rpb"][l][:, :, col_off], np.float32(NEG))
        m = np.arange(14)
        pair = np.stack([e[:, m + 1], e[:, m]], 1)
        nab.append(pair.transpose(0, 1, 3, 2, 4).reshape(HEADS, P, 14 * GRID))
    o["w1"], o["f_bias"], o["t_bias"], o["na_bias"] = map(np.stack, (w1, fb, tb, nab))
    o["qk_g"] = np.stack([np.concatenate([np.tile(a["q_norm_g"][l], 8), np.tile(a["k_norm_g"][l], 2)])
                          for l in range(LAYERS)])
    o["sg_gb"] = np.stack([a["sg_ln_g"], a["sg_ln_b"]], 1)
    o["sg_w"] = a["sg_w"].transpose(0, 3, 1, 2)
    o["sg_b"] = a["sg_b"].transpose(0, 2, 1)
    o["b_out"] = a["b_out"]
    o["ln_post"] = np.stack([a["ln_post_g"], a["ln_post_b"]], 1)
    b = {k[:-2]: v[0] for k, v in a.items() if k.endswith("_2")}
    w = b["w_in"]
    mats = {"in": w, "fdt": np.concatenate([w[:, C_F:C_F + 8], w[:, C_DT:C_DT + 8]], 1),
            "glu": b["s5_w_glu"], "out": b["w_out"]}
    for r, tag in enumerate("abc"):
        mats["br_" + tag] = b["w_branch"][r]
    o["w2"] = pack_units(mixer_units()[1], mats)
    up = b["ffn_w_up"].reshape(D, 2, NF2, P).transpose(0, 2, 1, 3).reshape(D, 2 * D_FF)
    o["w3"] = pack_units(ffn_units()[1], {"up": up, "down": b["ffn_w_down"]})
    o["bias16"] = np.concatenate([b["fox_f_bias"], b["ssd_dt_bias"]])
    o["dskip"], o["a_log"], o["ssd_norm_w"] = b["ssd_d"], b["ssd_a_log"], b["ssd_norm_w"]
    o["cw"] = np.concatenate([b["ssd_conv_w"], b["ssd_conv_b"][None]]).reshape(
        5, NXBC, P).transpose(2, 1, 0).reshape(P, -1)
    o["s5d"] = b["s5_d"].reshape(NW, P).T
    o["glub"] = b["s5_b_glu"].reshape(NW, P).T
    o["gb"] = b["b_gate"].reshape(3 * ND, P).T
    tiles = lambda v: v.reshape(S5_TILES, P).T
    o["s5in"] = np.stack([tiles(b["s5_a_re"]), tiles(b["s5_a_im"]),
                          tiles(np.repeat(b["s5_log_step"], 64))], 1)

    def block_diagonal(v):
        out = np.zeros((2, 64, S5_TILES, 2, 16), np.float32)
        for i in range(2):
            out[i, :, :, i, :] = v.reshape(S5_TILES, 2, 64, 16)[:, i].transpose(1, 0, 2)
        return out.reshape(P, S5_TILES * 32)

    o["s5_b"] = np.stack([block_diagonal(b["s5_b_re"]), block_diagonal(b["s5_b_im"])])
    o["s5_c"] = np.stack([block_diagonal(b["s5_c_re"].transpose(0, 2, 1)),
                          block_diagonal(b["s5_c_im"].transpose(0, 2, 1))])
    o["ln1"] = np.stack([b["ln1_g"], b["ln1_b"]])
    o["ln2"] = np.stack([b["ln2_g"], b["ln2_b"]])
    cf = np.concatenate([b["ffn_conv_w"], b["ffn_conv_b"][None]])
    o["ffn_cw"] = cf.reshape(4, 2, NF2, P).transpose(3, 2, 1, 0).reshape(P, -1)
    return {"in_" + k: np.ascontiguousarray(v) for k, v in o.items()}


def dram_tensors(nc, shapes):
    d = {k[3:]: nc.dram_tensor(k, list(shape), F32, kind="ExternalInput").ap()
         for k, shape in shapes.items()}
    d["resid"] = nc.dram_tensor("residual", [NT, P, D], F32, kind="Internal").ap()
    d["rows"] = nc.dram_tensor("row_sums_dram", [16, SEQ], F32, kind="Internal").ap()
    d["out"] = nc.dram_tensor("out_0", [NT, P, D], F32, kind="ExternalOutput").ap()
    return d


def kernel(**inputs):
    import concourse.bacc as bacc
    from concourse.bass_utils import run_bass_kernel_spmd

    arrays = lay_out({k: np.asarray(v) for k, v in inputs.items()})
    shapes = {k: v.shape for k, v in arrays.items()}
    known = None
    for _ in range(2):
        nc = bacc.Bacc("TRN2", target_bir_lowering=False, num_devices=1)
        known = program(nc, dram_tensors(nc, shapes), known)
    r = run_bass_kernel_spmd(nc, [arrays], core_ids=[0])
    return r.results[0]["out_0"].reshape(1, SEQ, D)
```

```python
from contextlib import ExitStack

import concourse.bass as bass
import numpy as np
from concourse import mybir

F32 = mybir.dt.float32
F32R = mybir.dt.float32r
I32 = mybir.dt.int32
ACT = mybir.ActivationFunctionType
ALU = mybir.AluOpType
AX = mybir.AxisListType

P = 128
SEQ, D = 512, 1024
NT = SEQ // P
ND = D // P
HD = 64
HEADS = 8
WID = HEADS * HD
NW = WID // P
GRID = 64
KW = 16
LAYERS = 2
ALPHA_1 = (2.0 * LAYERS) ** 0.25
ALPHA_2 = 2.0 ** 0.25
LN_EPS, RMS_EPS, RMS_EPS_2 = 1e-5, 1e-6, 1e-5
UNIT = 2048
RAW, SPLIT = 3, 2
AHEAD = RAW
GRING = 4
SM = HD ** -0.5
NEG = -1e30
LOWEST = -3.0e38


class Signals:

    def __init__(self, nc, known):
        self.nc, self.known = nc, known
        self.sems, self.count, self.seen, self.phase = {}, {}, {}, ""

    def sem(self, name):
        if name not in self.sems:
            self.sems[name] = self.ctx.enter_context(self.nc.semaphore(name))
        return self.sems[name]

    def begin(self, phase):
        self.phase, self.count, self.sems = phase, {}, {}
        self.ctx = ExitStack()

    def end(self):
        nc = self.nc
        engines = (nc.sync, nc.scalar, nc.vector, nc.tensor, nc.gpsimd)
        for i, s in enumerate(self.sems.values()):
            engines[i % len(engines)].sem_clear(s)
        self.nc.all_engine_barrier()
        self.ctx.close()

    def inc(self, name, *key, by=1):
        self.count[name] = self.count.get(name, 0) + by
        self.seen[(self.phase, name) + key] = self.count[name]
        return self.sem(name), by

    def after(self, name, *key):
        if self.known is None:
            return self.sem(name) if name != "unit_done" else self.sem("group"), 1
        value = self.known[(self.phase, name) + key]
        return self.after(*value) if isinstance(value, tuple) else (self.sem(name), value)


class Unit:

    def __init__(self, kind, src, nk, cols, evac, k0=0, of=None, col0=0):
        self.kind, self.src, self.nk, self.cols, self.evac = kind, src, nk, cols, evac
        self.k0, self.of, self.col0 = k0, of or nk, col0
        self.n = nk * cols
        self.gids = []
        self.banks = 4


def plan_groups(units):
    gid = 0
    for n, u in enumerate(units):
        u.n_ = n
        if u.kind == "F":
            blocks = max(u.cols // P, 1)
            u.gids = list(range(gid, gid + blocks))
            gid += blocks
        elif u.k0 == 0:
            u.gids = list(range(gid, gid + NT))
            gid += NT
        else:
            u.gids = units[n - 1].gids


def quarters(u):
    if u.kind == "F" and u.cols == 2 * P:
        h = u.nk // 2
        return [(q // 2, (q % 2) * h, (q % 2) * h + h) for q in range(4)]
    if u.kind == "F" and u.cols < P:
        return [(0, q * u.nk // 4, (q + 1) * u.nk // 4) for q in range(4)]
    return [(q, 0, u.nk) for q in range(4)]


class Stream:

    def __init__(self, nc, sig, mem, units, w_dram, srcs, ready, nxt=None, offset=0):
        self.nc, self.sig, self.mem, self.units, self.w_dram = nc, sig, mem, units, w_dram
        self.nxt, self.offset = nxt, offset
        self.pool_units = ()
        self.srcs, self.ready = srcs, ready
        plan_groups(units)
        self.by_gid = {}
        for u in units:
            for b, g in enumerate(u.gids):
                self.by_gid[g] = (u, b)
        self.bank_of, self.before, last = {}, {}, {}
        for g in sorted(self.by_gid):
            bank = g % self.by_gid[g][0].banks
            self.bank_of[g], self.before[g] = bank, last.get(bank)
            last[bank] = g

    def wait_slot_free(self, eng, gid):
        if self.before[gid] is not None:
            self.wait_read(eng, self.before[gid])

    def wait_read(self, eng, gid):
        u, b = self.by_gid[gid]
        for name in EVAC_READERS[u.evac[0]]:
            eng.wait_ge(*self.sig.after(name, gid))

    def bank(self, gid):
        return self.mem.bank[self.bank_of[gid]]

    def splits(self, n):
        last = len(self.units)
        return n < last and n > 0 or n == last and self.nxt is not None

    def size(self, n):
        return self.units[n].n if n < len(self.units) else UNIT

    def load(self, sp, n):
        if n < AHEAD and self.units:
            return
        s, count = (n + self.offset) % RAW, self.size(n)
        if n > RAW:
            sp.wait_ge(*self.sig.after("w_lo", n - RAW))
        src = self.w_dram(n) if n < len(self.units) else self.nxt(n - len(self.units))
        sp.dma_start(self.mem.raw[s][:, 0:count], src[:, 0:count]).then_inc(
            *self.sig.inc(f"w_raw{s}", n, by=16))

    def load_next(self, sp):
        for n in range(len(self.units), len(self.units) + AHEAD):
            self.load(sp, n)
        for n in range(len(self.units), len(self.units) + AHEAD):
            sp.wait_ge(*self.sig.after(f"w_raw{(n + self.offset) % RAW}", n))

    def hi(self, act, n):
        if not self.splits(n):
            return
        s, r, count = (n + self.offset) % SPLIT, (n + self.offset) % RAW, self.size(n)
        if n >= AHEAD or not self.units:
            act.wait_ge(*self.sig.after(f"w_raw{r}", n))
        if n >= SPLIT:
            act.wait_ge(*self.sig.after("unit_done", n - SPLIT))
        self.nc.scalar.activation(self.mem.wh[s][:, 0:count], self.mem.raw[r][:, 0:count],
                                  ACT.Copy).then_inc(*self.sig.inc("w_hi", n))

    def lo(self, dve, n):
        if n not in self.pool_units:
            self.subtract(dve, self.nc.vector, n, "w_lo")

    def lo_on_pool(self, pool, n):
        if n in self.pool_units:
            self.subtract(pool, self.nc.gpsimd, n, "w_lo_pool")

    def subtract(self, eng, on, n, signal):
        if not self.splits(n):
            return
        s, r, count = (n + self.offset) % SPLIT, (n + self.offset) % RAW, self.size(n)
        eng.wait_ge(*self.sig.after("w_hi", n))
        on.tensor_tensor(self.mem.wl[s][:, 0:count], self.mem.raw[r][:, 0:count],
                         self.mem.wh[s][:, 0:count].bitcast(F32), ALU.subtract).then_inc(
            *self.sig.inc(signal, n))
        if signal != "w_lo":
            self.sig.seen[(self.sig.phase, "w_lo", n)] = (signal, n)

    def multiply(self, pe, n, q):
        u, s = self.units[n], (n + self.offset) % SPLIT
        if q == 0:
            if n:
                pe.wait_ge(*self.sig.after("w_lo", n))
            for what in self.ready(u):
                pe.wait_ge(*self.sig.after(*what))
        b, ka, kb = quarters(u)[q]
        gid = u.gids[b]
        first = u.k0 + ka == 0
        if first:
            self.wait_slot_free(pe, gid)
            if self.before[gid] is None:
                pe.wait_ge(*self.sig.after("x_lo", ND // 2 + self.bank_of[gid]))
        wh = self.mem.wh[s][:, 0:u.n].rearrange("p (k c) -> p k c", c=u.cols)
        wl = self.mem.wl[s][:, 0:u.n].rearrange("p (k c) -> p k c", c=u.cols)
        xh, xl = self.srcs[u.src]
        last = None
        for k in range(ka, kb):
            kk = u.k0 + k
            if n == 0 and b == 0:
                pe.wait_ge(*self.sig.after("x_lo", k))
            stop = kk == u.of - 1
            if u.kind == "F":
                w = slice(b * P, min((b + 1) * P, u.cols))
                trio = [(wh[:, k, w], xh[:, kk, :]), (wh[:, k, w], xl[:, kk, :]),
                        (wl[:, k, w], xh[:, kk, :])]
                dst = self.bank(gid)[0:min(P, u.cols), :]
            else:
                t = slice(b * P, (b + 1) * P)
                trio = [(xh[:, kk, t], wh[:, k, :]), (xh[:, kk, t], wl[:, k, :]),
                        (xl[:, kk, t], wh[:, k, :])]
                dst = self.bank(gid)[:, 0:u.cols]
            for i, (stationary, moving) in enumerate(trio):
                last = self.nc.tensor.matmul(dst, stationary, moving, start=kk == 0 and i == 0,
                                             stop=stop and i == 2)
        complete = u.k0 + kb == u.of
        if complete:
            last.then_inc(*self.sig.inc("group", gid))
        if q == 3:
            if complete:
                self.sig.seen[(self.sig.phase, "unit_done", n)] = ("group", gid)
            else:
                last.then_inc(*self.sig.inc("unit_part", n))
                self.sig.seen[(self.sig.phase, "unit_done", n)] = ("unit_part", n)


EVAC_READERS = {
    "scaled": ("ev_act",), "silu": ("ev_act",), "gate": ("ev_act",), "biased": ("ev_dve",),
    "branch": ("ev_dve",), "residual": ("ev_dve",), "plain": ("ev_act",), "copy_t": ("ev_dve",),
    "few": ("ev_act",), "conv": ("ev_dve",), "conv_ffn": ("ev_dve",), "glu": ("ev_act",),
}


class Memory:

    def __init__(self, nc, ctx):
        self.nc, self.ctx = nc, ctx
        sb = lambda name, shape, dt=F32: ctx.enter_context(nc.sbuf_tensor(name, shape, dt))
        self.x_base = (nc.sbuf_base + 31) // 32 * 32
        self.xh = sb("x_hi", [P, ND, SEQ], F32R)
        self.xl = sb("x_lo", [P, ND, SEQ], F32R)
        self.raw = [sb(f"w_raw_{i}", [P, UNIT]) for i in range(RAW)]
        self.wh = [sb(f"w_hi_{i}", [P, UNIT], F32R) for i in range(SPLIT)]
        self.wl = [sb(f"w_lo_{i}", [P, UNIT], F32R) for i in range(SPLIT)]
        self.ident = sb("ident", [P, P])
        self.tbias = [sb(f"tbias_{i}", [P, 512]) for i in range(2)]
        self.half = sb("minus_half", [P, 12])
        self.cols = sb("ln_columns", [P, 2 * ND])
        self.small = sb("small", [P, 512])
        self.small2 = sb("small_2", [P, 352])
        self.rope = sb("rope", [P, 2 * NT * 32])
        self.mask = sb("causal_mask", [P, P])
        self.arena_kb = 110
        self.base = (nc.sbuf_base + 31) // 32 * 32
        ctx.enter_context(nc.sbuf_tensor("arena", [P, self.arena_kb * 256], F32))
        self.bank = [ctx.enter_context(nc.psum_tensor(f"bank_{i}", [P, 512], F32)) for i in range(4)]
        self.upper = ctx.enter_context(nc.psum_tensor("banks_4_to_7", [P, 4, 512], F32))
        self.bank += [self.upper[:, i, :] for i in range(4)]

    def at(self, name, kb, shape, dt=F32):
        n = 4 * int(np.prod(shape[1:]))
        assert kb * 1024 + n <= self.arena_kb * 1024, name
        return self.nc.alloc_sbuf_tensor_at(name, shape, dt, offset=int(self.base + kb * 1024))


class LayerNorm:

    def __init__(self, nc, sig, mem, xt, keep, source, answer=False, bank_free=None):
        self.nc, self.sig, self.mem, self.xt = nc, sig, mem, xt
        self.keep, self.source, self.answer, self.bank_free = keep, source, answer, bank_free
        self.stats = mem.small[:, 0:NT * 12].rearrange("p (t s) -> p t s", s=12)
        self.mv = mem.small[:, 48:48 + 2 * NT].rearrange("p (t s) -> p t s", s=2)
        self.rstd = mem.small[:, 56:56 + NT]
        self.shift = mem.small[:, 60:60 + NT]

    def half(self, dve, t, i):
        dve.wait_ge(*self.sig.after(*self.source(t, i)))
        self.nc.vector.bn_stats(self.stats[:, t, 6 * i:6 * i + 6],
                                self.xt[:, t, 512 * i:512 * i + 512]).then_inc(
            *self.sig.inc("ln_stats", t, i))

    def moments(self, dve, t):
        sig, nc = self.sig, self.nc
        for i in range(2):
            dve.wait_ge(*sig.after("ln_stats", t, i))
        nc.vector.bn_aggr(self.mv[:, t, :], self.stats[:, t, :]).then_inc(*sig.inc("ln_mv", t))
        dve.wait_ge(*sig.after("ln_mv", t))
        nc.vector.tensor_scalar(self.mv[:, t, 1:2], self.mv[:, t, 1:2], LN_EPS, None,
                                ALU.add).then_inc(*sig.inc("ln_var", t))

    def power(self, pool, t):
        pool.wait_ge(*self.sig.after("ln_var", t))
        self.nc.gpsimd.tensor_tensor(self.rstd[:, t:t + 1], self.mv[:, t, 1:2],
                                     self.mem.half[:, 0:1], ALU.pow).then_inc(
            *self.sig.inc("ln_rstd", t))
        if self.answer:
            return
        pool.wait_ge(*self.sig.after("ln_rstd", t))
        self.nc.gpsimd.tensor_scalar(self.shift[:, t:t + 1], self.mv[:, t, 0:1],
                                     self.rstd[:, t:t + 1], -1.0, ALU.mult, ALU.mult).then_inc(
            *self.sig.inc("ln_shift", t))

    def normalise(self, act, t):
        act.wait_ge(*self.sig.after("ln_shift", t))
        for i in range(2):
            x = self.xt[:, t, 512 * i:512 * i + 512]
            self.nc.scalar.activation(x, x, ACT.Identity, bias=self.shift[:, t:t + 1],
                                      scale=self.rstd[:, t:t + 1]).then_inc(
                *self.sig.inc("ln_centred", t, i))

    def finish(self, dve, t, gamma, beta):
        sig, x = self.sig, self.xt[:, t, :]
        self.nc.vector.scalar_tensor_tensor(x, x, self.mv[:, t, 0:1], gamma[:, :], ALU.subtract,
                                            ALU.mult).then_inc(*sig.inc("ln_scaled", t))
        dve.wait_ge(*sig.after("ln_scaled", t))
        dve.wait_ge(*sig.after("ln_rstd", t))
        self.nc.vector.scalar_tensor_tensor(x, x, self.rstd[:, t:t + 1], beta[:, :], ALU.mult,
                                            ALU.add).then_inc(*sig.inc("ln_centred", t, 1))

    def store(self, sp, t):
        sp.wait_ge(*self.sig.after("ln_centred", t, 1))
        sp.dma_start(self.keep(t), self.xt[:, t, :]).then_inc(*self.sig.inc("ln_stored", t, by=16))

    def bank(self, f):
        return self.mem.bank[(f + 4) % 8]

    def transpose(self, pe):
        sig = self.sig
        for i in range(2):
            for t in range(NT):
                pe.wait_ge(*sig.after("ln_centred", t, i))
                for f in range(4 * i, 4 * i + 4):
                    if i and t == 0 and self.bank_free is not None:
                        pe.wait_ge(*sig.after(*self.bank_free(f - 4)))
                    ins = self.nc.tensor.transpose(self.bank(f)[:, t * P:(t + 1) * P],
                                                   self.xt[:, t, f * P:(f + 1) * P],
                                                   self.mem.ident[:, :])
                    if t == NT - 1:
                        ins.then_inc(*sig.inc("x_transposed", f))

class InputSplit:

    ORDER = (4, 0, 1, 2, 3, 5, 6, 7)

    def __init__(self, nc, sig, mem, work):
        self.nc, self.sig, self.mem, self.work = nc, sig, mem, work

    def bank(self, f):
        return self.mem.bank[(f + 4) % 8]

    def affine(self, f):
        return self.mem.cols[:, f:f + 1], self.mem.cols[:, ND + f:ND + f + 1]

    def split_hi(self, act):
        for i, f in enumerate(self.ORDER):
            g, b = self.affine(f)
            if i % 2 == 0:
                if i >= 2:
                    act.wait_ge(*self.sig.after("x_lo", self.ORDER[i - 2]))
                self.nc.scalar.activation(self.work[:, 0, :], self.bank(f)[:, :], ACT.Identity,
                                          bias=b, scale=g)
            self.nc.scalar.activation(self.mem.xh[:, f, :], self.bank(f)[:, :], ACT.Identity,
                                      bias=b, scale=g).then_inc(*self.sig.inc("x_hi", f))

    def split_lo(self, dve):
        sig = self.sig
        for i, f in enumerate(self.ORDER):
            dve.wait_ge(*sig.after("x_hi", f))
            if i % 2:
                if i >= 2:
                    dve.wait_ge(*sig.after("x_lo", self.ORDER[i - 2]))
                g, b = self.affine(f)
                self.nc.vector.tensor_scalar(self.work[:, 1, :], self.bank(f)[:, :], g, b,
                                             ALU.mult, ALU.add).then_inc(*sig.inc("x_whole", f))
                dve.wait_ge(*sig.after("x_whole", f))
            self.nc.vector.tensor_tensor(self.mem.xl[:, f, :], self.work[:, i % 2, :],
                                         self.mem.xh[:, f, :].bitcast(F32),
                                         ALU.subtract).then_inc(*sig.inc("x_lo", f))


def scale_residual(pool, nc, sig, xt, rows, alpha, more=None):
    g, b = rows
    pool.wait_ge(*sig.after("residual_rows"))
    nc.gpsimd.tensor_scalar(g[:, :], g[:, :], alpha, None, ALU.mult)
    nc.gpsimd.tensor_scalar(b[:, :], b[:, :], alpha, None, ALU.mult).then_inc(
        *sig.inc("rows_scaled"))
    pool.wait_ge(*sig.after("rows_scaled"))
    if more is not None:
        pool.wait_ge(*sig.after("b_out"))
        nc.gpsimd.tensor_tensor(b[:, :], b[:, :], more[:, :], ALU.add).then_inc(
            *sig.inc("rows_summed"))
        pool.wait_ge(*sig.after("rows_summed"))


def residual_block(pool, nc, sig, xt, rows, t):
    x = xt[:, t, :]
    if t == 0:
        pool.wait_ge(*sig.after("x_t_loaded"))
    nc.gpsimd.tensor_tensor(x, x, rows[0][:, :], ALU.mult).then_inc(*sig.inc("x_scaled", t))
    pool.wait_ge(*sig.after("x_scaled", t))
    nc.gpsimd.tensor_tensor(x, x, rows[1][:, :], ALU.add).then_inc(*sig.inc("residual", t))


class Attention:

    LAG_PV = 7
    STEPS = HEADS * NT + LAG_PV

    def __init__(self, nc, sig, mem, name, q, k, v, y, causal, bias, probs, pt, scale=1.0,
                 gate=None, needs=None, base=(), rows=None,
                 lag=2):
        self.nc, self.sig, self.mem, self.name = nc, sig, mem, name
        self.q, self.k, self.v, self.y, self.causal, self.bias = q, k, v, y, causal, bias
        self.probs, self.pt, self.scale, self.gate = probs, pt, scale, gate
        self.needs, self.base, self.rows, self.lag = needs, base, rows, lag

    def keys(self, i):
        return (i + 1) * P if self.causal else SEQ

    def scores(self, pe, j):
        if not 0 <= j < HEADS * NT:
            return
        h, i = divmod(j, NT)
        if j >= 2:
            pe.wait_ge(*self.sig.after(self.name + "_exp", j - 2))
        else:
            for w in self.base:
                pe.wait_ge(*self.sig.after(*w))
        for w in self.needs(h):
            pe.wait_ge(*self.sig.after(*w))
        n = self.keys(i)
        self.nc.tensor.matmul(self.mem.bank[4 + j % 2][:, 0:n], self.q(h, i), self.k(h)[:, 0:n],
                              start=True, stop=True).then_inc(*self.sig.inc(self.name + "_scores", j))

    def maximum(self, dve, j):
        if not 0 <= j < HEADS * NT:
            return
        sig, nc, name = self.sig, self.nc, self.name
        h, i = divmod(j, NT)
        n = self.keys(i)
        dve.wait_ge(*sig.after(name + "_scores", j))
        mx, nmx = self.mem.small[:, 64 + j % 8:65 + j % 8], self.mem.small[:, 72 + j % 8:73 + j % 8]
        ps = self.mem.bank[4 + j % 2]
        if self.bias is not None:
            if self.causal:
                nc.vector.tensor_tensor(ps[:, n - P:n], ps[:, n - P:n], self.mem.mask[:, :],
                                        ALU.add).then_inc(*sig.inc(name + "_masked", j))
                dve.wait_ge(*sig.after(name + "_masked", j))
            ap, ready = self.bias(h, i)
            dve.wait_ge(*sig.after(*ready))
            if j >= 3:
                dve.wait_ge(*sig.after(name + "_transposed", j - 3))
            nc.vector.tensor_tensor_reduce(
                out=self.probs[:, j % 3, 0:n], in0=ps[:, 0:n], in1=ap[:, 0:n], scale=1.0,
                scalar=LOWEST, op0=ALU.add, op1=ALU.max, accum_out=mx).then_inc(
                *sig.inc(name + "_max", j))
        else:
            nc.vector.tensor_reduce(mx, ps[:, 0:n], AX.X, ALU.max).then_inc(
                *sig.inc(name + "_max", j))
        dve.wait_ge(*sig.after(name + "_max", j))
        if self.rows is not None:
            c = self.rows(h, i)
            nc.vector.tensor_scalar(mx, mx, c, -1.0, ALU.add, ALU.mult).then_inc(
                *sig.inc(name + "_rowmax", j))
            dve.wait_ge(*sig.after(name + "_rowmax", j))
            nc.vector.tensor_scalar(nmx, mx, c, None, ALU.add).then_inc(*sig.inc(name + "_nmax", j))
        else:
            nc.vector.tensor_scalar(nmx, mx, -self.scale, None, ALU.mult).then_inc(
                *sig.inc(name + "_nmax", j))

    def exponent(self, act, j):
        if not 0 <= j < HEADS * NT:
            return
        sig, name = self.sig, self.name
        n = self.keys(j % NT)
        act.wait_ge(*sig.after(name + "_nmax", j))
        src = self.probs[:, j % 3, 0:n] if self.bias is not None else self.mem.bank[4 + j % 2][:, 0:n]
        if self.bias is None and j >= 3:
            act.wait_ge(*sig.after(name + "_transposed", j - 3))
        self.nc.scalar.activation(self.probs[:, j % 3, 0:n], src, ACT.Exp,
                                  bias=self.mem.small[:, 72 + j % 8:73 + j % 8], scale=self.scale,
                                  accum_out=self.mem.small[:, 80 + j % 8:81 + j % 8]).then_inc(
            *sig.inc(name + "_exp", j))

    def normalise(self, dve, j):
        if not 0 <= j < HEADS * NT:
            return
        sig, nc, name = self.sig, self.nc, self.name
        n = self.keys(j % NT)
        dve.wait_ge(*sig.after(name + "_exp", j))
        inv = self.mem.small[:, 88 + j % 8:89 + j % 8]
        nc.vector.reciprocal(inv, self.mem.small[:, 80 + j % 8:81 + j % 8]).then_inc(
            *sig.inc(name + "_inv", j))
        dve.wait_ge(*sig.after(name + "_inv", j))
        nc.vector.tensor_scalar(self.probs[:, j % 3, 0:n], self.probs[:, j % 3, 0:n], inv, None,
                                ALU.mult).then_inc(*sig.inc(name + "_probs", j))

    def transpose(self, pe, j):
        if not 0 <= j < HEADS * NT:
            return
        sig, name = self.sig, self.name
        pe.wait_ge(*sig.after(name + "_probs", j))
        if j:
            pe.wait_ge(*sig.after(name + "_pt", j - 1))
        for kb in range(self.keys(j % NT) // P):
            last = self.nc.tensor.transpose(self.mem.bank[6][:, kb * P:(kb + 1) * P],
                                            self.probs[:, j % 3, kb * P:(kb + 1) * P],
                                            self.mem.ident[:, :])
        last.then_inc(*sig.inc(name + "_transposed", j))

    def keep_transposed(self, act, j):
        if not 0 <= j < HEADS * NT:
            return
        sig, name = self.sig, self.name
        h, i = divmod(j, NT)
        nk = self.keys(i) // P
        act.wait_ge(*sig.after(name + "_transposed", j))
        if h >= 2:
            act.wait_ge(*sig.after(name + "_pv", h - 2))
        self.nc.scalar.activation(
            self.pt[:, h % 2, 0:nk, i * P:(i + 1) * P],
            self.mem.bank[6][:, 0:nk * P].rearrange("p (k c) -> p k c", c=P), ACT.Copy).then_inc(
            *sig.inc(name + "_pt", j))

    def values(self, pe, j):
        if not 0 <= j < HEADS * NT:
            return
        sig, name = self.sig, self.name
        h, kb = divmod(j, NT)
        if kb == 0:
            pe.wait_ge(*sig.after(name + "_pt", h * NT + NT - 1))
            if h:
                pe.wait_ge(*sig.after(name + "_y", h - 1))
        q0 = kb * P if self.causal else 0
        half = slice((h % 2) * HD, (h % 2) * HD + HD)
        ins = self.nc.tensor.matmul(self.mem.bank[7][half, q0:SEQ], self.v(h, kb),
                                    self.pt[:, h % 2, kb, q0:SEQ], start=kb == 0, stop=kb == NT - 1)
        if kb == NT - 1:
            ins.then_inc(*sig.inc(name + "_pv", h))

    def output(self, dve, j):
        if not 0 <= j < HEADS * NT or j % NT != NT - 1:
            return
        sig, h = self.sig, j // NT
        dve.wait_ge(*sig.after(self.name + "_pv", h))
        half = slice((h % 2) * HD, (h % 2) * HD + HD)
        y = self.y[half, h // 2, :]
        if self.gate is None:
            ins = self.nc.vector.tensor_copy(y, self.mem.bank[7][half, :])
        else:
            dve.wait_ge(*sig.after(*self.gate(h)))
            ins = self.nc.vector.tensor_tensor(y, self.mem.bank[7][half, :], y, ALU.mult)
        ins.then_inc(*sig.inc(self.name + "_y", h))

    def on_pe(self, pe, j):
        self.scores(pe, j)
        self.transpose(pe, j - self.lag)
        self.values(pe, j - self.LAG_PV)

    def on_act(self, act, j):
        self.exponent(act, j)
        self.keep_transposed(act, j - self.lag)

    def on_dve(self, dve, j):
        self.maximum(dve, j)
        self.normalise(dve, j - 1)
        self.output(dve, j - self.LAG_PV)


def emit_common_evac(nc, sig, mem, stream, u, b, gid, eng_name, eng, ctx):
    kind, tag = u.evac[0], u.evac[1]
    ps = stream.bank(gid)
    if eng_name == "act":
        if kind == "scaled":
            dst, bias, scale = ctx["scaled"](tag, u.evac[2] + b)
            eng.wait_ge(*sig.after("group", gid))
            for w in ctx["before"](tag):
                eng.wait_ge(*sig.after(*w))
            nc.scalar.activation(dst, ps[:, :], ACT.Identity, bias=bias, scale=scale).then_inc(
                *sig.inc("ev_act", gid))
        elif kind in ("silu", "gate"):
            g = ctx["g_slot"][gid]
            eng.wait_ge(*sig.after("group", gid))
            if g >= GRING:
                eng.wait_ge(*sig.after(*ctx["g_used"][g - GRING]))
            for w in ctx["before"](tag):
                eng.wait_ge(*sig.after(*w))
            bias = ctx["half_bias"](tag, u.evac[2] + b)
            ins = nc.scalar.activation(ctx["g"][:, g % GRING, :], ps[:, :], ACT.Tanh, bias=bias,
                                       scale=0.5)
            if kind == "silu":
                ins.then_inc(*sig.inc("tanh", gid))
                nc.scalar.activation(ctx["scaled"](tag, u.evac[2] + b)[0], ps[:, :], ACT.Identity,
                                     bias=bias, scale=0.5).then_inc(*sig.inc("ev_act", gid))
            else:
                ins.then_inc(*sig.inc("ev_act", gid))
        elif kind == "plain":
            eng.wait_ge(*sig.after("group", gid))
            nc.scalar.activation(ctx["scaled"](tag, u.evac[2] + b)[0], ps[:, :], ACT.Copy).then_inc(
                *sig.inc("ev_act", gid))
    if eng_name == "dve":
        if kind == "silu":
            g = ctx["g_slot"][gid]
            eng.wait_ge(*sig.after("ev_act", gid))
            z = ctx["scaled"](tag, u.evac[2] + b)[0]
            nc.vector.scalar_tensor_tensor(z, ctx["g"][:, g % GRING, :], 1.0, z, ALU.add,
                                           ALU.mult).then_inc(*sig.inc("silu", gid))
        elif kind == "biased":
            eng.wait_ge(*sig.after("group", gid))
            if b == 0:
                eng.wait_ge(*sig.after("tbias", u.evac[2]))
                for w in ctx["before"](tag):
                    eng.wait_ge(*sig.after(*w))
            nc.vector.tensor_tensor(ctx["t_dst"](tag, b), ps[:, 0:u.cols],
                                    mem.tbias[u.evac[2] % 2][:, 0:u.cols], ALU.add).then_inc(
                *sig.inc("ev_dve", gid))
        elif kind == "copy_t":
            eng.wait_ge(*sig.after("group", gid))
            nc.vector.tensor_copy(ctx["t_dst"](tag, b), ps[:, 0:u.cols]).then_inc(
                *sig.inc("ev_dve", gid))
        elif kind == "branch":
            fb = u.evac[2] + b
            gate_gid = ctx["gate_of"][(tag, fb)]
            eng.wait_ge(*sig.after("group", gid))
            eng.wait_ge(*sig.after("ev_act", gate_gid))
            if tag == "a":
                if fb == 0:
                    for w in ctx["before"]("merged"):
                        eng.wait_ge(*sig.after(*w))
                dst = ctx["merged"][:, fb, :]
            else:
                i = ctx["tmp_index"][gid]
                dst = ctx["tmp"][:, i % 2, :]
                if i >= 2:
                    eng.wait_ge(*sig.after("merge", i - 2))
            nc.vector.scalar_tensor_tensor(dst, ctx["g"][:, ctx["g_slot"][gate_gid] % GRING, :], 1.0,
                                           ps[:, :], ALU.add, ALU.mult).then_inc(
                *sig.inc("ev_dve", gid))
        elif kind == "residual":
            eng.wait_ge(*sig.after("group", gid))
            eng.wait_ge(*sig.after("residual", b))
            c = u.evac[2]
            nc.vector.tensor_tensor(ctx["xt"][:, b, c:c + 512], ctx["xt"][:, b, c:c + 512],
                                    ps[:, :], ALU.add).then_inc(*sig.inc("ev_dve", gid))
    if eng_name == "pool" and kind == "branch" and tag != "a":
        fb = u.evac[2] + b
        i = ctx["tmp_index"][gid]
        eng.wait_ge(*sig.after("ev_dve", gid))
        if i == 0:
            eng.wait_ge(*sig.after("ev_dve", ctx["branch_gid"][("a", ND - 1)]))
        if i >= ND:
            eng.wait_ge(*sig.after("merge", i - ND))
        nc.gpsimd.tensor_tensor(ctx["merged"][:, fb, :], ctx["merged"][:, fb, :],
                                ctx["tmp"][:, i % 2, :], ALU.add).then_inc(*sig.inc("merge", i))


def gate_plan(stream):
    slot, used, gate_of, branch_gid, tmp_index, n, m = {}, {}, {}, {}, {}, 0, 0
    for gid in sorted(stream.by_gid):
        u, b = stream.by_gid[gid]
        if u.evac[0] in ("silu", "gate"):
            slot[gid] = n
            if u.evac[0] == "silu":
                used[n] = ("silu", gid)
            else:
                gate_of[(u.evac[1], u.evac[2] + b)] = gid
            n += 1
        elif u.evac[0] == "branch":
            branch_gid[(u.evac[1], u.evac[2] + b)] = gid
            if u.evac[1] != "a":
                tmp_index[gid] = m
                m += 1
    for key, gid in branch_gid.items():
        used[slot[gate_of[key]]] = ("ev_dve", gid)
    return dict(g_slot=slot, g_used=used, gate_of=gate_of, branch_gid=branch_gid,
                tmp_index=tmp_index)


def layer_units():
    units, what = [], []

    def f_blocks(evac, tag, col, nblocks, blk0=0):
        for i in range(0, nblocks, 2):
            units.append(Unit("F", "x", ND, 2 * P, (evac, tag, blk0 + i)))
            what.append(("in", 0, ND, col + i * P, 2 * P))

    def t_cols(evac, tag, col, section, src="x", w="in"):
        for half in range(2):
            units.append(Unit("T", src, 4, 512, (evac, tag, section), k0=4 * half, of=ND))
            what.append((w, 4 * half, 4, col, 512))

    def branch(tag, col):
        for half in range(2):
            f_blocks("gate", tag, col + 4 * half * P, 4, 4 * half)
            units.append(Unit("F", "y", NW, 512, ("branch", tag, 4 * half)))
            what.append(("br_" + tag, 0, NW, 512 * half, 512))

    f_blocks("scaled", "na_q", 0, NW)
    f_blocks("scaled", "na_k", WID, NW)
    t_cols("biased", "na_v", 2 * WID, 0)
    f_blocks("silu", "z_a", 3 * WID, NW)
    gq = 4 * WID
    t_cols("biased", "gq_q", gq, 1)
    for half in range(2):
        units.append(Unit("T", "x", 4, 256, ("biased", "gq_kv", 2), k0=4 * half, of=ND))
        what.append(("in", 4 * half, 4, gq + WID, 256))
    gz = gq + WID + 256
    sg = gz + WID
    t_cols("biased", "sg_u", sg, 3)
    t_cols("biased", "sg_v", sg + WID, 4)
    t_cols("biased", "sg_z", sg + 2 * WID, 5)
    f_blocks("silu", "z_b", gz, NW)
    gates = sg + 3 * WID
    branch("a", gates)
    branch("c", gates + 2 * D)
    branch("b", gates + D)
    for c in (0, 512):
        t_cols("residual", "out", c, c, src="m", w="out")
    return units, what


F_BIAS = [(0, NW, SM), (WID, NW, 1.0), (3 * WID, NW, 0.5), (4 * WID + WID + 256, NW, 0.5),
          (5 * WID + 256 + 4 * WID, 3 * ND, 0.5)]
F_BLOCK = {"na_q": 0, "na_k": 4, "z_a": 8, "z_b": 12, "a": 16, "b": 24, "c": 32}
NF = 40


def layer_phase(nc, sig, mem, d, layer):
    units, _ = layer_units()
    n_units = len(units)
    at = mem.at
    nq = at("na_q", 0, [P, NW, SEQ])
    nk = at("na_k", 8, [P, NW, SEQ])
    nv = at("na_v", 16, [P, NT, WID])
    yh = at("y_hi", 0, [P, NW, SEQ], F32R)
    yl = at("y_lo", 8, [P, NW, SEQ], F32R)
    sz = at("sg_z", 0, [P, NT, WID])
    sgw = at("sg_w", 8, [P, 8, P])
    sgg = at("sg_g", 12, [P, WID])
    sgbeta = at("sg_beta", 14, [P, WID])
    qkg = at("qk_g", 41, [P, 10, HD])
    yc = at("y_c", 16, [P, NW, SEQ])
    rows = at("gamma", 16, [P, D]), at("beta", 20, [P, D])
    qk = at("gq_qk", 24, [P, NT, 640])
    yb = at("y_b", 24, [P, NW, SEQ])
    mh = at("m_hi", 24, [P, ND, SEQ], F32R)
    ml = at("m_lo", 40, [P, ND, SEQ], F32R)
    gv = at("gq_v", 34, [P, NT, P])
    gq = at("gq_q", 36, [P, NW, SEQ])
    gk = at("gq_k", 44, [P, 2, SEQ])
    probs = at("probs", 48, [P, 3, SEQ])
    pt = at("probs_t", 54, [P, 2, NT, SEQ])
    sgt = at("sg_tanh", 54, [P, NT, WID])
    nab = at("na_bias", 70, [P, 2, 14 * GRID])
    xt = at("x_t", 58, [P, NT, D])
    sq = at("squares", 36, [P, 2, 640])
    rp = at("rope_products", 70, [P, 640])
    ro = at("rotated", 72.5, [P, 6 * P])
    su = at("sg_u", 77, [P, NT, WID])
    sv = at("sg_v", 85, [P, NT, WID])
    merged = at("merged", 77, [P, ND, SEQ])
    ya = at("y_a", 93, [P, NW, SEQ])
    bout = at("b_out", 93, [P, D])
    tmp = at("branch_tmp", 97, [P, 2, SEQ])
    g = at("gates", 101, [P, GRING, SEQ])
    sgb = mem.small[:, 96:104]
    ss, r = mem.small[:, 104:114], mem.small[:, 114:124]
    sst = mem.small[:, 124:148].rearrange("p (t s) -> p t s", s=6)
    smv = mem.small[:, 148:156].rearrange("p (t s) -> p t s", s=2)
    srs = mem.small[:, 156:160]
    fb_raw = mem.small[:, 160:160 + NF]
    fb_ = mem.small[:, 200:200 + NF]
    fscale = mem.small[:, 240:240 + NF]
    cos = mem.rope[:, 0:NT * 32].rearrange("p (t f) -> p t f", f=32)
    sin = mem.rope[:, NT * 32:].rearrange("p (t f) -> p t f", f=32)

    w_dram = lambda n: d["w1"][bass.ds(layer, 1), n].rearrange("o p c -> (o p) c")
    gid_of = {}

    def ready(u):
        if u.src == "y":
            return [("y_lo", u.evac[1])]
        if u.src == "m":
            return [("m_lo", 4 * (u.k0 // 4) + 3)]
        return []

    st = Stream(nc, sig, mem, units, w_dram, {"x": (mem.xh, mem.xl), "y": (yh, yl), "m": (mh, ml)},
                ready, nxt=lambda j: d["w_first"][bass.ds(layer + 1, 1), j].rearrange(
                    "o p c -> (o p) c"))
    assert n_units % (RAW * SPLIT) == 0
    tags = [u.evac[:2] for u in units]
    st.pool_units = [*range(tags.index(("silu", "z_a")), tags.index(("biased", "sg_u"))),
                     *range(tags.index(("branch", "a")), tags.index(("gate", "b")))]
    for gid, (u, b) in st.by_gid.items():
        gid_of[(u.evac[1], u.evac[2] + b if u.kind == "F" else b)] = gid
        if u.evac[0] == "residual":
            gid_of[("out", u.evac[2], b)] = gid
    G = gid_of.get
    last_u = {u.evac[1]: n for n, u in enumerate(units)}

    def before(tag):
        return {"sg_z": [("na_pv", HEADS - 1)], "z_b": [("rope_done", NT - 1)],
                "merged": [("yct", NW - 1), ("mix", 3)]}.get(tag, [])

    dst = {"na_q": nq, "na_k": nk, "z_a": ya, "z_b": yb}
    ctx = dict(g=g, merged=merged, tmp=tmp, xt=xt, before=before, **gate_plan(st))
    ctx["scaled"] = lambda tag, b: (dst[tag][:, b, :], fb_[:, F_BLOCK[tag] + b:F_BLOCK[tag] + b + 1],
                                    SM if tag == "na_q" else 1.0)
    ctx["half_bias"] = lambda tag, b: fb_[:, F_BLOCK[tag] + b:F_BLOCK[tag] + b + 1]
    ctx["t_dst"] = lambda tag, t: {"na_v": nv[:, t, :], "gq_q": qk[:, t, 0:WID], "sg_u": su[:, t, :],
                                   "sg_v": sv[:, t, :], "sg_z": sz[:, t, :]}[tag]

    na = Attention(
        nc, sig, mem, "na",
        q=lambda h, i: nq[(h % 2) * HD:(h % 2) * HD + HD, h // 2, i * P:(i + 1) * P],
        k=lambda h: nk[(h % 2) * HD:(h % 2) * HD + HD, h // 2, :],
        v=lambda h, kb: nv[:, kb, h * HD:(h + 1) * HD], y=ya, causal=False,
        bias=lambda h, i: (nab[:, h % 2, (6 - 2 * i) * GRID:(6 - 2 * i) * GRID + SEQ],
                           ("na_bias", h)),
        probs=probs, pt=pt, gate=lambda h: ("silu", G(("z_a", h // 2))),
        needs=lambda h: [("ev_act", G(("na_k", h // 2))), ("ev_dve", G(("na_v", NT - 1)))])
    gqa = Attention(
        nc, sig, mem, "gq",
        q=lambda h, i: gq[(h % 2) * HD:(h % 2) * HD + HD, h // 2, i * P:(i + 1) * P],
        k=lambda h: gk[(h % 2) * HD:(h % 2) * HD + HD, h // 4, :],
        v=lambda h, kb: gv[:, kb, (h // 4) * HD:(h // 4) * HD + HD], y=yb, causal=False,
        bias=None, probs=probs, pt=pt, scale=SM, gate=lambda h: ("silu", G(("z_b", h // 2))),
        base=[("na_y", HEADS - 1), ("rot_kept", NT - 1), ("ycf", NW - 1), ("mixed", 3)],
        needs=lambda h: [])
    ln = LayerNorm(nc, sig, mem, xt, lambda t: d["resid"][t],
                   lambda t, i: ("ev_dve", G(("out", 512 * i, t))),
                   bank_free=lambda b: ("ev_dve", max(g for g in st.by_gid if st.bank_of[g] == b)))

    split = InputSplit(nc, sig, mem, merged[:, 0:2, :])

    steps = []
    order = [(n, q) for n in range(n_units) for q in range(4)]
    i_na = next(n for n, u in enumerate(units) if u.evac[1] == "z_a") * 4
    i_sz = next(n for n, u in enumerate(units) if u.evac[1] == "sg_z") * 4
    i_zb = next(n for n, u in enumerate(units) if u.evac[1] == "z_b") * 4
    i_br = next(n for n, u in enumerate(units) if u.evac[1] == "a") * 4
    extras = {}

    def extra(at_step, *e):
        extras.setdefault(at_step, []).append(e)

    spare = Attention.STEPS - (i_sz - i_na)
    for j in range(Attention.STEPS):
        extra(min(i_na + j, i_sz - 1), "na", j)
    assert spare < 8
    i_rms = 4 * (last_u["gq_kv"] + 1)
    for t in range(NT):
        extra(i_rms + 3 * t, "square", t)
        extra(i_rms + 3 * t + 1, "rms", t)
        extra(i_sz - 4 + t, "vstat", t)
        extra(i_sz + t, "rope", t)
        extra(i_sz + t, "vnorm", t)
        extra(i_sz + t + 1, "rot", t)
    for p in range(4):
        extra(i_sz + 5 + p, "mix", p)
    extra(i_zb, "sg_tanh")
    extra(i_zb + 2, "sg_gate")
    for f in range(NW):
        extra(i_zb + 4 + f, "yct", f)
    extra(i_br, "y_split", "a")
    for j in range(Attention.STEPS):
        extra(i_br + 1 + j, "gq", j)
    n_c = next(n for n, u in enumerate(units) if u.evac[:2] == ("branch", "c")) * 4
    extra(n_c - 3, "y_split", "c")
    extra(4 * last_u["c"] + 4, "y_split", "b")
    assert 4 * last_u["a"] + 3 < n_c - 3
    i_out = next(n for n, u in enumerate(units) if u.evac[1] == "out") * 4
    for fb in range(ND):
        n_b = [n for n, u in enumerate(units) if u.evac[:2] == ("branch", "b")][fb // 4]
        extra(4 * n_b + fb % 4, "m_split", fb)
    extra(i_out - 12, "resid_rows")
    for t in range(NT):
        extra(i_out - 8 + 2 * t, "resid", t)
        extra(4 * n_units - 4 + t, "ln", t)
    steps = [(n, q, extras.get(4 * n + q, [])) for n, q in order]
    assert max(extras) < len(order)

    y_of = {"a": (ya, "na_y"), "c": (yc, None), "b": (yb, "gq_y")}

    def split_y_hi(act, tag):
        y, head = y_of[tag]
        if tag == "a":
            act.wait_ge(*sig.after("sg_y"))
            act.wait_ge(*sig.after("mix", 3))
            act.wait_ge(*sig.after("na_y", HEADS - 1))
        elif tag == "c":
            act.wait_ge(*sig.after("unit_done", last_unit("branch", "a")))
        else:
            act.wait_ge(*sig.after("unit_done", last_unit("branch", "c")))
            act.wait_ge(*sig.after("gq_y", HEADS - 1))
        nc.scalar.activation(yh[:, :, :], y[:, :, :], ACT.Copy).then_inc(*sig.inc("y_hi", tag))

    def last_unit(kind, tag):
        return max(n for n, u in enumerate(units) if u.evac[:2] == (kind, tag))

    def rope(dve, t):
        dve.wait_ge(*sig.after("qk_normed", t))
        if t == 0:
            dve.wait_ge(*sig.after("na_max", HEADS * NT - 1))
        x = qk[:, t, :].rearrange("p (h c two) -> p h c two", c=HD // 2, two=2)
        x0, x1 = x[:, :, :, 0], x[:, :, :, 1]
        c = cos[:, t, :].unsqueeze(1).broadcast_to([P, 10, 32])
        s = sin[:, t, :].unsqueeze(1).broadcast_to([P, 10, 32])
        a = rp[:, 0:320].rearrange("p (h c) -> p h c", c=32)
        b = rp[:, 320:640].rearrange("p (h c) -> p h c", c=32)
        oq = ro[:, 0:WID].rearrange("p (h c two) -> p h c two", c=32, two=2)
        ok = ro[:, WID:].rearrange("p (h r c two) -> p h r c two", r=2, c=32, two=2)
        for part, (f0, f1, op) in enumerate(((c, s, ALU.subtract), (s, c, ALU.add))):
            nc.vector.tensor_tensor(a, x0, f0, ALU.mult)
            nc.vector.tensor_tensor(b, x1, f1, ALU.mult).then_inc(
                *sig.inc("rope_products", t, part))
            dve.wait_ge(*sig.after("rope_products", t, part))
            if t and part == 0:
                dve.wait_ge(*sig.after("rot_transposed", t - 1))
            nc.vector.tensor_tensor(oq[:, :, :, part], a[:, 0:8, :], b[:, 0:8, :], op)
            for rep in range(2):
                ins = nc.vector.tensor_tensor(ok[:, :, rep, :, part], a[:, 8:10, :],
                                              b[:, 8:10, :], op)
            ins.then_inc(*sig.inc("rope_out", t, part))
            dve.wait_ge(*sig.after("rope_out", t, part))
        sig.seen[(sig.phase, "rope_done", t)] = ("rope_out", t, 1)

    with nc.Block() as block:
        @block.sync
        def _(sp):
            for n in range(n_units):
                st.load(sp, n)
            for t in range(NT):
                if t == 0:
                    st.load_next(sp)
                ln.store(sp, t)
            sp.wait_ge(*sig.after("ln_stored", NT - 1))

        @block.gpsimd
        def _(pool):
            for n, q, ex in steps:
                u = units[n]
                if q == 0:
                    st.lo_on_pool(pool, n + 1)
                for e in ex:
                    if e[0] == "square":
                        t = e[1]
                        pool.wait_ge(*sig.after("ev_dve", G(("gq_kv", t))))
                        if t >= 2:
                            pool.wait_ge(*sig.after("mean_square", t - 2))
                        nc.gpsimd.tensor_tensor(sq[:, t % 2, :], qk[:, t, :], qk[:, t, :],
                                                ALU.mult).then_inc(*sig.inc("squared", t))
                    if e[0] == "rms":
                        t = e[1]
                        heads = qk[:, t, :].rearrange("p (h c) -> p h c", c=HD)
                        pool.wait_ge(*sig.after("mean_square", t))
                        nc.gpsimd.tensor_tensor(r, ss, mem.half[:, 0:10], ALU.pow).then_inc(
                            *sig.inc("rms", t))
                        pool.wait_ge(*sig.after("rms", t))
                        nc.gpsimd.tensor_tensor(heads, heads,
                                                r.unsqueeze(2).broadcast_to([P, 10, HD]),
                                                ALU.mult).then_inc(*sig.inc("rms_scaled", t))
                        pool.wait_ge(*sig.after("rms_scaled", t))
                        if t == 0:
                            pool.wait_ge(*sig.after("qk_g"))
                        nc.gpsimd.tensor_tensor(heads, heads, qkg[:, :, :], ALU.mult).then_inc(
                            *sig.inc("qk_normed", t))
                    if e[0] == "vstat":
                        t = e[1]
                        pool.wait_ge(*sig.after("sv_var", t))
                        nc.gpsimd.tensor_tensor(srs[:, t:t + 1], smv[:, t, 1:2], mem.half[:, 0:1],
                                                ALU.pow).then_inc(*sig.inc("sv_rstd", t))
                    if e[0] == "vnorm":
                        t = e[1]
                        if t == 0:
                            pool.wait_ge(*sig.after("sg_g"))
                            pool.wait_ge(*sig.after("sg_beta"))
                        pool.wait_ge(*sig.after("sv_centred", t))
                        nc.gpsimd.tensor_tensor(sv[:, t, :], sv[:, t, :], sgg[:, :],
                                                ALU.mult).then_inc(*sig.inc("sv_scaled", t))
                        pool.wait_ge(*sig.after("sv_scaled", t))
                        nc.gpsimd.tensor_tensor(sv[:, t, :], sv[:, t, :], sgbeta[:, :],
                                                ALU.add).then_inc(*sig.inc("sv_ready", t))
                for gid, b in [(gg, bb) for gg, (uu, bb) in st.by_gid.items() if uu is u]:
                    if completes(u, q, b):
                        emit_common_evac(nc, sig, mem, st, u, b, gid, "pool", pool, ctx)
                for e in ex:
                    if e[0] == "resid_rows":
                        scale_residual(pool, nc, sig, xt, rows, ALPHA_1, bout)
                    if e[0] == "resid":
                        residual_block(pool, nc, sig, xt, rows, e[1])
                    if e[0] == "ln":
                        ln.power(pool, e[1])

        @block.scalar
        def _(act):
            split.split_hi(act)
            one = lambda ap, n: ap.rearrange("o c -> (o c)").partition_broadcast(P)
            act.dma_start(fb_raw, d["f_bias"][bass.ds(layer, 1)].rearrange("o p c -> (o p) c")
                           ).then_inc(*sig.inc("f_bias_raw", by=16))
            act.dma_start(fscale, d["f_scale"]).then_inc(*sig.inc("f_scale", by=16))
            act.dma_start(sgb, d["sg_b"][bass.ds(layer, 1)].rearrange("o p c -> (o p) c")).then_inc(
                *sig.inc("sg_b", by=16))

            def tbias(m):
                cols = 256 if m == 2 else 512
                if m >= 2:
                    tag = ("na_v", "gq_q", "gq_kv", "sg_u", "sg_v", "sg_z")[m - 2]
                    act.wait_ge(*sig.after("ev_dve", G((tag, NT - 1))))
                act.dma_start(mem.tbias[m % 2][:, 0:cols],
                               one(d["t_bias"][bass.ds(layer, 1), m * 512:m * 512 + cols], cols)
                               ).then_inc(*sig.inc(f"tbias_{m % 2}", m, by=16))
                sig.seen[(sig.phase, "tbias", m)] = (f"tbias_{m % 2}", m)

            def na_bias(h):
                if h >= 2:
                    act.wait_ge(*sig.after("na_max", 4 * (h - 2) + 3))
                act.dma_start(nab[:, h % 2, :], d["na_bias"][bass.ds(layer, 1), h].rearrange(
                    "o p c -> (o p) c")).then_inc(*sig.inc(f"na_bias_{h % 2}", h, by=16))
                sig.seen[(sig.phase, "na_bias", h)] = (f"na_bias_{h % 2}", h)

            act.dma_start(qkg[:, :, :], one(d["qk_g"][bass.ds(layer, 1)], 640).rearrange(
                "p (h c) -> p h c", c=HD)).then_inc(*sig.inc("qk_g", by=16))
            for m in range(2):
                tbias(m)
            for h in range(2):
                na_bias(h)
            act.wait_ge(*sig.after("x_lo", ND - 1))
            act.dma_start(mem.cols[:, :], d["ln_cols"][bass.ds(layer, 1)].rearrange(
                "o p c -> (o p) c")).then_inc(*sig.inc("ln_cols", by=16))
            st.hi(act, 1)
            act.wait_ge(*sig.after("f_bias"))
            for n, q, ex in steps:
                u = units[n]
                if q == 0 and n:
                    st.hi(act, n + 1)
                for gid, b in [(gg, bb) for gg, (uu, bb) in st.by_gid.items() if uu is u]:
                    if completes(u, q, b):
                        emit_common_evac(nc, sig, mem, st, u, b, gid, "act", act, ctx)
                for e in ex:
                    if e[0] == "na":
                        na.on_act(act, e[1])
                    if e[0] == "gq":
                        gqa.on_act(act, e[1])
                    if e[0] == "rot":
                        t = e[1]
                        act.wait_ge(*sig.after("rot_transposed", t))
                        if t == 0:
                            act.wait_ge(*sig.after("qk_normed", NT - 1))
                        nc.scalar.activation(gq[:, :, t * P:(t + 1) * P],
                                             mem.bank[4][:, :].rearrange("p (f c) -> p f c", c=P),
                                             ACT.Copy)
                        nc.scalar.activation(gk[:, :, t * P:(t + 1) * P],
                                             mem.bank[5][:, 0:2 * P].rearrange(
                                                 "p (f c) -> p f c", c=P),
                                             ACT.Copy).then_inc(*sig.inc("rot_kept", t))
                    if e == ("sg_tanh",):
                        act.wait_ge(*sig.after("ev_dve", G(("sg_z", NT - 1))))
                        act.wait_ge(*sig.after("na_pv", HEADS - 1))
                        for t in range(NT):
                            nc.scalar.activation(sgt[:, t, :], sz[:, t, :], ACT.Tanh,
                                                 scale=0.5).then_inc(*sig.inc("sg_tanh", t))
                    if e[0] == "yct":
                        f = e[1]
                        act.wait_ge(*sig.after("yct", f))
                        nc.scalar.activation(yc[:, f, :], mem.bank[4 + f][:, :], ACT.Copy).then_inc(
                            *sig.inc("ycf", f))
                    if e[0] == "y_split":
                        split_y_hi(act, e[1])
                    if e[0] == "m_split":
                        fb = e[1]
                        act.wait_ge(*sig.after("merge", ND + fb))
                        nc.scalar.activation(mh[:, fb, :], merged[:, fb, :], ACT.Copy,
                                             scale=0.5).then_inc(*sig.inc("m_hi", fb))
                    if e[0] == "ln":
                        ln.normalise(act, e[1])
                    if e[0] == "na" and e[1] % 4 == 3 and 2 <= (e[1] + 1) // 4 + 1 < HEADS:
                        na_bias((e[1] + 1) // 4 + 1)
                    if e == ("na", Attention.STEPS - 1):
                        act.wait_ge(*sig.after("na_pv", HEADS - 1))
                        act.dma_start(sgg[:, :], one(d["sg_gb"][bass.ds(layer, 1), 0], 512)
                                       ).then_inc(*sig.inc("sg_g", by=16))
                        act.dma_start(sgbeta[:, :], one(d["sg_gb"][bass.ds(layer, 1), 1], 512)
                                       ).then_inc(*sig.inc("sg_beta", by=16))
                        act.dma_start(sgw[:, :, :], d["sg_w"][bass.ds(layer, 1)].rearrange(
                            "o p g c -> (o p) g c")).then_inc(*sig.inc("sg_w", by=16))
                    if e == ("y_split", "c"):
                        act.wait_ge(*sig.after("y_lo", "a"))
                        act.dma_start(bout[:, :], one(d["b_out"][bass.ds(layer, 1)], D)).then_inc(
                            *sig.inc("b_out", by=16))
                    if e == ("y_split", "b"):
                        act.wait_ge(*sig.after("y_lo", "c"))
                        for i, row in enumerate(rows):
                            act.dma_start(row[:, :], one(d["ln_rows"][bass.ds(layer, 1), i], D)
                                           ).then_inc(*sig.inc("residual_rows", by=16))
                        act.wait_ge(*sig.after("gq_y", HEADS - 1))
                        act.dma_start(xt[:, :, :], d["resid"].rearrange("t p c -> p t c")).then_inc(
                            *sig.inc("x_t_loaded", by=16))
                tags = ("na_v", "gq_q", "gq_kv", "sg_u", "sg_v", "sg_z")
                if u.evac[1] in tags and q == 3 and u.k0 + u.nk == ND:
                    m = tags.index(u.evac[1]) + 2
                    if m < len(tags):
                        tbias(m)
            act.wait_ge(*sig.after("ln_cols"))

        @block.vector
        def _(dve):
            split.split_lo(dve)
            st.lo(dve, 1)
            dve.wait_ge(*sig.after("f_bias_raw"))
            dve.wait_ge(*sig.after("f_scale"))
            nc.vector.tensor_tensor(fb_, fb_raw, fscale, ALU.mult).then_inc(*sig.inc("f_bias"))
            for n, q, ex in steps:
                u = units[n]
                if q == 0 and n:
                    st.lo(dve, n + 1)
                for gid, b in [(gg, bb) for gg, (uu, bb) in st.by_gid.items() if uu is u]:
                    if completes(u, q, b):
                        if u.evac[1] == "gq_kv":
                            dve.wait_ge(*sig.after("group", gid))
                            if b == 0:
                                dve.wait_ge(*sig.after("tbias", 2))
                            nc.vector.tensor_tensor(qk[:, b, WID:WID + P], st.bank(gid)[:, 0:P],
                                                    mem.tbias[0][:, 0:P], ALU.add)
                            nc.vector.tensor_tensor(gv[:, b, :], st.bank(gid)[:, P:2 * P],
                                                    mem.tbias[0][:, P:2 * P], ALU.add).then_inc(
                                *sig.inc("ev_dve", gid))
                        else:
                            emit_common_evac(nc, sig, mem, st, u, b, gid, "dve", dve, ctx)
                        if u.evac[0] == "residual":
                            ln.half(dve, b, u.evac[2] // 512)
                for e in ex:
                    if e[0] == "na":
                        na.on_dve(dve, e[1])
                    if e[0] == "gq":
                        gqa.on_dve(dve, e[1])
                    if e[0] == "rms":
                        t = e[1]
                        dve.wait_ge(*sig.after("squared", t))
                        if t:
                            dve.wait_ge(*sig.after("rms", t - 1))
                        nc.vector.tensor_reduce(
                            ss, sq[:, t % 2, :].rearrange("p (h c) -> p h c", c=HD), AX.X,
                            ALU.add).then_inc(*sig.inc("sum_square", t))
                        dve.wait_ge(*sig.after("sum_square", t))
                        nc.vector.tensor_scalar(ss, ss, 1.0 / HD, RMS_EPS, ALU.mult,
                                                ALU.add).then_inc(*sig.inc("mean_square", t))
                    if e[0] == "rope":
                        rope(dve, e[1])
                    if e[0] == "vstat":
                        t = e[1]
                        dve.wait_ge(*sig.after("ev_dve", G(("sg_v", t))))
                        nc.vector.bn_stats(sst[:, t, :], sv[:, t, :]).then_inc(
                            *sig.inc("sv_stats", t))
                        dve.wait_ge(*sig.after("sv_stats", t))
                        nc.vector.bn_aggr(smv[:, t, :], sst[:, t, :]).then_inc(*sig.inc("sv_mv", t))
                        dve.wait_ge(*sig.after("sv_mv", t))
                        nc.vector.tensor_scalar(smv[:, t, 1:2], smv[:, t, 1:2], LN_EPS, None,
                                                ALU.add).then_inc(*sig.inc("sv_var", t))
                    if e[0] == "vnorm":
                        t = e[1]
                        dve.wait_ge(*sig.after("sv_rstd", t))
                        nc.vector.tensor_scalar(sv[:, t, :], sv[:, t, :], smv[:, t, 0:1],
                                                srs[:, t:t + 1], ALU.subtract, ALU.mult).then_inc(
                            *sig.inc("sv_centred", t))
                    if e[0] == "mix":
                        p = e[1]
                        dve.wait_ge(*sig.after("mix", p))
                        if p == 0:
                            dve.wait_ge(*sig.after("sg_b"))
                            dve.wait_ge(*sig.after("ev_dve", G(("sg_u", NT - 1))))
                        for i in range(2):
                            gg = 2 * p + i
                            cols = su[:, :, gg * HD:(gg + 1) * HD]
                            ins = nc.vector.scalar_tensor_tensor(
                                cols, mem.bank[4 + p][:, i * 256:(i + 1) * 256].rearrange(
                                    "p (c d) -> p c d", d=HD), sgb[:, gg:gg + 1], cols,
                                ALU.add, ALU.mult)
                        ins.then_inc(*sig.inc("mixed", p))
                    if e == ("sg_gate",):
                        dve.wait_ge(*sig.after("mixed", 3))
                        for t in range(NT):
                            dve.wait_ge(*sig.after("sg_tanh", t))
                            nc.vector.scalar_tensor_tensor(
                                sz[:, t, :], sgt[:, t, :], 1.0, sz[:, t, :], ALU.add,
                                ALU.mult).then_inc(*sig.inc("sg_silu", t))
                            dve.wait_ge(*sig.after("sg_silu", t))
                            ins = nc.vector.scalar_tensor_tensor(
                                su[:, t, :], su[:, t, :], 0.5, sz[:, t, :], ALU.mult, ALU.mult)
                        ins.then_inc(*sig.inc("sg_y"))
                    if e[0] == "y_split":
                        y, _ = y_of[e[1]]
                        dve.wait_ge(*sig.after("y_hi", e[1]))
                        nc.vector.tensor_tensor(yl[:, :, :], y[:, :, :], yh[:, :, :].bitcast(F32),
                                                ALU.subtract).then_inc(*sig.inc("y_lo", e[1]))
                    if e[0] == "m_split":
                        fb = e[1]
                        dve.wait_ge(*sig.after("m_hi", fb))
                        nc.vector.scalar_tensor_tensor(
                            ml[:, fb, :], merged[:, fb, :], 0.5, mh[:, fb, :].bitcast(F32), ALU.mult,
                            ALU.subtract).then_inc(*sig.inc("m_lo", fb))
                    if e[0] == "ln":
                        ln.moments(dve, e[1])

        @block.tensor
        def _(pe):
            for n, q, ex in steps:
                st.multiply(pe, n, q)
                for e in ex:
                    if e[0] == "na":
                        na.on_pe(pe, e[1])
                    if e[0] == "gq":
                        gqa.on_pe(pe, e[1])
                    if e[0] == "rot":
                        t = e[1]
                        pe.wait_ge(*sig.after("rope_done", t))
                        if t:
                            pe.wait_ge(*sig.after("rot_kept", t - 1))
                        else:
                            pe.wait_ge(*sig.after("na_exp", HEADS * NT - 1))
                        for f in range(6):
                            last = nc.tensor.transpose(
                                mem.bank[4 + f // 4][:, (f % 4) * P:(f % 4 + 1) * P],
                                ro[:, f * P:(f + 1) * P], mem.ident[:, :])
                        last.then_inc(*sig.inc("rot_transposed", t))
                    if e[0] == "mix":
                        p = e[1]
                        if p == 0:
                            pe.wait_ge(*sig.after("sg_w"))
                            pe.wait_ge(*sig.after("sv_ready", NT - 1))
                            pe.wait_ge(*sig.after("rot_kept", NT - 1))
                            pe.wait_ge(*sig.after("na_y", HEADS - 1))
                            pe.wait_ge(*sig.after("na_pt", HEADS * NT - 1))
                        for i in range(2):
                            gg = 2 * p + i
                            last = nc.tensor.matmul(
                                mem.bank[4 + p][:, i * 256:(i + 1) * 256].rearrange(
                                    "p (c d) -> p c d", d=HD), sgw[:, gg, :],
                                sv[:, :, gg * HD:(gg + 1) * HD], start=True, stop=True)
                        last.then_inc(*sig.inc("mix", p))
                    if e[0] == "yct":
                        f = e[1]
                        pe.wait_ge(*sig.after("sg_y"))
                        pe.wait_ge(*sig.after("mixed", f))
                        for t in range(NT):
                            last = nc.tensor.transpose(mem.bank[4 + f][:, t * P:(t + 1) * P],
                                                       su[:, t, f * P:(f + 1) * P], mem.ident[:, :])
                        last.then_inc(*sig.inc("yct", f))
            ln.transpose(pe)


def completes(u, q, b):
    if u.kind == "F" and u.cols == 2 * P:
        return q == 2 * b + 1
    if u.kind == "F" and u.cols < P:
        return q == 3
    return q == b and u.k0 + u.nk == u.of


C_F = 3 * WID
C_Z = C_F + HEADS
C_XBC = C_Z + WID
NXBC = 6
C_DT = C_XBC + NXBC * P
C_U = C_DT + HEADS
C_GATE = C_U + WID
S5_TILES = 16
S5_IT = 16
S5_LAG = 4
TWO_PI_PARTS = (6.28125, 0.0019350051879882812, 3.019915981956753e-07)
ROUND = 12582912.0
PI_BELOW = 3.1415925
D_FF = 2816
NF2 = D_FF // P
GELU_A, GELU_B = 0.044715, 0.7978845608028654


def mixer_units():
    units, what = [], []

    def f_blocks(evac, tag, col, nblocks, blk0=0):
        for i in range(0, nblocks, 2):
            units.append(Unit("F", "x", ND, 2 * P, (evac, tag, blk0 + i)))
            what.append(("in", 0, ND, col + i * P, 2 * P))

    def t_cols(evac, tag, col, section, src="x", w="in"):
        for half in range(2):
            units.append(Unit("T", src, 4, 512, (evac, tag, section), k0=4 * half, of=ND))
            what.append((w, 4 * half, 4, col, 512))

    units.append(Unit("F", "x", ND, 16, ("few", "fdt", 0)))
    what.append(("fdt", 0, ND, 0, 16))
    f_blocks("plain", "fq", 0, NW)
    f_blocks("plain", "fk", WID, NW)
    t_cols("copy_t", "fv", 2 * WID, 0)
    t_cols("copy_t", "z", C_Z, 0)
    f_blocks("plain", "xbc", C_XBC, NXBC)
    f_blocks("plain", "u", C_U, NW)
    for r, tag in enumerate("abc"):
        for half in range(2):
            f_blocks("gate", tag, C_GATE + r * D + 4 * half * P, 4, 4 * half)
            if tag == "c" and half == 0:
                units.append(Unit("F", "y", NW, 512, ("glu", "glu", 0)))
                what.append(("glu", 0, NW, 0, 512))
            units.append(Unit("F", "y", NW, 512, ("branch", tag, 4 * half)))
            what.append(("br_" + tag, 0, NW, 512 * half, 512))
    for c in (0, 512):
        t_cols("residual", "out", c, c, src="m", w="out")
    return units, what


def mixer_phase(nc, sig, mem, d):
    units, _ = mixer_units()
    n_units = len(units)
    at = lambda name, *a: mem.at("mx_" + name, *a)
    fq = at("fox_q", 0, [P, NW, SEQ])
    fk = at("fox_k", 8, [P, NW, SEQ])
    fv = at("fox_v", 16, [P, NT, WID])
    yh = at("y_hi", 0, [P, NW, SEQ], F32R)
    yl = at("y_lo", 8, [P, NW, SEQ], F32R)
    xh = at("ssd_x", 16, [P, NT, WID])
    ct = at("s5_c", 16, [P, 2, S5_TILES, 32])
    bbt = at("s5_bt", 20, [P, 2, 4, P])
    rows = at("gamma", 16, [P, D]), at("beta", 20, [P, D])
    minus_cum = at("minus_cum", 24, [P, HEADS, SEQ])
    merged = at("merged", 24, [P, ND, SEQ])
    z = at("z", 40, [P, NT, WID])
    yb = at("y_b", 40, [P, NW, SEQ])
    yc = at("y_c", 40, [P, NW, SEQ])
    ones = at("ones", 48, [P, P])
    probs = at("probs", 48, [P, 3, SEQ])
    pt = at("probs_t", 54, [P, 2, NT, SEQ])
    xdt = at("ssd_xdt", 48, [P, NT, WID])
    states = at("ssd_states", 56, [P, 3, WID])
    xdd = at("ssd_x_decayed", 62, [P, WID])
    bt = at("ssd_b_t", 64, [P, NT, P])
    cbm = at("ssd_cb", 66, [P, 2, SEQ])
    norm_w = at("ssd_norm_w", 70, [P, WID])
    z_tanh = at("z_tanh", 62, [P, 2, WID])
    tab = at("s5_cos_sin", 48, [P, 2, 2, SEQ])
    ctab, stab = tab[:, :, 0, :], tab[:, :, 1, :]
    powers = mem.rope.rearrange("p (j r k) -> p j r k", r=2, k=S5_TILES)
    mtab = at("s5_mag", 56, [P, 2, SEQ])
    w_s5 = at("s5_w", 60, [P, 2, 2, SEQ])
    p_s5 = at("s5_p", 68, [P, 2, 4, SEQ])
    acc = at("conv_acc", 70, [P, SEQ])
    xbc = at("xbc", 72, [P, NXBC, SEQ + 3])
    yt = at("ssd_y", 72, [P, NT, WID])
    u_ = at("s5_u", 84.5, [P, NW, SEQ])
    tri = at("tri", 92.5, [P, P])
    ya = at("y_a", 93, [P, NW, SEQ])
    seg = at("ssd_seg", 93, [P, 2, SEQ])
    ubd = at("s5_u_blocks", 93, [P, 2, SEQ])
    tmp = at("branch_tmp", 97, [P, 2, SEQ])
    g = at("gates", 101, [P, GRING, SEQ])
    s5p = at("s5_params", 109, [P, 16, 16])
    mh = at("m_hi", 44, [P, ND, SEQ], F32R)
    ml = at("m_lo", 60, [P, ND, SEQ], F32R)
    xt = at("x_t", 76, [P, NT, D])
    sm = lambda a, b: mem.small[:, a:b]
    fd = sm(104, 168).rearrange("p (t c) -> p t c", c=16)
    e_ = sm(168, 232).rearrange("p (t c) -> p t c", c=16)
    l_ = sm(232, 296).rearrange("p (t c) -> p t c", c=16)
    w_ = sm(296, 360).rearrange("p (t c) -> p t c", c=16)
    cums = sm(360, 424).rearrange("p (t c) -> p t c", c=16)
    tot = sm(424, 456).rearrange("p (t h) -> p t h", h=8)
    dte = sm(456, 488).rearrange("p (t h) -> p t h", h=8)
    r8 = sm(488, 496)
    dskip = sm(496, 504)
    a_neg = sm(504, 512)
    bias16 = mem.small2[:, 0:16]
    cw = mem.small2[:, 16:46].rearrange("p (f k) -> p f k", k=5)
    s5d = mem.small2[:, 46:50]
    glub = mem.small2[:, 50:54]
    dout = mem.small2[:, 54:86].rearrange("p (t h) -> p t h", h=8)
    ncum = mem.small2[:, 86:118].rearrange("p (t h) -> p t h", h=8)
    pre = mem.small2[:, 118:150].rearrange("p (t h) -> p t h", h=8)
    lf = mem.small2[:, 150:182].rearrange("p (t h) -> p t h", h=8)
    adt = mem.small2[:, 182:214].rearrange("p (t h) -> p t h", h=8)
    gb = mem.small2[:, 214:238]
    nacs = mem.small2[:, 238:270].rearrange("p (t h) -> p t h", h=8)
    carry = mem.small2[:, 270:302].rearrange("p (k a i) -> p k a i", k=4, i=4)
    t4 = mem.small2[:, 302:334]
    qmask = mem.small2[:, 334:338]
    ones4 = mem.small2[:, 338:342]
    cum_f = at("row_sums", 50, [16, SEQ])
    fd_rows = at("fdt_rows", 52, [16, SEQ])

    w_dram = lambda n: d["w2"][n]

    def ready(u):
        if u.src == "y":
            return [("y_lo", "gy" if u.evac[0] == "glu" else u.evac[1])]
        if u.src == "m":
            return [("m_lo", 4 * (u.k0 // 4) + 3)]
        return []

    n_glu = next(n for n, u in enumerate(units) if u.evac[0] == "glu")
    n_s5 = next(n for n, u in enumerate(units) if u.evac[:2] == ("gate", "b"))
    for u in units[n_s5:n_glu]:
        u.banks = 3
    st = Stream(nc, sig, mem, units, w_dram, {"x": (mem.xh, mem.xl), "y": (yh, yl), "m": (mh, ml)},
                ready, nxt=lambda j: d["w_first"][LAYERS + 1][j])
    tags = [u.evac[:2] for u in units]
    st.pool_units = range(tags.index(("copy_t", "fv")) + 1, tags.index(("branch", "a")) + 1)
    last_in_3 = max(g for g, (u, _) in st.by_gid.items() if st.bank_of[g] == 3 and u.n_ < n_s5)
    gid_of = {}
    for gid, (u, b) in st.by_gid.items():
        gid_of[(u.evac[1], u.evac[2] + b if u.kind == "F" else b)] = gid
        if u.evac[0] == "residual":
            gid_of[("out", u.evac[2], b)] = gid
    G = gid_of.get
    first_u = {}
    for n, u in enumerate(units):
        first_u.setdefault(u.evac[:2], n)
    last_u = {u.evac[:2]: n for n, u in enumerate(units)}

    def before(tag):
        return {"merged": [("a_y", HEADS - 1)]}.get(tag, [])

    plain = {"fq": fq, "fk": fk, "u": u_}
    ctx = dict(g=g, merged=merged, tmp=tmp, xt=xt, before=before, **gate_plan(st))
    ctx["scaled"] = lambda tag, b: (xbc[:, b, 3:SEQ + 3] if tag == "xbc" else plain[tag][:, b, :],
                                    None, SM if tag == "fq" else 1.0)
    ctx["half_bias"] = lambda tag, b: gb[:, "abc".index(tag) * ND + b:"abc".index(tag) * ND + b + 1]
    ctx["t_dst"] = lambda tag, t: {"fdt": fd[:, t, :], "fv": fv[:, t, :], "z": z[:, t, :]}[tag]

    fox = Attention(
        nc, sig, mem, "a",
        q=lambda h, i: fq[(h % 2) * HD:(h % 2) * HD + HD, h // 2, i * P:(i + 1) * P],
        k=lambda h: fk[(h % 2) * HD:(h % 2) * HD + HD, h // 2, :],
        v=lambda h, kb: fv[:, kb, h * HD:(h + 1) * HD], y=ya, causal=True,
        bias=lambda h, i: (minus_cum[:, h, :], ("minus_cum", h)),
        probs=probs, pt=pt, rows=lambda h, i: ncum[:, i, h:h + 1],
        base=[("cums_kept",)],
        needs=lambda h: [("ev_act", G(("fk", h // 2))), ("ev_dve", G(("fv", NT - 1)))])
    ln = LayerNorm(nc, sig, mem, xt, lambda t: d["resid"][t],
                   lambda t, i: ("ev_dve", G(("out", 512 * i, t))),
                   bank_free=lambda b: ("ev_dve", max(g for g in st.by_gid if st.bank_of[g] == b)))

    split = InputSplit(nc, sig, mem, merged[:, 0:2, :])
    extras = {}

    def extra(at_step, *e):
        extras.setdefault(at_step, []).append(e)

    extra(4 * first_u[("plain", "fq")], "setup")
    i_z = 4 * first_u[("copy_t", "z")]
    i_a = 4 * first_u[("gate", "a")]
    i_ya = 4 * first_u[("branch", "a")]
    for j in range(Attention.STEPS):
        extra(min(i_z + j, i_ya - 1), "fox", j)
    x0 = 4 * first_u[("plain", "xbc")]
    for f in range(NXBC):
        extra(x0 + 4 + 3 * f, "conv", f)
        extra(x0 + 5 + 3 * f, "conv_silu", f)
    extra(i_ya - 1, "y_split", "a")
    s = i_ya
    for f in range(5):
        extra(s + 1 + f // 2, "x_t", f)
    extra(s + 3, "cb")
    extra(s + 3, "xdt")
    for c in range(3):
        extra(s + 4 + c, "state", c)
    for c in range(NT):
        extra(s + 6 + c, "z_silu", c)
    for h in range(HEADS):
        extra(s + 6 + h, "head_decay", h)
        extra(s + 7 + h, "head", h)
        extra(s + 8 + h, "head_out", h)
        extra(s + 9 + h, "ssd_gate", h)
    extra(s + 17, "ssd_out")
    for f in range(NW):
        extra(s + 17, "ybt", f)
    extra(4 * first_u[("branch", "b")] - 2, "y_split", "b")
    s5_at = s + 18
    extra(s + 16, "s5_load")
    extra(s + 17, "s5_bb")
    extra(s5_at, "s5_b")
    n_it = S5_IT
    s5_last = 4 * first_u[("glu", "glu")] - 2
    s5_end = s5_last - 4
    s5_slots = S5_IT + S5_LAG
    for slot in range(s5_slots):
        at_step = s5_at + 1 + (s5_end - s5_at - 1) * slot // s5_slots
        if slot >= 4 and slot % 4 == 2 and slot < S5_IT - 4:
            extra(at_step, "s5_tables", slot // 4 + 1)
        extra(at_step, "s5", slot)
    extra(s5_end, "gelu")
    extra(s5_last, "y_split", "gy")
    extra(4 * first_u[("branch", "c")] - 1, "y_split", "c")
    i_out = 4 * first_u[("residual", "out")]
    for fb in range(ND):
        n_b = [n for n, u in enumerate(units) if u.evac[:2] == ("branch", "c")][fb // 4]
        extra(4 * n_b + fb % 4, "m_split", fb)
    extra(i_out - 9, "resid_rows")
    for t in range(NT):
        extra(i_out - 8 + 2 * t, "resid", t)
        extra(4 * n_units - 4 + t, "ln", t)
    steps = [(n, q, extras.get(4 * n + q, [])) for n in range(n_units) for q in range(4)]
    assert max(extras) < len(steps)

    def groups_done(u, q):
        return [(gid, b) for b, gid in enumerate(u.gids) if completes(u, q, b)]

    def s5_in_slot(slot):
        return slot if 0 <= slot < S5_IT else None

    def s5_it(k):
        return k // NT, k % NT

    (A_RE, A_IM, L_STEP, MAG, TH, CO, SI, K_RE, K_IM, T0, T1, T2, T3, MR, MI, T4_) = range(16)
    row = lambda i: s5p[:, i, :]

    class Chain:

        def __init__(self, eng, name):
            self.eng, self.name, self.n = eng, name, 0

        def __call__(self, ins):
            key = self.n
            self.n += 1
            ins.then_inc(*sig.inc(self.name, key))
            self.eng.wait_ge(*sig.after(self.name, key))

    V, A, Q = nc.vector, nc.scalar, nc.gpsimd
    tt, ts = V.tensor_tensor, V.tensor_scalar

    def act_extra(act, e):
        if e[0] == "setup":
            act.wait_ge(*sig.after("fd_abs"))
            A.activation(e_, e_, ACT.Exp, scale=-1.0).then_inc(*sig.inc("fd_exp"))
            act.wait_ge(*sig.after("a_log"))
            A.activation(a_neg, a_neg, ACT.Exp).then_inc(*sig.inc("a_exp"))
            act.wait_ge(*sig.after("s5in"))
            A.activation(row(L_STEP), row(L_STEP), ACT.Exp).then_inc(*sig.inc("s5_step"))
            act.wait_ge(*sig.after("s5_lam"))
            A.activation(row(MAG), row(MAG), ACT.Exp).then_inc(*sig.inc("s5_mag"))
            act.wait_ge(*sig.after("fd_one_plus"))
            A.activation(l_, w_, ACT.Ln).then_inc(*sig.inc("fd_ln"))
            act.wait_ge(*sig.after("s5_angle"))
            A.activation(row(SI), row(TH), ACT.Sin).then_inc(*sig.inc("s5_sin"))
            A.activation(row(CO), row(TH), ACT.Sin, scale=0.5).then_inc(*sig.inc("s5_sin_half"))
            act.wait_ge(*sig.after("cum_transposed"))
            A.activation(cum_f[:, :], mem.bank[5][0:16, :], ACT.Copy).then_inc(
                *sig.inc("cum_rows"))
            act.wait_ge(*sig.after("decay_arg"))
            A.activation(dte, dte, ACT.Exp)
            A.activation(dout, dout, ACT.Exp)
            A.activation(tot, tot, ACT.Exp).then_inc(*sig.inc("decays"))
        if e[0] == "fox":
            fox.on_act(act, e[1])
        if e[0] == "conv":
            f = e[1]
            act.wait_ge(*sig.after("ev_act", G(("xbc", f))))
            act.wait_ge(*sig.after("params_halved"))
            if f:
                act.wait_ge(*sig.after("conv", f - 1))
            A.activation(acc[:, :], xbc[:, f, 3:SEQ + 3], ACT.Identity, bias=cw[:, f, 4:5],
                         scale=cw[:, f, 3:4]).then_inc(*sig.inc("conv_acc", f))
        if e[0] == "conv_silu":
            f = e[1]
            act.wait_ge(*sig.after("conv_taps", f))
            A.activation(xbc[:, f, 3:SEQ + 3], acc[:, :], ACT.Tanh).then_inc(
                *sig.inc("conv_tanh", f))
        if e[0] == "y_split":
            tag = e[1]
            if tag == "a":
                act.wait_ge(*sig.after("a_y", HEADS - 1))
                y = ya
            if tag == "b":
                act.wait_ge(*sig.after("unit_done", last_u[("branch", "a")]))
                y = yb
            if tag == "gy":
                act.wait_ge(*sig.after("unit_done", last_u[("branch", "b")]))
                act.wait_ge(*sig.after("gelu"))
                y = yc
            if tag == "c":
                act.wait_ge(*sig.after("unit_done", first_u[("glu", "glu")]))
                act.wait_ge(*sig.after("glu_used", NW - 1))
                y = yc
            A.activation(yh[:, :, :], y[:, :, :], ACT.Copy,
                         scale=0.5 if tag in ("gy", "c") else 1.0).then_inc(
                *sig.inc("y_hi", tag))
            if tag == "b":
                act.wait_ge(*sig.after("ssd_skip", HEADS - 1))
            if tag == "c":
                act.wait_ge(*sig.after("s5_done"))
                for i, r_ in enumerate(rows):
                    act.dma_start(r_[:, :], d["ln_rows"][LAYERS][i].partition_broadcast(P)
                                  ).then_inc(*sig.inc("residual_rows", by=16))
        if e[0] == "x_t":
            f = e[1]
            act.wait_ge(*sig.after("x_t", f))
            dst = bt[:, :, :] if f == 4 else xh[:, :, f * P:(f + 1) * P]
            A.activation(dst, mem.bank[4 + f % 4][:, :].rearrange("p (c k) -> p c k", k=P),
                         ACT.Copy).then_inc(*sig.inc("x_t_kept", f))
            if f == 4:
                act.wait_ge(*sig.after("conv", NXBC - 1))
                act.dma_start(norm_w[:, :], d["ssd_norm_w"].partition_broadcast(P)).then_inc(
                    *sig.inc("norm_w", by=16))
                act.wait_ge(*sig.after("y_lo", "a"))
                for h in range(2):
                    seg_load(act, h)
        if e[0] == "head_decay":
            h = e[1]
            act.wait_ge(*sig.after("seg", h))
            A.activation(seg[:, h % 2, :], seg[:, h % 2, :], ACT.Exp).then_inc(
                *sig.inc("seg_exp", h))
        if e[0] == "head":
            h = e[1]
            act.wait_ge(*sig.after("ssd_products", h))
            A.activation(yt[:, :, h * HD:(h + 1) * HD],
                         mem.bank[4 + h % 2][:, 0:256].rearrange("p (c k) -> p c k", k=HD),
                         ACT.Copy).then_inc(*sig.inc("ssd_diag", h))
            if h + 2 < HEADS:
                seg_load(act, h + 2)
        if e[0] == "z_silu":
            c = e[1]
            if c == 0:
                act.wait_ge(*sig.after("state_product", 2))
                act.wait_ge(*sig.after("ev_dve", G(("z", NT - 1))))
            if c >= 2:
                act.wait_ge(*sig.after("z_silu", c - 2))
            A.activation(z_tanh[:, c % 2, :], z[:, c, :], ACT.Tanh, scale=0.5).then_inc(
                *sig.inc("z_tanh", c))
        if e[0] == "ybt":
            f = e[1]
            act.wait_ge(*sig.after("ybt", f))
            A.activation(yb[:, f, :], mem.bank[4 + f][:, :], ACT.Copy).then_inc(
                *sig.inc("ybf", f))
        if e[0] == "s5_load":
            act.wait_ge(*sig.after("ssd_skip", HEADS - 1))
            for i in range(2):
                act.dma_start(ct[:, i, :, :], d["s5_c"][i].rearrange("p (t c) -> p t c", c=32)
                              ).then_inc(*sig.inc("s5_c", i, by=16))
                act.dma_start(w_s5[:, 0, i, :], d["s5_b"][i]).then_inc(
                    *sig.inc("s5_b", i, by=16))
        if e[0] == "s5_b":
            act.wait_ge(*sig.after("s5_b_transposed"))
            for i in range(2):
                A.activation(bbt[:, i, :, :],
                             mem.bank[4 + i][:, :].rearrange("p (a c) -> p a c", c=P),
                             ACT.Copy).then_inc(*sig.inc("s5_b_kept", i))
        if e[0] == "gelu":
            act.wait_ge(*sig.after("gelu_arg"))
            A.activation(p_s5[:, 0, :, :], p_s5[:, 0, :, :], ACT.Tanh, scale=GELU_B).then_inc(
                *sig.inc("gelu_tanh"))
        if e[0] == "m_split":
            fb = e[1]
            act.wait_ge(*sig.after("merge", ND + fb))
            if fb == 0:
                act.wait_ge(*sig.after("y_lo", "c"))
            A.activation(mh[:, fb, :], merged[:, fb, :], ACT.Copy, scale=0.5).then_inc(
                *sig.inc("m_hi", fb))
            if fb == 3:
                act.dma_start(xt[:, :, :], d["resid"].rearrange("t p c -> p t c")).then_inc(
                    *sig.inc("x_t_loaded", by=16))
        if e[0] == "ln":
            ln.normalise(act, e[1])

    def seg_load(act, h):
        if h >= 2:
            act.wait_ge(*sig.after("ssd_products", h - 2))
        act.dma_start(seg[:, h % 2, :], d["rows"][8 + h].partition_broadcast(P)).then_inc(
            *sig.inc(f"seg_loaded_{h % 2}", h, by=16))
        sig.seen[(sig.phase, "seg_loaded", h)] = (f"seg_loaded_{h % 2}", h)

    def pool_extra(pool, e, pch):
        bh = lambda ap: ap.unsqueeze(2).broadcast_to([P, HEADS, HD])
        hv = lambda ap: ap.rearrange("p (h c) -> p h c", c=HD)
        if e[0] == "xdt":
            for f in range(NW):
                pool.wait_ge(*sig.after("x_t_kept", f))
            pool.wait_ge(*sig.after("a_pv", HEADS - 1))
            pool.wait_ge(*sig.after("decays"))
            for c in range(NT):
                ins = Q.tensor_tensor(hv(xdt[:, c, :]), hv(xh[:, c, :]), bh(fd[:, c, 8:16]),
                                      ALU.mult)
            ins.then_inc(*sig.inc("xdt"))
            pool.wait_ge(*sig.after("xdt"))
            pool.wait_ge(*sig.after("dskip"))
            for c in range(NT):
                ins = Q.tensor_tensor(hv(xh[:, c, :]), hv(xh[:, c, :]), bh(dskip), ALU.mult)
            ins.then_inc(*sig.inc("x_skip"))
        if e[0] == "state":
            c = e[1]
            pool.wait_ge(*sig.after("xdt"))
            if c:
                pool.wait_ge(*sig.after("state_product", c - 1))
            Q.tensor_tensor(hv(xdd[:, :]), hv(xdt[:, c, :]), bh(dte[:, c, :]),
                            ALU.mult).then_inc(*sig.inc("xdd", c))
            if c:
                pool.wait_ge(*sig.after("state", c - 1))
                Q.tensor_tensor(hv(states[:, c, :]), hv(states[:, c - 1, :]), bh(tot[:, c, :]),
                                ALU.mult).then_inc(*sig.inc("state_decayed", c))
        if e[0] == "head_decay":
            h = e[1]
            pool.wait_ge(*sig.after("seg_exp", h))
            pool.wait_ge(*sig.after("cb_masked", h // 4))
            Q.tensor_tensor(seg[:, h % 2, :], seg[:, h % 2, :], cbm[:, h // 4, :],
                            ALU.mult).then_inc(*sig.inc("ssd_m", h))
        if e[0] == "head_out":
            h = e[1]
            hs = slice(h * HD, (h + 1) * HD)
            if h == 0:
                pool.wait_ge(*sig.after("x_skip"))
                pool.wait_ge(*sig.after("norm_w"))
            pool.wait_ge(*sig.after("ssd_head", h))
            Q.tensor_tensor(yt[:, :, hs], yt[:, :, hs], xh[:, :, hs], ALU.add).then_inc(
                *sig.inc("ssd_skip", h))
        if e[0] == "ssd_gate":
            h = e[1]
            hs = slice(h * HD, (h + 1) * HD)
            pool.wait_ge(*sig.after("ssd_gated", h))
            pool.wait_ge(*sig.after("ssd_products", h))
            Q.tensor_tensor(xdt[:, :, hs], yt[:, :, hs], yt[:, :, hs], ALU.mult).then_inc(
                *sig.inc("ssd_square", h))
            pool.wait_ge(*sig.after("ssd_square", h))
            Q.tensor_tensor(yt[:, :, hs], yt[:, :, hs],
                            norm_w[:, hs].unsqueeze(1).broadcast_to([P, NT, HD]),
                            ALU.mult).then_inc(*sig.inc("ssd_weighted", h))
        if e[0] == "ssd_out":
            pool.wait_ge(*sig.after("ssd_ms"))
            Q.tensor_tensor(r8, r8, mem.half[:, 0:8], ALU.pow).then_inc(*sig.inc("ssd_rms"))
        if e[0] == "s5_b":
            s5_tables(pool, Q, 1, pch)
        if e[0] == "s5":
            slot = e[1]
            if slot == 0:
                pool.wait_ge(*sig.after("ssd_products", HEADS - 1))
                pool.wait_ge(*sig.after("s5_q"))
                pool.wait_ge(*sig.after("ev_act", G(("u", NW - 1))))
                s5_inputs(pool, 0)
            k = s5_in_slot(slot + 1)
            if k is not None:
                s5_inputs(pool, k)
            k = s5_in_slot(slot - 1)
            if k is not None:
                pool.wait_ge(*sig.after("s5_products", k))
                w = w_s5[:, k % 2, :, :]
                Q.tensor_tensor(w[:, 0, :], w[:, 0, :], mem.tbias[0][:, :], ALU.add)
                Q.tensor_tensor(w[:, 1, :], w[:, 1, :], mem.tbias[1][:, :],
                                ALU.subtract).then_inc(*sig.inc("s5_rotated", k))
            m = s5_in_slot(slot - 2)
            if m is not None:
                a, c = s5_it(m)
                pool.wait_ge(*sig.after("s5_scan", m, 1))
                if m >= 2:
                    pool.wait_ge(*sig.after("s5_out", m - 2))
                Q.tensor_tensor(p_s5[:, m % 2, 2, :], w_s5[:, m % 2, 0, :], stab[:, a % 2, :],
                                ALU.mult)
                Q.tensor_tensor(p_s5[:, m % 2, 3, :], w_s5[:, m % 2, 1, :], ctab[:, a % 2, :],
                                ALU.mult).then_inc(*sig.inc("s5_back_im", m))
        if e[0] == "gelu":
            pool.wait_ge(*sig.after("s5_y", n_it - 1))
            Q.tensor_tensor(p_s5[:, 0, :, :], yc[:, :, :], yc[:, :, :], ALU.mult).then_inc(
                *sig.inc("gelu_square"))
        if e[0] == "ln":
            ln.power(pool, e[1])
        if e[0] == "resid_rows":
            scale_residual(pool, nc, sig, xt, rows, ALPHA_2)
        if e[0] == "resid":
            residual_block(pool, nc, sig, xt, rows, e[1])

    def s5_inputs(pool, k):
        a, c = s5_it(k)
        if k >= 2:
            pool.wait_ge(*sig.after("s5_bu", k - 2))
        Q.tensor_tensor(ubd[:, k % 2, :].rearrange("p (q t) -> p q t", t=P),
                        u_[:, a, c * P:(c + 1) * P].unsqueeze(1).broadcast_to([P, 4, P]),
                        qmask.unsqueeze(2).broadcast_to([P, 4, P]), ALU.mult).then_inc(
            *sig.inc("s5_u", k))

    def s5_tables(eng, on, a, ch):
        tiles = slice(4 * a, 4 * a + 4)
        qtt = on.tensor_tensor
        by_tile = lambda ap: ap.rearrange("p (k t) -> p k t", t=P)
        cv, sv, mv = (by_tile(x[:, a % 2, :]) for x in (ctab, stab, mtab))
        if a >= 2:
            eng.wait_ge(*sig.after("s5_back", NT * (a - 1) - 1))
            eng.wait_ge(*sig.after("s5_back_im", NT * (a - 1) - 1))
            eng.wait_ge(*sig.after("s5_rotated", NT * (a - 1)))
        else:
            eng.wait_ge(*sig.after("ssd_ms"))
            eng.wait_ge(*sig.after("ssd_products", HEADS - 1))
            eng.wait_ge(*sig.after("s5_bb_rows"))
        on.memset(cv[:, :, 0:1], 1.0)
        on.memset(sv[:, :, 0:1], 0.0)
        ch(qtt(mv, row(MAG)[:, tiles].unsqueeze(2).broadcast_to([P, 4, P]),
               ones4.unsqueeze(2).broadcast_to([P, 4, P]), ALU.mult))
        ch(on.memset(mv[:, :, 0:1], 0.0))
        both = tab[:, a % 2, :, :].rearrange("p r (k t) -> p r k t", t=P)
        work = (ubd[:, 0, :], ubd[:, 1, :]) if a == 1 else (mem.tbias[0], mem.tbias[1])
        for r_ in range(int(np.log2(P))):
            n = 2 ** r_
            turn = [powers[:, r_, i, tiles].unsqueeze(1).unsqueeze(3).broadcast_to([P, 2, 4, n])
                    for i in range(2)]
            by_c, by_s = (x[:, 0:8 * n].rearrange("p (r k t) -> p r k t", r=2, t=n) for x in work)
            qtt(by_c, both[:, :, :, 0:n], turn[0], ALU.mult)
            ch(qtt(by_s, both[:, :, :, 0:n], turn[1], ALU.mult))
            qtt(cv[:, :, n:2 * n], by_c[:, 0, :, :], by_s[:, 1, :, :], ALU.subtract)
            last = qtt(sv[:, :, n:2 * n], by_s[:, 0, :, :], by_c[:, 1, :, :], ALU.add)
            if n < P // 2:
                ch(last)
        last.then_inc(*sig.inc(f"s5_tables_{a}"))
        eng.wait_ge(*sig.after(f"s5_tables_{a}"))

    def dve_extra(dve, e, ch):
        if e[0] == "setup":
            dve.wait_ge(*sig.after("bias16"))
            dve.wait_ge(*sig.after("fdt_transposed"))
            ch(tt(fd, mem.bank[4][:, 0:NT * 16].rearrange("p (t c) -> p t c", c=16), bias16.unsqueeze(1).broadcast_to([P, NT, 16]), ALU.add))
            ch(ts(fd[:, :, 0:8], fd[:, :, 0:8], -1.0, None, ALU.mult))
            ch(ts(e_, fd, -1.0, None, ALU.mult))
            tt(e_, e_, fd, ALU.max).then_inc(*sig.inc("fd_abs"))
            dve.wait_ge(*sig.after("fd_exp"))
            ts(w_, e_, 1.0, None, ALU.add).then_inc(*sig.inc("fd_one_plus"))
            dve.wait_ge(*sig.after("s5_step"))
            ch(ts(row(A_RE), row(A_RE), -1e-4, None, ALU.min))
            ch(tt(row(MAG), row(A_RE), row(L_STEP), ALU.mult))
            tt(row(TH), row(A_IM), row(L_STEP), ALU.mult).then_inc(*sig.inc("s5_lam"))
            dve.wait_ge(*sig.after("s5_lam"))
            ch(ts(row(T0), row(TH), 1.0 / (2 * np.pi), None, ALU.mult))
            ch(ts(row(T0), row(T0), ROUND, None, ALU.add))
            ch(ts(row(T0), row(T0), ROUND, None, ALU.subtract))
            for part in TWO_PI_PARTS:
                ch(V.scalar_tensor_tensor(row(TH), row(T0), -part, row(TH), ALU.mult, ALU.add))
            ts(row(TH), row(TH), PI_BELOW, -PI_BELOW, ALU.min, ALU.max).then_inc(
                *sig.inc("s5_angle"))
            dve.wait_ge(*sig.after("fd_ln"))
            ch(ts(w_, w_, 1.0, None, ALU.subtract))
            ch(ts(cums, w_, 0.0, None, ALU.is_equal))
            ch(tt(w_, w_, cums, ALU.add))
            ch(V.reciprocal(w_, w_))
            ch(tt(l_, l_, w_, ALU.mult))
            ch(tt(l_, l_, cums, ALU.add))
            ch(tt(l_, l_, e_, ALU.mult))
            ch(ts(fd, fd, 0.0, None, ALU.max))
            ch(tt(fd, fd, l_, ALU.add))
            ch(ts(lf, fd[:, :, 0:8], -1.0, None, ALU.mult))
            ch(V.memset(pre[:, 0, :], 0.0))
            for c in range(1, NT):
                ch(tt(pre[:, c, :], pre[:, c - 1, :], lf[:, c - 1, :], ALU.add))
            dve.wait_ge(*sig.after("a_exp"))
            ch(ts(a_neg, a_neg, -1.0, None, ALU.mult))
            tt(adt, fd[:, :, 8:16], a_neg.unsqueeze(1).broadcast_to([P, NT, 8]),
               ALU.mult).then_inc(*sig.inc("sums_ready"))
            dve.wait_ge(*sig.after("cum_sums"))
            b4 = mem.bank[4]
            v = lambda i: b4[:, 32 * i:32 * i + 32].rearrange("p (t h) -> p t h", h=8)
            V.tensor_copy(ncum, v(0))
            ts(cums[:, :, 0:8], v(0), -1.0, None, ALU.mult)
            V.tensor_copy(dout, v(1))
            V.tensor_copy(tot, v(2))
            V.tensor_copy(cums[:, :, 8:16], v(1)).then_inc(*sig.inc("cums"))
            dve.wait_ge(*sig.after("cums"))
            ts(nacs, cums[:, :, 8:16], -1.0, None, ALU.mult)
            tt(dte, tot, cums[:, :, 8:16], ALU.subtract).then_inc(*sig.inc("decay_arg"))
            sig.seen[(sig.phase, "cums_kept")] = ("decay_arg",)
            dve.wait_ge(*sig.after("s5_sin_half"))
            ch(tt(row(CO), row(CO), row(CO), ALU.mult))
            ch(ts(row(CO), row(CO), -2.0, 1.0, ALU.mult, ALU.add))
            dve.wait_ge(*sig.after("s5_mag"))
            ch(tt(row(T0), row(MAG), row(CO), ALU.mult))
            ch(ts(row(T0), row(T0), -1.0, None, ALU.add))
            ch(tt(row(T1), row(MAG), row(SI), ALU.mult))
            ch(tt(row(T2), row(A_RE), row(A_RE), ALU.mult))
            ch(tt(row(T3), row(A_IM), row(A_IM), ALU.mult))
            ch(tt(row(T2), row(T2), row(T3), ALU.add))
            ch(V.reciprocal(row(T2), row(T2)))
            ch(tt(row(K_RE), row(T0), row(A_RE), ALU.mult))
            ch(tt(row(T3), row(T1), row(A_IM), ALU.mult))
            ch(tt(row(K_RE), row(K_RE), row(T3), ALU.add))
            ch(tt(row(K_RE), row(K_RE), row(T2), ALU.mult))
            ch(tt(row(K_IM), row(T1), row(A_RE), ALU.mult))
            ch(tt(row(T3), row(T0), row(A_IM), ALU.mult))
            ch(tt(row(K_IM), row(K_IM), row(T3), ALU.subtract))
            ch(tt(row(K_IM), row(K_IM), row(T2), ALU.mult))
            cp = lambda i: powers[:, 0, i, :]
            V.tensor_copy(cp(0), row(CO))
            ch(V.tensor_copy(cp(1), row(SI)))
            for r_ in range(int(np.log2(P))):
                re, im = powers[:, r_, 0, :], powers[:, r_, 1, :]
                last = r_ == int(np.log2(P)) - 1
                nre, nim = (row(MR), row(MI)) if last else (
                    powers[:, r_ + 1, 0, :], powers[:, r_ + 1, 1, :])
                tt(row(T0), re, re, ALU.mult)
                tt(row(T1), im, im, ALU.mult)
                ch(V.scalar_tensor_tensor(nim, re, 2.0, im, ALU.mult, ALU.mult))
                ch(tt(nre, row(T0), row(T1), ALU.subtract))
            tt(row(MR), row(MR), row(MAG), ALU.mult)
            tt(row(MI), row(MI), row(MAG), ALU.mult)
            V.memset(ones4, 1.0).then_inc(*sig.inc("s5_bb_rows"))
        if e[0] == "fox":
            fox.on_dve(dve, e[1])
        if e[0] == "conv":
            f = e[1]
            if f == 0:
                dve.wait_ge(*sig.after("conv_pad"))
            dve.wait_ge(*sig.after("conv_acc", f))
            for k in range(3):
                V.scalar_tensor_tensor(acc[:, :], xbc[:, f, k:k + SEQ], cw[:, f, k:k + 1],
                                       acc[:, :], ALU.mult, ALU.add).then_inc(
                    *sig.inc("conv_tap", f, k))
                dve.wait_ge(*sig.after("conv_tap", f, k))
            sig.seen[(sig.phase, "conv_taps", f)] = ("conv_tap", f, 2)
        if e[0] == "conv_silu":
            f = e[1]
            dve.wait_ge(*sig.after("conv_tanh", f))
            x = xbc[:, f, 3:SEQ + 3]
            V.scalar_tensor_tensor(x, x, 1.0, acc[:, :], ALU.add, ALU.mult).then_inc(
                *sig.inc("conv", f))
        if e[0] == "y_split":
            tag = e[1]
            y = {"a": ya, "b": yb, "gy": yc, "c": yc}[tag]
            dve.wait_ge(*sig.after("y_hi", tag))
            if tag in ("gy", "c"):
                V.scalar_tensor_tensor(yl[:, :, :], y[:, :, :], 0.5, yh[:, :, :].bitcast(F32),
                                       ALU.mult, ALU.subtract).then_inc(*sig.inc("y_lo", tag))
            else:
                tt(yl[:, :, :], y[:, :, :], yh[:, :, :].bitcast(F32), ALU.subtract).then_inc(
                    *sig.inc("y_lo", tag))
        if e[0] == "cb":
            for gg in range(2):
                dve.wait_ge(*sig.after("cb", gg))
                tt(cbm[:, gg, :].rearrange("p (c l) -> p c l", l=P),
                   mem.bank[6 + gg][:, :].rearrange("p (c l) -> p c l", l=P),
                   tri[:, :].unsqueeze(1).broadcast_to([P, NT, P]), ALU.mult).then_inc(
                    *sig.inc("cb_masked", gg))
        if e[0] == "state":
            c = e[1]
            dve.wait_ge(*sig.after("state_product", c))
            if c:
                dve.wait_ge(*sig.after("state_decayed", c))
                tt(states[:, c, :], states[:, c, :], mem.bank[4][:, :], ALU.add).then_inc(
                    *sig.inc("state", c))
            else:
                V.tensor_copy(states[:, 0, :], mem.bank[4][:, :]).then_inc(
                    *sig.inc("state", c))
        if e[0] == "head_decay":
            h = e[1]
            dve.wait_ge(*sig.after("seg_loaded", h))
            for c in range(NT):
                x = seg[:, h % 2, c * P:(c + 1) * P]
                ins = ts(x, x, nacs[:, c, h:h + 1], 0.0, ALU.add, ALU.min)
            ins.then_inc(*sig.inc("seg", h))
        if e[0] == "head_out":
            h = e[1]
            dve.wait_ge(*sig.after("ssd_diag", h))
            for c in range(1, NT):
                y = yt[:, c, h * HD:(h + 1) * HD]
                ins = V.scalar_tensor_tensor(
                    y, mem.bank[4 + h % 2][:, 256 + (c - 1) * HD:256 + c * HD],
                    dout[:, c, h:h + 1], y, ALU.mult, ALU.add)
            ins.then_inc(*sig.inc("ssd_head", h))
        if e[0] == "z_silu":
            c = e[1]
            dve.wait_ge(*sig.after("z_tanh", c))
            V.scalar_tensor_tensor(z[:, c, :], z_tanh[:, c % 2, :], 1.0, z[:, c, :], ALU.add,
                                   ALU.mult).then_inc(*sig.inc("z_silu", c))
        if e[0] == "ssd_gate":
            h = e[1]
            hs = slice(h * HD, (h + 1) * HD)
            dve.wait_ge(*sig.after("ssd_skip", h))
            dve.wait_ge(*sig.after("z_silu", NT - 1))
            V.scalar_tensor_tensor(yt[:, :, hs], yt[:, :, hs], 0.5, z[:, :, hs], ALU.mult,
                                   ALU.mult).then_inc(*sig.inc("ssd_gated", h))
        if e[0] == "ssd_out":
            dve.wait_ge(*sig.after("ssd_square", HEADS - 1))
            ch(V.tensor_reduce(r8, xdt[:, :, :].rearrange("p t (g k) -> p (t g) k", g=2), AX.X,
                               ALU.add))
            ts(r8, r8, 1.0 / 256, RMS_EPS_2, ALU.mult, ALU.add).then_inc(*sig.inc("ssd_ms"))
            dve.wait_ge(*sig.after("ssd_rms"))
            dve.wait_ge(*sig.after("ssd_weighted", HEADS - 1))
            for c in range(NT):
                for gg in range(2):
                    x = yt[:, c, gg * 256:gg * 256 + 256]
                    ins = ts(x, x, r8[:, 2 * c + gg:2 * c + gg + 1], None, ALU.mult)
                ins.then_inc(*sig.inc("ssd_normed", c))
        if e[0] == "s5_tables":
            s5_tables(dve, V, e[1], ch)
        if e[0] == "s5_b":
            s5_tables(dve, V, 0, ch)
        if e[0] == "s5_bb":
            for i in range(2):
                dve.wait_ge(*sig.after("s5_b", i))
                dve.wait_ge(*sig.after("s5_c", i))
            b3 = lambda i: w_s5[:, 0, i, :].rearrange("p (t c) -> p t c", c=32)
            o3 = lambda i: (w_s5[:, 1, i, :] if i < 2 else mem.tbias[i - 2][:, :]).rearrange(
                "p (t c) -> p t c", c=32)
            kb = lambda r_: row(r_).unsqueeze(2).broadcast_to([P, S5_TILES, 32])
            ch(ts(ct[:, 1, :, :], ct[:, 1, :, :], -1.0, None, ALU.mult))
            ch(tt(o3(0), b3(0), kb(K_RE), ALU.mult))
            ch(tt(o3(2), b3(1), kb(K_IM), ALU.mult))
            ch(tt(o3(0), o3(0), o3(2), ALU.subtract))
            ch(tt(o3(1), b3(1), kb(K_RE), ALU.mult))
            ch(tt(o3(3), b3(0), kb(K_IM), ALU.mult))
            tt(o3(1), o3(1), o3(3), ALU.add).then_inc(*sig.inc("s5_bb"))
        if e[0] == "s5":
            s5_dve(dve, e[1], ch)
        if e[0] == "gelu":
            x = p_s5[:, 0, :, :]
            dve.wait_ge(*sig.after("gelu_square"))
            ch(ts(x, x, GELU_A, 1.0, ALU.mult, ALU.add))
            tt(x, x, yc[:, :, :], ALU.mult).then_inc(*sig.inc("gelu_arg"))
            dve.wait_ge(*sig.after("gelu_tanh"))
            V.scalar_tensor_tensor(yc[:, :, :], x, 1.0, yc[:, :, :], ALU.add,
                                   ALU.mult).then_inc(*sig.inc("gelu"))
        if e[0] == "m_split":
            fb = e[1]
            dve.wait_ge(*sig.after("m_hi", fb))
            V.scalar_tensor_tensor(ml[:, fb, :], merged[:, fb, :], 0.5,
                                   mh[:, fb, :].bitcast(F32), ALU.mult,
                                   ALU.subtract).then_inc(*sig.inc("m_lo", fb))
        if e[0] == "ln":
            ln.moments(dve, e[1])

    def s5_dve(dve, slot, ch):
        k = s5_in_slot(slot - 1)
        if k is not None:
            a, c = s5_it(k)
            if c == 0:
                dve.wait_ge(*sig.after(f"s5_tables_{a}"))
            dve.wait_ge(*sig.after("s5_bu", k))
            if k:
                dve.wait_ge(*sig.after("s5_rotated", k - 1))
            if k >= 2:
                dve.wait_ge(*sig.after("s5_back", k - 2))
                dve.wait_ge(*sig.after("s5_back_im", k - 2))
            re, im = mem.bank[4 + 2 * (k % 2)][:, :], mem.bank[5 + 2 * (k % 2)][:, :]
            w, cq, sq = w_s5[:, k % 2, :, :], ctab[:, a % 2, :], stab[:, a % 2, :]
            tt(w[:, 0, :], re, cq, ALU.mult)
            tt(mem.tbias[0][:, :], im, sq, ALU.mult)
            tt(w[:, 1, :], im, cq, ALU.mult)
            tt(mem.tbias[1][:, :], re, sq, ALU.mult).then_inc(*sig.inc("s5_products", k))
        m = s5_in_slot(slot - 2)
        if m is not None:
            a, c = s5_it(m)
            dve.wait_ge(*sig.after("s5_rotated", m))
            w = w_s5[:, m % 2, :, :]
            a4 = slice(4 * a, 4 * a + 4)
            first = [w[:, i, :].rearrange("p (k t) -> p k t", t=P)[:, :, 0] for i in range(2)]
            last = [w[:, i, :].rearrange("p (k t) -> p k t", t=P)[:, :, P - 1] for i in range(2)]
            if c:
                for i in range(2):
                    tt(first[i], first[i], carry[:, i, 0, :], ALU.add).then_inc(
                        *sig.inc("s5_entered", m, i))
                dve.wait_ge(*sig.after("s5_entered", m, 1))
            for i in range(2):
                V.tensor_tensor_scan(w[:, i, :], mtab[:, a % 2, :], w[:, i, :], 0.0, ALU.mult,
                                     ALU.add).then_inc(*sig.inc("s5_scan", m, i))
            dve.wait_ge(*sig.after("s5_scan", m, 1))
            pm = p_s5[:, m % 2, :, :]
            if c < NT - 1:
                t_ = [t4[:, 4 * i:4 * i + 4] for i in range(4)]
                tt(t_[0], last[0], row(MR)[:, a4], ALU.mult)
                tt(t_[1], last[1], row(MI)[:, a4], ALU.mult)
                tt(t_[2], last[0], row(MI)[:, a4], ALU.mult)
                tt(t_[3], last[1], row(MR)[:, a4], ALU.mult).then_inc(*sig.inc("s5_end", m))
            if m >= 2:
                dve.wait_ge(*sig.after("s5_out", m - 2))
            tt(pm[:, 0, :], w[:, 0, :], ctab[:, a % 2, :], ALU.mult)
            if c < NT - 1:
                dve.wait_ge(*sig.after("s5_end", m))
                tt(carry[:, 0, 0, :], t_[0], t_[1], ALU.subtract)
                tt(carry[:, 1, 0, :], t_[2], t_[3], ALU.add).then_inc(*sig.inc("s5_carry", m))
            V.scalar_tensor_tensor(pm[:, 1, :], w[:, 1, :], -1.0, stab[:, a % 2, :], ALU.mult,
                                   ALU.mult).then_inc(*sig.inc("s5_back", m))
            if c < NT - 1:
                dve.wait_ge(*sig.after("s5_carry", m))
        m = s5_in_slot(slot - S5_LAG)
        if m is not None:
            a, c = s5_it(m)
            dve.wait_ge(*sig.after("s5_out", m))
            if m == 0:
                dve.wait_ge(*sig.after("y_lo", "b"))
            cs = slice(c * P, (c + 1) * P)
            V.scalar_tensor_tensor(yc[:, a, cs], u_[:, a, cs], s5d[:, a:a + 1],
                                   mem.bank[3][:, 0:P], ALU.mult, ALU.add).then_inc(
                *sig.inc("s5_y", m))

    def pe_extra(pe, e):
        mm, tr = nc.tensor.matmul, nc.tensor.transpose
        if e[0] == "setup":
            pe.wait_ge(*sig.after("ev_act", G(("fdt", 0))))
            for c in range(NT):
                last = tr(mem.bank[4][:, 16 * c:16 * c + 16], fd_rows[:, c * P:(c + 1) * P],
                          mem.ident[0:16, 0:16])
            last.then_inc(*sig.inc("fdt_transposed"))
            pe.wait_ge(*sig.after("sums_ready"))
            pe.wait_ge(*sig.after("tri"))
            pe.wait_ge(*sig.after("ones"))
            b4 = mem.bank[4]
            flat = lambda ap: ap.rearrange("p t h -> p (t h)")
            mm(b4[:, 0:32], tri[:, :], flat(lf), start=True, stop=False)
            mm(b4[:, 0:32], ones[:, :], flat(pre), start=False, stop=True)
            mm(b4[:, 32:64], tri[:, :], flat(adt), start=True, stop=True)
            mm(b4[:, 64:96], ones[:, :], flat(adt), start=True, stop=True).then_inc(
                *sig.inc("cum_sums"))
            pe.wait_ge(*sig.after("cums"))
            for c in range(NT):
                last = tr(mem.bank[5][0:16, c * P:(c + 1) * P], cums[:, c, :], mem.ident[:, :])
            last.then_inc(*sig.inc("cum_transposed"))
        if e[0] == "fox":
            if e[1] == 0:
                pe.wait_ge(*sig.after("cum_rows"))
            fox.on_pe(pe, e[1])
        if e[0] == "x_t":
            f = e[1]
            pe.wait_ge(*sig.after("conv", f))
            if f == 0:
                pe.wait_ge(*sig.after("a_y", HEADS - 1))
            if f == 4:
                pe.wait_ge(*sig.after("x_t_kept", 0))
            for c in range(NT):
                last = tr(mem.bank[4 + f % 4][:, c * P:(c + 1) * P],
                          xbc[:, f, 3 + c * P:3 + (c + 1) * P], mem.ident[:, :])
            last.then_inc(*sig.inc("x_t", f))
        if e[0] == "cb":
            pe.wait_ge(*sig.after("conv", 5))
            pe.wait_ge(*sig.after("x_t_kept", 3))
            for gg in range(2):
                r_ = slice(gg * HD, gg * HD + HD)
                for c in range(NT):
                    x = slice(3 + c * P, 3 + (c + 1) * P)
                    last = mm(mem.bank[6 + gg][:, c * P:(c + 1) * P], xbc[r_, 4, x],
                              xbc[r_, 5, x], start=True, stop=True)
                last.then_inc(*sig.inc("cb", gg))
        if e[0] == "state":
            c = e[1]
            pe.wait_ge(*sig.after("xdd", c))
            pe.wait_ge(*sig.after("x_t_kept", 4))
            if c:
                pe.wait_ge(*sig.after("state", c - 1))
            mm(mem.bank[4][:, :], bt[:, c, :], xdd[:, :], start=True, stop=True).then_inc(
                *sig.inc("state_product", c))
        if e[0] == "head":
            h = e[1]
            pe.wait_ge(*sig.after("ssd_m", h))
            if h == 0:
                pe.wait_ge(*sig.after("state", 2))
            if h >= 2:
                pe.wait_ge(*sig.after("ssd_head", h - 2))
            bank, gg = mem.bank[4 + h % 2], h // 4
            r_ = slice(gg * HD, gg * HD + HD)
            hs = slice(h * HD, (h + 1) * HD)
            for c in range(NT):
                mm(bank[:, c * HD:(c + 1) * HD], seg[:, h % 2, c * P:(c + 1) * P],
                   xdt[:, c, hs], start=True, stop=True)
            for c in range(1, NT):
                last = mm(bank[:, 256 + (c - 1) * HD:256 + c * HD],
                          xbc[r_, 5, 3 + c * P:3 + (c + 1) * P], states[r_, c - 1, hs],
                          start=True, stop=True)
            last.then_inc(*sig.inc("ssd_products", h))
        if e[0] == "ybt":
            f = e[1]
            pe.wait_ge(*sig.after("ssd_normed", NT - 1))
            if f == 0:
                pe.wait_ge(*sig.after("ssd_head", HEADS - 1))
            for t in range(NT):
                last = tr(mem.bank[4 + f][:, t * P:(t + 1) * P], yt[:, t, f * P:(f + 1) * P],
                          mem.ident[:, :])
            last.then_inc(*sig.inc("ybt", f))
        if e[0] == "s5_b":
            pe.wait_ge(*sig.after("s5_bb"))
            pe.wait_ge(*sig.after("ybf", NW - 1))
            for i in range(2):
                for a in range(4):
                    last = tr(mem.bank[4 + i][:, a * P:(a + 1) * P],
                              w_s5[:, 1, i, a * P:(a + 1) * P], mem.ident[:, :])
            last.then_inc(*sig.inc("s5_b_transposed"))
        if e[0] == "s5":
            m = s5_in_slot(e[1] - S5_LAG)
            if m is not None:
                a, c = s5_it(m)
                pe.wait_ge(*sig.after("s5_back", m))
                pe.wait_ge(*sig.after("s5_back_im", m))
                if m == 0:
                    st.wait_read(pe, last_in_3)
                else:
                    pe.wait_ge(*sig.after("s5_y", m - 1))
                for q_ in range(4):
                    o = mem.bank[3][32 * q_:32 * q_ + 32, 0:P]
                    for i in range(4):
                        last = mm(o, ct[:, i // 2, 4 * a + q_, :],
                                  p_s5[:, m % 2, i, q_ * P:(q_ + 1) * P], start=i == 0,
                                  stop=i == 3, tile_position=(0, 32 * q_))
                last.then_inc(*sig.inc("s5_out", m))
                if m == n_it - 1:
                    sig.seen[(sig.phase, "s5_done")] = ("s5_out", m)
            k = s5_in_slot(e[1])
            if k is not None:
                a, c = s5_it(k)
                if k == 0:
                    pe.wait_ge(*sig.after("s5_b_kept", 1))
                if k >= 2:
                    pe.wait_ge(*sig.after("s5_products", k - 2))
                pe.wait_ge(*sig.after("s5_u", k))
                for i in range(2):
                    last = mm(mem.bank[4 + 2 * (k % 2) + i][:, :], bbt[:, i, a, :],
                              ubd[:, k % 2, :], start=True, stop=True)
                last.then_inc(*sig.inc("s5_bu", k))




    with nc.Block() as block:
        @block.sync
        def _(sp):
            for n in range(3):
                st.load(sp, n)
            sp.wait_ge(*sig.after("cum_rows"))
            sp.dma_start(d["rows"], cum_f[:, :]).then_inc(*sig.inc("rows_stored", by=16))
            for n in range(3, 6):
                st.load(sp, n)
            sp.wait_ge(*sig.after("rows_stored"))
            for h in range(HEADS):
                sp.dma_start(minus_cum[:, h, :], d["rows"][h].partition_broadcast(P)).then_inc(
                    *sig.inc(f"minus_cum_{h}", by=16))
                sig.seen[(sig.phase, "minus_cum", h)] = (f"minus_cum_{h}",)
            for n in range(6, n_units):
                st.load(sp, n)
            st.load_next(sp)
            for t in range(NT):
                ln.store(sp, t)
            sp.wait_ge(*sig.after("ln_stored", NT - 1))

        @block.scalar
        def _(act):
            split.split_hi(act)
            for name, dst in (("bias16", bias16), ("dskip", dskip), ("a_log", a_neg)):
                act.dma_start(dst, d[name].partition_broadcast(P)).then_inc(*sig.inc(name, by=16))
            for name, dst in (("cw", mem.small2[:, 16:46]), ("s5d", s5d), ("glub", glub),
                              ("gb", gb), ("s5_q", qmask), ("s5in", s5p[:, 0:3, :]), ("tri", tri[:, :]),
                              ("ones", ones[:, :])):
                act.dma_start(dst, d[name]).then_inc(*sig.inc(name, by=16))
            act.wait_ge(*sig.after("x_lo", ND - 1))
            act.dma_start(mem.cols[:, :], d["ln_cols"][LAYERS + 1]).then_inc(
                *sig.inc("ln_cols", by=16))
            st.hi(act, 1)
            for n, q, ex in steps:
                u = units[n]
                if q == 0 and n:
                    st.hi(act, n + 1)
                if n == 0 and q == 3:
                    act.wait_ge(*sig.after("params_halved"))
                for gid, b in groups_done(u, q):
                    if u.evac[0] == "few":
                        act.wait_ge(*sig.after("group", gid))
                        A.activation(fd_rows[:, :], st.bank(gid)[0:16, :], ACT.Copy).then_inc(
                            *sig.inc("ev_act", gid))
                    elif u.evac[0] == "plain":
                        dst, _, scale = ctx["scaled"](u.evac[1], u.evac[2] + b)
                        act.wait_ge(*sig.after("group", gid))
                        A.activation(dst, st.bank(gid)[:, :], ACT.Copy, scale=scale).then_inc(
                            *sig.inc("ev_act", gid))
                    elif u.evac[0] == "glu":
                        act.wait_ge(*sig.after("group", gid))
                        A.activation(p_s5[:, 1, b, :], st.bank(gid)[:, :], ACT.Tanh,
                                     bias=glub[:, b:b + 1], scale=0.5).then_inc(
                            *sig.inc("ev_act", gid))
                    else:
                        emit_common_evac(nc, sig, mem, st, u, b, gid, "act", act, ctx)
                for e in ex:
                    act_extra(act, e)
            act.wait_ge(*sig.after("ln_cols"))

        @block.gpsimd
        def _(pool):
            pch = Chain(pool, "pool_chain")
            Q.memset(xbc[:, :, 0:3], 0.0).then_inc(*sig.inc("conv_pad"))
            for n, q, ex in steps:
                u = units[n]
                if q == 0:
                    st.lo_on_pool(pool, n + 1)
                for gid, b in groups_done(u, q):
                    emit_common_evac(nc, sig, mem, st, u, b, gid, "pool", pool, ctx)
                for e in ex:
                    pool_extra(pool, e, pch)

        @block.vector
        def _(dve):
            ch = Chain(dve, "dve_chain")
            split.split_lo(dve)
            st.lo(dve, 1)
            for name in ("cw", "gb", "glub"):
                dve.wait_ge(*sig.after(name))
            ts(cw, cw, 0.5, None, ALU.mult)
            ts(gb, gb, 0.5, None, ALU.mult)
            ts(glub, glub, 0.5, None, ALU.mult).then_inc(*sig.inc("params_halved"))
            for n, q, ex in steps:
                u = units[n]
                if q == 0 and n:
                    st.lo(dve, n + 1)
                for gid, b in groups_done(u, q):
                    if u.evac[0] == "glu":
                        dve.wait_ge(*sig.after("ev_act", gid))
                        V.scalar_tensor_tensor(p_s5[:, 1, b, :], p_s5[:, 1, b, :], 1.0,
                                               yc[:, b, :], ALU.add, ALU.mult).then_inc(
                            *sig.inc("glu_product", b))
                        dve.wait_ge(*sig.after("glu_product", b))
                        ts(yc[:, b, :], p_s5[:, 1, b, :], 0.5, None, ALU.mult).then_inc(
                            *sig.inc("glu_used", b))
                    else:
                        emit_common_evac(nc, sig, mem, st, u, b, gid, "dve", dve, ctx)
                    if u.evac[0] == "residual":
                        ln.half(dve, b, u.evac[2] // 512)
                for e in ex:
                    dve_extra(dve, e, ch)

        @block.tensor
        def _(pe):
            for n, q, ex in steps:
                st.multiply(pe, n, q)
                for e in ex:
                    pe_extra(pe, e)
            ln.transpose(pe)

def ffn_units():
    units, what = [], []
    for i in range(NF2):
        units.append(Unit("F", "x", ND, 2 * P, ("conv_ffn", "up", 2 * i)))
        what.append(("up", 0, ND, 2 * i * P, 2 * P))
    for c in (0, 512):
        for k0 in range(0, NF2, 4):
            nk = min(4, NF2 - k0)
            units.append(Unit("T", "h", nk, 512, ("residual", "down", c), k0=k0, of=NF2))
            what.append(("down", k0, nk, c, 512))
    return units, what


def ffn_phase(nc, sig, mem, d):
    units, _ = ffn_units()
    n_units = len(units)
    at = lambda name, *a: mem.at("ff_" + name, *a)
    hh = at("h_hi", 0, [P, NF2, SEQ], F32R)
    hl = at("h_lo", 44, [P, NF2, SEQ], F32R)
    val = at("val", 88, [P, 2, SEQ])
    gat = at("gate", 92, [P, 2, SEQ])
    th = at("tanh", 96, [P, 2, SEQ])
    gamma = at("gamma", 100, [P, D])
    beta = at("beta", 104, [P, D])
    xt = nc.alloc_sbuf_tensor_at("ff_x_t", [P, NT, D], F32, offset=int(mem.x_base))
    rows = [nc.alloc_sbuf_tensor_at(f"ff_residual_{i}", [P, D], F32,
                                    offset=int(mem.x_base + 4 * (NT + i) * D)) for i in range(2)]
    cw = mem.small2[:, 0:4 * 2 * NF2].rearrange("p (f k) -> p f k", k=4)
    st = Stream(nc, sig, mem, units, lambda n: d["w3"][n],
                {"x": (mem.xh, mem.xl), "h": (hh, hl)},
                lambda u: [("h_lo", u.k0 + u.nk - 1)] if u.src == "h" else [],
                offset=len(mixer_units()[0]))
    gid_of = {(u.evac[1], u.evac[2], b): gid for gid, (u, b) in st.by_gid.items()}
    ctx = dict(xt=xt, before=lambda tag: [], **gate_plan(st))
    ln = LayerNorm(nc, sig, mem, xt, lambda t: d["out"][t],
                   lambda t, i: ("ev_dve", gid_of[("down", 512 * i, t)]), answer=True)
    split = InputSplit(nc, sig, mem, val)
    V, A, Q = nc.vector, nc.scalar, nc.gpsimd
    steps = [(n, q) for n in range(n_units) for q in range(4)]

    def groups_done(u, q):
        return [(gid, b) for b, gid in enumerate(u.gids) if completes(u, q, b)]

    def high(act, i):
        act.wait_ge(*sig.after("h", i))
        A.activation(hh[:, i, :], val[:, i % 2, :], ACT.Copy).then_inc(*sig.inc("h_hi", i))

    def low(dve, i):
        dve.wait_ge(*sig.after("h_hi", i))
        V.tensor_tensor(hl[:, i, :], val[:, i % 2, :], hh[:, i, :].bitcast(F32),
                        ALU.subtract).then_inc(*sig.inc("h_lo", i))

    with nc.Block() as block:
        @block.sync
        def _(sp):
            for n in range(n_units):
                st.load(sp, n)
                if n == NF2 + RAW:
                    sp.wait_ge(*sig.after("unit_done", NF2 - 1))
                    sp.dma_start(xt[:, :, :], d["resid"].rearrange("t p c -> p t c")).then_inc(
                        *sig.inc("x_t_loaded", by=16))
                    for i in range(2):
                        sp.dma_start(rows[i][:, :], d["ln_rows"][LAYERS + 1][i].partition_broadcast(
                            P)).then_inc(*sig.inc("residual_rows", by=16))
            for t in range(NT):
                ln.store(sp, t)
            sp.wait_ge(*sig.after("ln_stored", NT - 1))

        @block.gpsimd
        def _(pool):
            for i in range(NF2):
                pool.wait_ge(*sig.after("silu", i))
                Q.tensor_tensor(val[:, i % 2, :], val[:, i % 2, :], gat[:, i % 2, :],
                                ALU.mult).then_inc(*sig.inc("h", i))
            scale_residual(pool, nc, sig, xt, rows, ALPHA_2)
            for t in range(NT):
                residual_block(pool, nc, sig, xt, rows, t)
            for t in range(NT):
                ln.power(pool, t)

        @block.scalar
        def _(act):
            split.split_hi(act)
            act.dma_start(mem.small2[:, 0:8 * NF2], d["ffn_cw"]).then_inc(*sig.inc("cw", by=16))
            for i, r_ in enumerate((gamma, beta)):
                act.dma_start(r_[:, :], d["ln2"][i].partition_broadcast(P)).then_inc(
                    *sig.inc("ln_params", i, by=16))
            sig.seen[(sig.phase, "ln_params")] = ("ln_params", 1)
            st.hi(act, 1)
            act.wait_ge(*sig.after("cw_ready"))
            for n, q in steps:
                u = units[n]
                if q == 0 and n:
                    st.hi(act, n + 1)
                for gid, b in groups_done(u, q):
                    if u.evac[0] != "conv_ffn":
                        continue
                    f = u.evac[2] + b
                    dst = (val, gat)[b][:, n % 2, :]
                    act.wait_ge(*sig.after("group", gid))
                    if n >= 2:
                        act.wait_ge(*sig.after("h_lo", n - 2))
                    A.activation(dst, st.bank(gid)[:, :], ACT.Identity, bias=cw[:, f, 3:4],
                                 scale=cw[:, f, 2:3]).then_inc(*sig.inc("tap2", gid))
                if n < NF2 and q == 1 and n:
                    high(act, n - 1)
                if n < NF2 and q == 3:
                    act.wait_ge(*sig.after("ev_dve", u.gids[1]))
                    A.activation(th[:, n % 2, :], gat[:, n % 2, :], ACT.Tanh).then_inc(
                        *sig.inc("tanh", n))
                if n == NF2 and q == 0:
                    high(act, NF2 - 1)

        @block.vector
        def _(dve):
            split.split_lo(dve)
            st.lo(dve, 1)
            dve.wait_ge(*sig.after("cw"))
            gcw = mem.small2[:, 0:8 * NF2].rearrange("p (f two k) -> p f two k", two=2, k=4)
            V.tensor_scalar(gcw[:, :, 1, :], gcw[:, :, 1, :], 0.5, None, ALU.mult).then_inc(
                *sig.inc("cw_ready"))
            dve.wait_ge(*sig.after("cw_ready"))
            for n, q in steps:
                u = units[n]
                if q == 0 and n:
                    st.lo(dve, n + 1)
                for gid, b in groups_done(u, q):
                    if u.evac[0] == "conv_ffn":
                        f = u.evac[2] + b
                        dst = (val, gat)[b][:, n % 2, :]
                        ps = st.bank(gid)
                        dve.wait_ge(*sig.after("tap2", gid))
                        V.scalar_tensor_tensor(dst[:, 1:SEQ], ps[:, 0:SEQ - 1], cw[:, f, 1:2],
                                               dst[:, 1:SEQ], ALU.mult, ALU.add).then_inc(
                            *sig.inc("tap1", gid))
                        dve.wait_ge(*sig.after("tap1", gid))
                        V.scalar_tensor_tensor(dst[:, 2:SEQ], ps[:, 0:SEQ - 2], cw[:, f, 0:1],
                                               dst[:, 2:SEQ], ALU.mult, ALU.add).then_inc(
                            *sig.inc("ev_dve", gid))
                    else:
                        emit_common_evac(nc, sig, mem, st, u, b, gid, "dve", dve, ctx)
                        ln.half(dve, b, u.evac[2] // 512)
                if n < NF2 and q == 1 and n:
                    low(dve, n - 1)
                if n < NF2 and q == 3:
                    dve.wait_ge(*sig.after("tanh", n))
                    x = gat[:, n % 2, :]
                    V.scalar_tensor_tensor(x, th[:, n % 2, :], 1.0, x, ALU.add,
                                           ALU.mult).then_inc(*sig.inc("silu", n))
                if n == NF2 and q == 0:
                    low(dve, NF2 - 1)
                if n == n_units - 1:
                    ln.moments(dve, q)
                    if q == 0:
                        dve.wait_ge(*sig.after("ln_params"))
                    ln.finish(dve, q, gamma, beta)

        @block.tensor
        def _(pe):
            for n, q in steps:
                st.multiply(pe, n, q)


def third_phases(nc, sig, mem, d):
    sig.begin("mixer")
    mixer_phase(nc, sig, mem, d)
    sig.end()
    sig.begin("ffn")
    ffn_phase(nc, sig, mem, d)


def input_phase(nc, sig, mem, d):
    xt = mem.at("x_t_in", 58, [P, NT, D])
    st = Stream(nc, sig, mem, [], None, {}, None, nxt=lambda j: d["w_first"][0][j])
    ln = LayerNorm(nc, sig, mem, xt, lambda t: d["resid"][t], lambda t, i: (f"x_in_{t}",))
    with nc.Block() as block:
        @block.sync
        def _(sp):
            for t in range(NT):
                sp.dma_start(xt[:, t, :], d["x"][t]).then_inc(*sig.inc(f"x_in_{t}", by=16))
            st.load_next(sp)
            for t in range(NT):
                ln.store(sp, t)
            sp.wait_ge(*sig.after("ln_stored", NT - 1))

        @block.gpsimd
        def _(pool):
            nc.gpsimd.memset(mem.half[:, :], -0.5).then_inc(*sig.inc("half"))
            pool.wait_ge(*sig.after("half"))
            for t in range(NT):
                ln.power(pool, t)

        @block.scalar
        def _(act):
            act.dma_start(mem.ident[:, :], d["ident"]).then_inc(*sig.inc("ident", by=16))
            act.dma_start(mem.cols[:, :], d["ln_cols"][2]).then_inc(*sig.inc("ln_cols", by=16))
            act.dma_start(mem.rope[:, :], d["rope"]).then_inc(*sig.inc("consts", by=16))
            act.dma_start(mem.mask[:, :], d["mask"]).then_inc(*sig.inc("consts", by=16))
            for t in range(NT):
                ln.normalise(act, t)
            st.hi(act, 0)
            act.wait_ge(*sig.after("consts"))
            act.wait_ge(*sig.after("ln_cols"))

        @block.vector
        def _(dve):
            for t in range(NT):
                for i in range(2):
                    ln.half(dve, t, i)
                ln.moments(dve, t)
            st.lo(dve, 0)

        @block.tensor
        def _(pe):
            pe.wait_ge(*sig.after("ident"))
            ln.transpose(pe)


def program(nc, d, known):
    with ExitStack() as ctx:
        sig = Signals(nc, known)
        mem = Memory(nc, ctx)
        sig.begin("input")
        input_phase(nc, sig, mem, d)
        sig.end()
        sig.begin("layer")
        with nc.Fori(0, LAYERS) as layer:
            layer_phase(nc, sig, mem, d, layer)
            sig.end()
        third_phases(nc, sig, mem, d)
        return sig.seen


def pack_units(what, mats):
    out = np.zeros((len(what), P, UNIT), np.float32)
    for n, (w, k0, nk, c0, cols) in enumerate(what):
        part = mats[w][k0 * P:(k0 + nk) * P, c0:c0 + cols].reshape(nk, P, -1).transpose(1, 0, 2)
        if part.shape[2] < cols:
            part = np.concatenate([part, np.zeros((P, nk, cols - part.shape[2]), np.float32)], 2)
        out[n, :, :nk * cols] = part.reshape(P, -1)
    return out


def blocks(v, col, n):
    return v[col:col + n * P].reshape(n, P).T


def shape_constants():
    t = np.arange(SEQ)
    freqs = np.float32(10000.0) ** (-np.arange(0, 32, 2, dtype=np.float32) / np.float32(32))
    ang = np.concatenate([(t // GRID).astype(np.float32)[:, None] * freqs,
                          (t % GRID).astype(np.float32)[:, None] * freqs], -1).astype(np.float32)
    table = lambda f: f(ang).astype(np.float32).reshape(NT, P, 32).transpose(1, 0, 2).reshape(P, -1)
    i = np.arange(P)
    scale = np.concatenate([np.full((P, n), s, np.float32) for _, n, s in F_BIAS], 1)
    return {
        "ident": np.eye(P, dtype=np.float32),
        "rope": np.concatenate([table(np.cos), table(np.sin)], 1),
        "mask": np.where(i[None, :] <= i[:, None], 0.0, NEG).astype(np.float32),
        "f_scale": scale,
        "s5_q": (i[:, None] // 32 == np.arange(4)[None, :]).astype(np.float32),
        "tri": (i[:, None] <= i[None, :]).astype(np.float32),
        "ones": np.ones((P, P), np.float32),
    }


def lay_out(a):
    o = shape_constants()
    o["x"] = a["x"].reshape(NT, P, D)
    _, what = layer_units()
    w1, fb, tb, nab = [], [], [], []
    c = np.arange(GRID)
    start = np.clip(c - KW // 2, 0, GRID - KW)
    valid = (c[None, :] >= start[:, None]) & (c[None, :] < start[:, None] + KW)
    col_off = np.clip(c[None, :] - c[:, None] + KW - 1, 0, 2 * KW - 2)
    for l in range(LAYERS):
        mats = {"in": a["w_in"][l], "br_a": a["w_br_a"][l], "br_b": a["w_br_b"][l],
                "br_c": a["w_br_c"][l], "out": a["w_out"][l]}
        w1.append(pack_units(what, mats))
        b = a["b_in"][l]
        fb.append(np.concatenate([blocks(b, col, n) for col, n, _ in F_BIAS], 1))
        gq, sg = 4 * WID, 6 * WID + 256
        pad = np.zeros(256, np.float32)
        tb.append(np.concatenate([b[2 * WID:3 * WID], b[gq:gq + WID], b[gq + WID:gq + WID + 256],
                                  pad, b[sg:sg + 3 * WID]]))
        e = np.where(valid[None, None], a["na_rpb"][l][:, :, col_off], np.float32(NEG))
        m = np.arange(14)
        pair = np.stack([e[:, m + 1], e[:, m]], 1)
        nab.append(pair.transpose(0, 1, 3, 2, 4).reshape(HEADS, P, 14 * GRID))
    o["w1"], o["f_bias"], o["t_bias"], o["na_bias"] = map(np.stack, (w1, fb, tb, nab))
    o["qk_g"] = np.stack([np.concatenate([np.tile(a["q_norm_g"][l], 8), np.tile(a["k_norm_g"][l], 2)])
                          for l in range(LAYERS)])
    o["sg_gb"] = np.stack([a["sg_ln_g"], a["sg_ln_b"]], 1)
    o["sg_w"] = a["sg_w"].transpose(0, 3, 1, 2)
    o["sg_b"] = a["sg_b"].transpose(0, 2, 1)
    o["b_out"] = a["b_out"]
    b = {k[:-2]: v[0] for k, v in a.items() if k.endswith("_2")}
    w = b["w_in"]
    mats = {"in": w, "fdt": np.concatenate([w[:, C_F:C_F + 8], w[:, C_DT:C_DT + 8]], 1),
            "glu": b["s5_w_glu"], "out": b["w_out"]}
    for r, tag in enumerate("abc"):
        mats["br_" + tag] = b["w_branch"][r]
    o["w2"] = pack_units(mixer_units()[1], mats)
    up = b["ffn_w_up"].reshape(D, 2, NF2, P).transpose(0, 2, 1, 3).reshape(D, 2 * D_FF)
    o["w3"] = pack_units(ffn_units()[1], {"up": up, "down": b["ffn_w_down"]})
    o["w_first"] = np.stack([o["w1"][0][:AHEAD], o["w1"][1][:AHEAD], o["w2"][:AHEAD],
                             o["w3"][:AHEAD]])
    o["bias16"] = np.concatenate([b["fox_f_bias"], b["ssd_dt_bias"]])
    o["dskip"], o["a_log"], o["ssd_norm_w"] = b["ssd_d"], b["ssd_a_log"], b["ssd_norm_w"]
    o["cw"] = np.concatenate([b["ssd_conv_w"], b["ssd_conv_b"][None]]).reshape(
        5, NXBC, P).transpose(2, 1, 0).reshape(P, -1)
    o["s5d"] = b["s5_d"].reshape(NW, P).T
    o["glub"] = b["s5_b_glu"].reshape(NW, P).T
    o["gb"] = b["b_gate"].reshape(3 * ND, P).T
    tiles = lambda v: v.reshape(S5_TILES, P).T
    o["s5in"] = np.stack([tiles(b["s5_a_re"]), tiles(b["s5_a_im"]),
                          tiles(np.repeat(b["s5_log_step"], 64))], 1)

    def block_diagonal(v):
        out = np.zeros((2, 64, S5_TILES, 2, 16), np.float32)
        for i in range(2):
            out[i, :, :, i, :] = v.reshape(S5_TILES, 2, 64, 16)[:, i].transpose(1, 0, 2)
        return out.reshape(P, S5_TILES * 32)

    o["s5_b"] = np.stack([block_diagonal(b["s5_b_re"]), block_diagonal(b["s5_b_im"])])
    o["s5_c"] = np.stack([block_diagonal(b["s5_c_re"].transpose(0, 2, 1)),
                          block_diagonal(b["s5_c_im"].transpose(0, 2, 1))])
    norms = [(a["ln_in_g"], a["ln_in_b"]), (a["ln_post_g"][0], a["ln_post_b"][0]),
             (a["ln_post_g"][1], a["ln_post_b"][1]), (b["ln1_g"], b["ln1_b"])]
    o["ln_rows"] = np.stack([np.stack(gb) for gb in norms])
    o["ln_cols"] = np.stack([np.concatenate([blocks(v, 0, ND) for v in norms[i]], 1)
                             for i in (1, 2, 0, 3)])
    o["ln2"] = np.stack([b["ln2_g"], b["ln2_b"]])
    cf = np.concatenate([b["ffn_conv_w"], b["ffn_conv_b"][None]])
    o["ffn_cw"] = cf.reshape(4, 2, NF2, P).transpose(3, 2, 1, 0).reshape(P, -1)
    return {"in_" + k: np.ascontiguousarray(v) for k, v in o.items()}


def dram_tensors(nc, shapes):
    d = {k[3:]: nc.dram_tensor(k, list(shape), F32, kind="ExternalInput").ap()
         for k, shape in shapes.items()}
    d["resid"] = nc.dram_tensor("residual", [NT, P, D], F32, kind="Internal").ap()
    d["rows"] = nc.dram_tensor("row_sums_dram", [16, SEQ], F32, kind="Internal").ap()
    d["out"] = nc.dram_tensor("out_0", [NT, P, D], F32, kind="ExternalOutput").ap()
    return d


def kernel(**inputs):
    import concourse.bacc as bacc
    from concourse.bass_utils import run_bass_kernel_spmd

    arrays = lay_out({k: np.asarray(v) for k, v in inputs.items()})
    shapes = {k: v.shape for k, v in arrays.items()}
    known = None
    for _ in range(2):
        nc = bacc.Bacc("TRN2", target_bir_lowering=False, num_devices=1)
        known = program(nc, dram_tensors(nc, shapes), known)
    r = run_bass_kernel_spmd(nc, [arrays], core_ids=[0])
    return r.results[0]["out_0"].reshape(1, SEQ, D)
```
